# Optimizing a Trainium2 kernel written in Bass

```python
import jax, jax.numpy as jnp
from jax import lax
import numpy as np

D_MODEL = 1024
BATCH = 1
SEQ = 1024
DEPTH = 1
DEC_BATCH = 8
DEC_SEQ = 4
PAST_LEN = 1024
PAGE_SIZE = 128

A_HEADS = 8
A_HEAD_DIM = 64
A_ROT_DIM = A_HEAD_DIM // 4
A_PATTERNS = ((128, 1), (512, 4), (2048, 16))
A_MAX_WINDOW = 2048
A_WIDTH = A_HEADS * A_HEAD_DIM
B_HEADS = 8
B_NOPE_DIM = 64
B_ROPE_DIM = 32
B_V_DIM = 64
B_Q_LORA = 384
B_KV_LORA = 256
D_FF = 4 * D_MODEL
PLE_DIM = 256
ROPE_THETA = 500000.0
RMS_EPS = 1e-6
Q_BLOCK = 128
IN_SPLITS = (A_WIDTH, A_WIDTH, A_WIDTH, B_Q_LORA, B_KV_LORA, B_ROPE_DIM, D_MODEL, D_MODEL)
D_IN = sum(IN_SPLITS)

kernel_name = 'hybrid_dilated_mla_decoder_step'

def rms_norm(x, g):
    xf = x.astype(jnp.float32)
    y = xf * lax.rsqrt(jnp.mean(xf * xf, axis=-1, keepdims=True) + RMS_EPS)
    return (y * g.astype(jnp.float32)).astype(x.dtype)

def rope(x, pos, rot_dim):
    half = rot_dim // 2
    inv = ROPE_THETA ** (-jnp.arange(half, dtype=jnp.float32) * (2.0 / rot_dim))
    ang = pos.astype(jnp.float32)[:, None] * inv[None, :]
    cos = jnp.cos(ang)[None, :, None, :]
    sin = jnp.sin(ang)[None, :, None, :]
    xf = x.astype(jnp.float32)
    x1 = xf[..., :half]
    x2 = xf[..., half:rot_dim]
    out = jnp.concatenate([x1 * cos - x2 * sin, x2 * cos + x1 * sin, xf[..., rot_dim:]], axis=-1)
    return out.astype(x.dtype)

def masked_softmax(s, mask):
    s = jnp.where(mask, s, -jnp.inf)
    mx = jnp.max(s, axis=-1, keepdims=True)
    e = jnp.exp(s - mx)
    l = jnp.sum(e, axis=-1, keepdims=True)
    return e / l, (mx + jnp.log(l))[..., 0]

def in_projection(h, pos, w_in, g_q, w_uq, g_kv):
    n, t = h.shape[0], h.shape[1]
    cuts = [int(c) for c in np.cumsum(IN_SPLITS)[:-1]]
    qa, ka, va, cq, ckv, kpe, ga, gb = jnp.split(h @ w_in, cuts, axis=-1)
    qa = rope(qa.reshape(n, t, A_HEADS, A_HEAD_DIM), pos, A_ROT_DIM)
    ka = rope(ka.reshape(n, t, A_HEADS, A_HEAD_DIM), pos, A_ROT_DIM)
    va = va.reshape(n, t, A_HEADS, A_HEAD_DIM)
    qb = (rms_norm(cq, g_q) @ w_uq).reshape(n, t, B_HEADS, B_NOPE_DIM + B_ROPE_DIM)
    q_nope = qb[..., :B_NOPE_DIM]
    q_pe = rope(qb[..., B_NOPE_DIM:], pos, B_ROPE_DIM)
    ckv = rms_norm(ckv, g_kv)
    kpe = rope(kpe[:, :, None, :], pos, B_ROPE_DIM)[:, :, 0, :]
    return qa, ka, va, q_nope, q_pe, ckv, kpe, ga, gb

def dilated_attn_prompt(q, k, v, window, dilation):
    n, s_len, h, e = q.shape
    blk = window // dilation
    span = dilation * blk
    s_pad = -(-s_len // span) * span
    nb = s_pad // span

    def to_blocks(t):
        t = jnp.pad(t, ((0, 0), (0, s_pad - s_len), (0, 0), (0, 0)))
        t = t.reshape(n, nb * blk, dilation, h, e).transpose(0, 2, 1, 3, 4)
        return t.reshape(n, dilation, nb, blk, h, e)

    def with_prev(t):
        prev = jnp.pad(t[:, :, :-1], ((0, 0), (0, 0), (1, 0), (0, 0), (0, 0), (0, 0)))
        return jnp.concatenate([prev, t], axis=3)

    qb = to_blocks(q)
    kb = with_prev(to_blocks(k))
    vb = with_prev(to_blocks(v))
    s = jnp.einsum('ndbqhe,ndbkhe->ndbhqk', qb, kb, preferred_element_type=jnp.float32) * (e ** -0.5)
    qi = jnp.arange(blk)[:, None]
    kj = jnp.arange(2 * blk)[None, :]
    dist = blk + qi - kj
    band = (dist >= 0) & (dist <= blk)
    first = (jnp.arange(nb) == 0)[:, None, None]
    mask = band[None] & ~(first & (kj < blk)[None])
    p, lse = masked_softmax(s, mask[None, None, :, None])
    o = jnp.einsum('ndbhqk,ndbkhe->ndbqhe', p.astype(v.dtype), vb, preferred_element_type=jnp.float32)
    o = o.reshape(n, dilation, nb * blk, h, e).transpose(0, 2, 1, 3, 4).reshape(n, s_pad, h, e)[:, :s_len]
    lse = lse.transpose(0, 1, 2, 4, 3).reshape(n, dilation, nb * blk, h)
    lse = lse.transpose(0, 2, 1, 3).reshape(n, s_pad, h)[:, :s_len]
    return o, lse

def dilated_attn_sample(q, k_ext, v_ext, window, dilation):
    n, t, h, e = q.shape
    l = k_ext.shape[1]
    nk = window // dilation + 1
    qpos = l - t + jnp.arange(t)
    idx = qpos[:, None] - dilation * jnp.arange(nk)[None, :]
    valid = idx >= 0
    idx_c = jnp.clip(idx, 0, l - 1).reshape(-1)
    kg = jnp.take(k_ext, idx_c, axis=1).reshape(n, t, nk, h, e)
    vg = jnp.take(v_ext, idx_c, axis=1).reshape(n, t, nk, h, e)
    s = jnp.einsum('nthe,ntjhe->nthj', q, kg, preferred_element_type=jnp.float32) * (e ** -0.5)
    p, lse = masked_softmax(s, valid[None, :, None, :])
    o = jnp.einsum('nthj,ntjhe->nthe', p.astype(vg.dtype), vg, preferred_element_type=jnp.float32)
    return o, lse

def combine_patterns(outs):
    o = jnp.stack([a for a, _ in outs], axis=-2)
    w = jax.nn.softmax(jnp.stack([b for _, b in outs], axis=-1), axis=-1)
    return jnp.sum(w[..., None] * o, axis=-2)

def mla_prompt(q_nope, q_pe, ckv, kpe, w_uk, w_uv):
    n, s_len, h, _ = q_nope.shape
    k_nope = jnp.einsum('nsc,che->nshe', ckv, w_uk)
    v = jnp.einsum('nsc,che->nshe', ckv, w_uv)
    scale = (B_NOPE_DIM + B_ROPE_DIM) ** -0.5
    nb = s_len // Q_BLOCK
    qn = q_nope.reshape(n, nb, Q_BLOCK, h, B_NOPE_DIM).transpose(1, 0, 2, 3, 4)
    qp = q_pe.reshape(n, nb, Q_BLOCK, h, B_ROPE_DIM).transpose(1, 0, 2, 3, 4)
    kpos = jnp.arange(s_len)

    def one_block(args):
        qn_b, qp_b, b = args
        s = (jnp.einsum('nqhe,nkhe->nhqk', qn_b, k_nope, preferred_element_type=jnp.float32)
             + jnp.einsum('nqhr,nkr->nhqk', qp_b, kpe, preferred_element_type=jnp.float32)) * scale
        qpos = b * Q_BLOCK + jnp.arange(Q_BLOCK)
        p, _ = masked_softmax(s, kpos[None, :] <= qpos[:, None])
        return jnp.einsum('nhqk,nkhe->nqhe', p.astype(v.dtype), v, preferred_element_type=jnp.float32)

    o = lax.map(one_block, (qn, qp, jnp.arange(nb)))
    return o.transpose(1, 0, 2, 3, 4).reshape(n, s_len, h, B_V_DIM)

def mla_sample(q_nope, q_pe, ckv_ext, kpe_ext, w_uk, w_uv):
    t = q_nope.shape[1]
    l = ckv_ext.shape[1]
    scale = (B_NOPE_DIM + B_ROPE_DIM) ** -0.5
    q_lat = jnp.einsum('nthe,che->nthc', q_nope, w_uk)
    s = (jnp.einsum('nthc,nkc->nhtk', q_lat, ckv_ext, preferred_element_type=jnp.float32)
         + jnp.einsum('nthr,nkr->nhtk', q_pe, kpe_ext, preferred_element_type=jnp.float32)) * scale
    qpos = l - t + jnp.arange(t)
    p, _ = masked_softmax(s, jnp.arange(l)[None, :] <= qpos[:, None])
    o_lat = jnp.einsum('nhtk,nkc->nthc', p.astype(ckv_ext.dtype), ckv_ext, preferred_element_type=jnp.float32)
    return jnp.einsum('nthc,che->nthe', o_lat.astype(w_uv.dtype), w_uv)

def finish_layer(x, o_a, o_b, ga, gb, p_emb, w_oa, w_ob, w_o, g_ffn, w_up, w_down, g_ple, w_ple_gate, w_ple):
    n, t = x.shape[0], x.shape[1]
    ya = o_a.reshape(n, t, A_WIDTH).astype(x.dtype) @ w_oa
    yb = o_b.reshape(n, t, B_HEADS * B_V_DIM).astype(x.dtype) @ w_ob
    x = x + (jax.nn.sigmoid(ga) * ya + jax.nn.sigmoid(gb) * yb) @ w_o
    x = x + jnp.square(jax.nn.relu(rms_norm(x, g_ffn) @ w_up)) @ w_down
    x = x + jax.nn.sigmoid(rms_norm(x, g_ple) @ w_ple_gate) * (p_emb @ w_ple)
    return x

def setup_inputs(seed: int = 0) -> dict:
    key = jax.random.key(seed)
    ks = jax.random.split(key, 26)
    n_pages = PAST_LEN // PAGE_SIZE
    n_used = DEC_BATCH * n_pages
    n_phys = (5 * n_used + 3) // 4
    wb = min(A_MAX_WINDOW, PAST_LEN)
    f32 = jnp.float32

    def nrm(k, shape, scale=1.0):
        return jax.random.normal(k, shape, f32) * scale

    def gain(k, shape):
        return 1.0 + 0.05 * jax.random.normal(k, shape, f32)

    page_table = jax.random.permutation(ks[6], n_phys)[:n_used].reshape(DEC_BATCH, n_pages).astype(jnp.int32)
    return {
        'x_prompt': nrm(ks[0], (BATCH, SEQ, D_MODEL)),
        'x_sample': nrm(ks[1], (DEC_BATCH, DEC_SEQ, D_MODEL)),
        'cache_win_k': nrm(ks[2], (DEPTH, DEC_BATCH, wb, A_HEADS, A_HEAD_DIM)),
        'cache_win_v': nrm(ks[3], (DEPTH, DEC_BATCH, wb, A_HEADS, A_HEAD_DIM)),
        'cache_ckv': nrm(ks[4], (DEPTH, n_phys, PAGE_SIZE, B_KV_LORA)),
        'cache_kpe': nrm(ks[5], (DEPTH, n_phys, PAGE_SIZE, B_ROPE_DIM)),
        'page_table': page_table,
        'p_prompt': nrm(ks[7], (DEPTH, BATCH, SEQ, PLE_DIM)),
        'p_sample': nrm(ks[8], (DEPTH, DEC_BATCH, DEC_SEQ, PLE_DIM)),
        'g_mix': gain(ks[9], (DEPTH, D_MODEL)),
        'w_in': nrm(ks[10], (DEPTH, D_MODEL, D_IN), D_MODEL ** -0.5),
        'g_q': gain(ks[11], (DEPTH, B_Q_LORA)),
        'w_uq': nrm(ks[12], (DEPTH, B_Q_LORA, B_HEADS * (B_NOPE_DIM + B_ROPE_DIM)), B_Q_LORA ** -0.5),
        'g_kv': gain(ks[13], (DEPTH, B_KV_LORA)),
        'w_uk': nrm(ks[14], (DEPTH, B_KV_LORA, B_HEADS, B_NOPE_DIM), B_KV_LORA ** -0.5),
        'w_uv': nrm(ks[15], (DEPTH, B_KV_LORA, B_HEADS, B_V_DIM), B_KV_LORA ** -0.5),
        'w_oa': nrm(ks[16], (DEPTH, A_WIDTH, D_MODEL), A_WIDTH ** -0.5),
        'w_ob': nrm(ks[17], (DEPTH, B_HEADS * B_V_DIM, D_MODEL), (B_HEADS * B_V_DIM) ** -0.5),
        'w_o': nrm(ks[18], (DEPTH, D_MODEL, D_MODEL), D_MODEL ** -0.5),
        'g_ffn': gain(ks[19], (DEPTH, D_MODEL)),
        'w_up': nrm(ks[20], (DEPTH, D_MODEL, D_FF), D_MODEL ** -0.5),
        'w_down': nrm(ks[21], (DEPTH, D_FF, D_MODEL), D_FF ** -0.5),
        'g_ple': gain(ks[22], (DEPTH, D_MODEL)),
        'w_ple_gate': nrm(ks[23], (DEPTH, D_MODEL, D_MODEL), D_MODEL ** -0.5),
        'w_ple': nrm(ks[24], (DEPTH, PLE_DIM, D_MODEL), PLE_DIM ** -0.5),
        'g_final': gain(ks[25], (D_MODEL,)),
    }

def reference(x_prompt, x_sample, cache_win_k, cache_win_v, cache_ckv, cache_kpe, page_table,
              p_prompt, p_sample, g_mix, w_in, g_q, w_uq, g_kv, w_uk, w_uv, w_oa, w_ob, w_o,
              g_ffn, w_up, w_down, g_ple, w_ple_gate, w_ple, g_final):
    s_len = x_prompt.shape[1]
    n_dec, t_dec = x_sample.shape[0], x_sample.shape[1]
    past_len = page_table.shape[1] * cache_ckv.shape[2]
    pos_p = jnp.arange(s_len, dtype=jnp.int32)
    pos_s = past_len + jnp.arange(t_dec, dtype=jnp.int32)
    keep_p = min(A_MAX_WINDOW, s_len)
    xp, xs = x_prompt, x_sample
    wkp, wvp, ckvp, kpep, wks, wvs, ckvs, kpes = [], [], [], [], [], [], [], []
    for i in range(DEPTH):
        qa, ka, va, qn, qpe, ckv, kpe, ga, gb = in_projection(
            rms_norm(xp, g_mix[i]), pos_p, w_in[i], g_q[i], w_uq[i], g_kv[i])
        o_a = combine_patterns([dilated_attn_prompt(qa, ka, va, w, d) for w, d in A_PATTERNS])
        o_b = mla_prompt(qn, qpe, ckv, kpe, w_uk[i], w_uv[i])
        wkp.append(ka[:, s_len - keep_p:])
        wvp.append(va[:, s_len - keep_p:])
        ckvp.append(ckv)
        kpep.append(kpe)
        xp = finish_layer(xp, o_a, o_b, ga, gb, p_prompt[i], w_oa[i], w_ob[i], w_o[i],
                          g_ffn[i], w_up[i], w_down[i], g_ple[i], w_ple_gate[i], w_ple[i])
        qa, ka, va, qn, qpe, ckv, kpe, ga, gb = in_projection(
            rms_norm(xs, g_mix[i]), pos_s, w_in[i], g_q[i], w_uq[i], g_kv[i])
        k_ext = jnp.concatenate([cache_win_k[i], ka], axis=1)
        v_ext = jnp.concatenate([cache_win_v[i], va], axis=1)
        o_a = combine_patterns([dilated_attn_sample(qa, k_ext, v_ext, w, d) for w, d in A_PATTERNS])
        ckv_past = cache_ckv[i][page_table].reshape(n_dec, past_len, B_KV_LORA)
        kpe_past = cache_kpe[i][page_table].reshape(n_dec, past_len, B_ROPE_DIM)
        o_b = mla_sample(qn, qpe, jnp.concatenate([ckv_past, ckv], axis=1),
                         jnp.concatenate([kpe_past, kpe], axis=1), w_uk[i], w_uv[i])
        keep_s = min(A_MAX_WINDOW, k_ext.shape[1])
        wks.append(k_ext[:, k_ext.shape[1] - keep_s:])
        wvs.append(v_ext[:, v_ext.shape[1] - keep_s:])
        ckvs.append(ckv)
        kpes.append(kpe)
        xs = finish_layer(xs, o_a, o_b, ga, gb, p_sample[i], w_oa[i], w_ob[i], w_o[i],
                          g_ffn[i], w_up[i], w_down[i], g_ple[i], w_ple_gate[i], w_ple[i])
    y_prompt = rms_norm(xp, g_final)
    y_sample = rms_norm(xs, g_final)
    return (y_prompt, y_sample, jnp.stack(wkp), jnp.stack(wvp), jnp.stack(ckvp), jnp.stack(kpep),
            jnp.stack(wks), jnp.stack(wvs), jnp.stack(ckvs), jnp.stack(kpes))


_drawn_inputs = setup_inputs


def setup_inputs(seed=0):
    import zlib

    import numpy as np

    out = dict(_drawn_inputs(seed))
    spreads = {}
    factors = {'cache_kpe': 3.624, 'g_q': 8.0, 'g_ple': 22.136}
    for name, (base, spread) in spreads.items():
        noise = np.random.default_rng([zlib.crc32(name.encode()), seed]).standard_normal(out[name].shape)
        drawn = base * np.exp(spread * noise) if base else spread * noise
        out[name] = __import__('jax').numpy.asarray(drawn.astype(out[name].dtype))
    for name, factor in factors.items():
        out[name] = (out[name] * factor).astype(out[name].dtype)
    return out
```

```python
from contextlib import ExitStack

import numpy as np

import concourse.bass as bass
from concourse import mybir

F32 = mybir.dt.float32
F32R = mybir.dt.float32r
I32 = mybir.dt.int32
ALU = mybir.AluOpType
ACT = mybir.ActivationFunctionType
AX_X = mybir.AxisListType.X

P = 128
D = 1024
SEQ = 1024
NSEQ, TDEC = 8, 4
NS = NSEQ * TDEC
T = SEQ + NS
NT = SEQ // P + 1
ROWS = [P] * (NT - 1) + [NS]
CH = 352
NCH = T // CH
KD = D // P
H = 8
E = 64
PATTERNS = ((128, 1), (512, 4), (2048, 16))
QL, KL, RD = 384, 256, 32
BH = E + RD
FF = 4 * D
NF = FF // D
PLE = 256
PAST, PAGE = 1024, 128
NPAGE = PAST // PAGE
NPHYS = (5 * NSEQ * NPAGE + 3) // 4
EPS = 1e-6
NEG = -1e30
BLK_COLS = [(1536, QL), (1920, KL + RD), (0, 512), (512, 512), (1024, 512)]
GATE_COL = 2208
SK = 5
SKEYS = SK * P + TDEC
FLOOR = -3e38



BYTES = 4
BASE = 16512
MAIN = BASE + 7168
R1 = MAIN
R2 = R1 + 2 * KD * T * BYTES
RX = R2 + 2 * KD * T * BYTES
RW = RX + KD * T * BYTES
RM = RW + 6 * KD * P * BYTES
TOP = 229368
R_CQ = (TOP - NT * (QL + KL + RD) * BYTES) // 32 * 32 - 64


class Room:

    def __init__(self, nc, start, end=TOP):
        self.nc, self.next, self.end = nc, start, end

    def __call__(self, name, shape, dt=F32):
        size = -(-int(np.prod(shape[1:])) * BYTES // 32) * 32
        assert self.next + size <= self.end, (name, self.next + size, self.end)
        made = self.nc.alloc_sbuf_tensor_at(name, list(shape), dt, offset=self.next)
        self.next += size
        return made


class Program:

    def __init__(self, nc, io):
        self.nc = nc
        self.x_prompt = io["x_prompt"]
        self.x_sample = io["x_sample"]
        self.cache_win_k = io["cache_win_k"]
        self.cache_win_v = io["cache_win_v"]
        self.cache_ckv = io["cache_ckv"]
        self.cache_kpe = io["cache_kpe"]
        self.page_table = io["page_table"]
        self.p_prompt = io["p_prompt"]
        self.p_sample = io["p_sample"]
        self.g_mix = io["g_mix"]
        self.w_in = io["w_in"]
        self.g_q = io["g_q"]
        self.w_uq = io["w_uq"]
        self.g_kv = io["g_kv"]
        self.w_uk = io["w_uk"]
        self.w_uv = io["w_uv"]
        self.w_oa = io["w_oa"]
        self.w_ob = io["w_ob"]
        self.w_o = io["w_o"]
        self.g_ffn = io["g_ffn"]
        self.w_up = io["w_up"]
        self.w_down = io["w_down"]
        self.g_ple = io["g_ple"]
        self.w_ple_gate = io["w_ple_gate"]
        self.w_ple = io["w_ple"]
        self.g_final = io["g_final"]
        self.ident_c = io["ident_c"]
        self.cos_a_c = io["cos_a_c"]
        self.sin_a_c = io["sin_a_c"]
        self.cos_b_c = io["cos_b_c"]
        self.sin_b_c = io["sin_b_c"]
        self.mask_w_c = io["mask_w_c"]
        self.mask_b_c = io["mask_b_c"]
        self.mask_ws_c = io["mask_ws_c"]
        self.mask_ls_c = io["mask_ls_c"]
        self.y_prompt = io["y_prompt"]
        self.y_sample = io["y_sample"]
        self.win_k_prompt = io["win_k_prompt"]
        self.win_v_prompt = io["win_v_prompt"]
        self.ckv_prompt = io["ckv_prompt"]
        self.kpe_prompt = io["kpe_prompt"]
        self.win_k_sample = io["win_k_sample"]
        self.win_v_sample = io["win_v_sample"]
        self.ckv_sample = io["ckv_sample"]
        self.kpe_sample = io["kpe_sample"]


def build(nc, io):
    with ExitStack() as ctx:
        g = Program(nc, io)
        g.stage_sems = []

        def sem(name):
            g.stage_sems.append(nc.alloc_semaphore(name=name))
            return g.stage_sems[-1]

        g.sem = sem
        g.bank = ctx.enter_context(nc.psum_tensor("bank", [P, 8, 512], F32))
        dram = lambda name, shape: nc.dram_tensor(name, shape, F32, kind="Internal").ap()
        g.xt_d = dram("xt_d", (P, KD, T))
        g.p_t_d = dram("p_t_d", (P, 2, T))
        g.gate_d = dram("gate_d", (2, KD, P, T))
        g.q_d = dram("q_d", (T, H * E))
        g.k_d = dram("k_d", (T, H * E))
        g.v_d = dram("v_d", (T, H * E))
        room = Room(nc, BASE, MAIN)
        g.ident = room("ident", [P, P])
        g.ones = room("ones", [P, P])
        g.nhalf = room("nhalf", [P, 1])
        g.gains = room("gains", [P, 4, KD])
        g.rstd_bc = room("rstd_bc", [P, T])
        g.rstd = room("rstd", [P, NT])
        g.rstd8 = room("rstd8", [P, NT])
        g.sq = room("tail_square", [P, CH])
        g.w_loaded = [ctx.enter_context(nc.semaphore(f"w_loaded{j}")) for j in range(2)]
        g.w_hi, g.w_split, g.full, g.free = (
            ctx.enter_context(nc.semaphore(n)) for n in ("w_hi", "w_split", "full", "free"))
        g.units = g.chunks = g.turns = 0
        room = Room(nc, R1, R2)
        g.h_hi = room("h_hi", [P, KD, T], F32R)
        g.h_lo = room("h_lo", [P, KD, T], F32R)
        room = Room(nc, R_CQ)
        g.cq = room("cq", [P, NT, QL])
        g.ckv = room("ckv", [P, NT, KL + RD])
        load_tokens(g)
        project_natural(g)
        project_gates(g)
        room = Room(nc, R1, R2)
        g.o_hi = room("o_hi", [P, KD, T], F32R)
        g.o_lo = room("o_lo", [P, KD, T], F32R)
        room = Room(nc, R2)
        g.qb_t = room("qb_t", [BH, H, T])
        g.kb_t = room("kb_t", [BH, H, SEQ])
        g.vb = room("vb", [P, NT - 1, H * E])
        g.room_kept = room.next
        g.w_uv_sb = room("w_uv_sb", [P, 2, H * E])
        g.ckv_t = room("ckv_t", [P, 2, T])
        g.kpe_t = room("kpe_t", [RD, NS])
        g.ql_t = room("ql_t", [P, 2, NSEQ, H, TDEC])
        g.qpe_t = room("qpe_t", [RD, NSEQ, H, TDEC])
        g.room_b = room.next
        project_latents(g)
        renew_semaphores(g)
        attend_prompt(g, "latent")
        attend_sample(g, "latent")
        attend_prompt(g, "window")
        attend_sample(g, "window")
        renew_semaphores(g)
        run_tail(g)
        nc.clear_and_free_semaphores(g.stage_sems)


def renew_semaphores(g):
    g.nc.clear_and_free_semaphores(g.stage_sems)
    g.stage_sems.clear()
    g.nc.all_engine_barrier()


def load_tokens(g):
    nc = g.nc
    room = Room(nc, R2, R_CQ)
    x_nat = room("x_nat", [P, 3, D])
    x_t = room("x_t", [P, KD, T])
    p_nat = room("p_nat", [P, 2, PLE])
    p_t = room("p_t", [P, 2, T])
    square = room("square", [P, D])
    hg = room("hg", [P, 2, KD // 2, P])
    stat = room("stat", [P, NT])
    diag = room("diag", [P, 2, P])
    gain_nat = room("gain_nat", [4 * KD, P])
    consts, x_squared, tr, t_copied, hg_ready, hi_done, lo_done, stat_ready, \
        rstd_ready, diag_ready, bc_full, stored, gain_in, gain_t, set_up, got_gain = map(
            g.sem, ("consts", "x_squared", "tr", "t_copied", "hg_ready", "hi_done",
                    "lo_done", "stat_ready", "rstd_ready", "diag_ready", "bc_full", "stored",
                    "gain_in", "gain_t", "set_up", "got_gain"))
    x_in = [g.sem(f"x_in{j}") for j in range(3)]
    p_in = [g.sem(f"p_in{j}") for j in range(2)]
    p_full, p_got = g.sem("p_full"), g.sem("p_got")
    with nc.Block() as block:

        @block.sync
        def _(sp):
            sp.dma_start(g.ident[:, :], g.ident_c).then_inc(consts, 16)
            for n, gain in enumerate((g.g_mix, g.g_ffn, g.g_ple, g.g_final)):
                row = gain if n == 3 else gain[0, :]
                sp.dma_start(gain_nat[n * KD:(n + 1) * KD, :], row.rearrange("(k p) -> k p", p=P)).then_inc(gain_in, 16)
            for t in range(NT):
                if t >= 3:
                    sp.wait_ge(tr, 2 * (t - 2))
                    sp.wait_ge(x_squared, t - 2)
                src = g.x_prompt[0, t * P:(t + 1) * P, :] if t < NT - 1 else g.x_sample.rearrange("n t d -> (n t) d")
                sp.dma_start(x_nat[:ROWS[t], t % 3, :], src).then_inc(x_in[t % 3], 16)
            for t in range(NT):
                if t >= 2:
                    sp.wait_ge(p_full, t - 1)
                src = g.p_prompt[0, 0, t * P:(t + 1) * P, :] if t < NT - 1 else g.p_sample[0].rearrange("s t c -> (s t) c")
                sp.dma_start(p_nat[:ROWS[t], t % 2, :], src).then_inc(p_in[t % 2], 16)
            sp.wait_ge(t_copied, 2 * NT)
            sp.dma_start(g.xt_d, x_t[:, :, :]).then_inc(stored, 16)
            sp.wait_ge(p_got, NT)
            sp.dma_start(g.p_t_d, p_t[:, :, :]).then_inc(stored, 16)
            sp.wait_ge(stored, 32)

        @block.tensor
        def _(pe):
            pe.wait_ge(consts, 16)
            pe.wait_ge(gain_in, 64)
            pe.transpose(g.bank[:, 7, 0:4 * KD], gain_nat[:, :], g.ident[:4 * KD, :4 * KD]).then_inc(gain_t, 1)
            for t in range(NT):
                pe.wait_ge(x_in[t % 3], 16 * (t // 3 + 1))
                for half in range(2):
                    n = 2 * t + half
                    if n >= 4:
                        pe.wait_ge(hg_ready, n - 3)
                    for k in range(4):
                        at = (4 * half + k) * P
                        last = pe.transpose(g.bank[:, n % 4, k * P:k * P + ROWS[t]],
                                            x_nat[:ROWS[t], t % 3, at:at + P], g.ident[:ROWS[t], :ROWS[t]])
                    last.then_inc(tr, 1)
            for t in range(NT):
                pe.wait_ge(diag_ready, t + 1)
                pe.matmul(g.bank[:, 4 + t // 3, (t % 3) * P:(t % 3) * P + ROWS[t]], g.ones[:ROWS[t], :],
                          diag[:ROWS[t], t % 2, :ROWS[t]], start=True, stop=True).then_inc(bc_full, 1)
            for t in range(NT):
                r = ROWS[t]
                pe.wait_ge(p_in[t % 2], 16 * (t // 2 + 1))
                if t >= 2:
                    pe.wait_ge(p_got, t - 1)
                for k in range(2):
                    last = pe.transpose(g.bank[:, t % 2, k * P:k * P + r], p_nat[:r, t % 2, k * P:(k + 1) * P], g.ident[:r, :r])
                last.then_inc(p_full, 1)

        @block.vector
        def _(dve):
            dve.memset(g.ones[:, :], 1.0)
            dve.memset(g.nhalf[:, :], -0.5)
            dve.memset(stat[:, :], float(D)).then_inc(set_up, 1)
            dve.wait_ge(gain_t, 1)
            dve.tensor_copy(g.gains[:, :, :].rearrange("p a b -> p (a b)"), g.bank[:, 7, 0:4 * KD]).then_inc(got_gain, 1)
            dve.wait_ge(got_gain, 1)
            for t in range(NT):
                for half in range(2):
                    n = 2 * t + half
                    r = ROWS[t]
                    dve.wait_ge(tr, n + 1)
                    got = g.bank[:, n % 4, :].rearrange("p (k c) -> p k c", k=4)[:, :, :r]
                    ks = slice(4 * half, 4 * half + 4)
                    dve.tensor_copy(x_t[:, ks, t * P:t * P + r], got).then_inc(t_copied, 1)
                    if n >= 2:
                        dve.wait_ge(lo_done, n - 1)
                    gain = g.gains[:, 0, ks].unsqueeze(2).to_broadcast([P, 4, r])
                    dve.tensor_tensor(hg[:, n % 2, :, :r], got, gain, ALU.mult).then_inc(hg_ready, 1)
            dve.wait_ge(rstd_ready, 1)
            dve.tensor_scalar(g.rstd8[:, :], g.rstd[:, :], E ** -0.5, None, ALU.mult)
            for t in range(NT):
                if t >= 2:
                    dve.wait_ge(bc_full, t - 1)
                dve.tensor_scalar(diag[:, t % 2, :], g.ident[:, :], g.rstd[:, t:t + 1], None, ALU.mult).then_inc(diag_ready, 1)
            for t in range(NT):
                dve.wait_ge(bc_full, min(NT, 3 * (t // 3) + 3))
                dve.tensor_copy(g.rstd_bc[:, t * P:t * P + ROWS[t]],
                                g.bank[:, 4 + t // 3, (t % 3) * P:(t % 3) * P + ROWS[t]])
            for t in range(NT):
                dve.wait_ge(p_full, t + 1)
                dve.tensor_copy(p_t[:, :, t * P:t * P + ROWS[t]],
                                g.bank[:, t % 2, :2 * P].rearrange("p (k c) -> p k c", k=2)[:, :, :ROWS[t]]).then_inc(p_got, 1)

        @block.scalar
        def _(act):
            act.wait_ge(set_up, 1)
            for t in range(NT):
                act.wait_ge(x_in[t % 3], 16 * (t // 3 + 1))
                if t >= 1:
                    act.wait_ge(x_squared, t)
                act.activation(square[:ROWS[t], :], x_nat[:ROWS[t], t % 3, :], ACT.Square,
                               accum_out=stat[:ROWS[t], t:t + 1]).then_inc(x_squared, 1)
                for half in range(2):
                    n = 2 * t + half
                    act.wait_ge(hg_ready, n + 1)
                    act.activation(g.h_hi[:, 4 * half:4 * half + 4, t * P:t * P + ROWS[t]], hg[:, n % 2, :, :ROWS[t]],
                                   ACT.Copy).then_inc(hi_done, 1)

        @block.gpsimd
        def _(pool):
            for n in range(2 * NT):
                t, half = divmod(n, 2)
                pool.wait_ge(hi_done, n + 1)
                where = (slice(None), slice(4 * half, 4 * half + 4), slice(t * P, t * P + ROWS[t]))
                pool.tensor_tensor(g.h_lo[where], hg[:, n % 2, :, :ROWS[t]], g.h_hi[where].bitcast(F32),
                                   ALU.subtract).then_inc(lo_done, 1)
            pool.wait_ge(x_squared, NT)
            inverse_root(pool, g, g.rstd[:, :], stat[:, :], 1.0 / D, stat_ready, 1, rstd_ready)


def inverse_root(pool, g, out, total, scale, scaled, at, done):
    pool.tensor_scalar(out, total, scale, EPS, ALU.mult, ALU.add).then_inc(scaled, 1)
    pool.wait_ge(scaled, at)
    half = g.nhalf[:out.shape[0], :].to_broadcast(list(out.shape))
    pool.tensor_tensor(out, out, half, ALU.pow).then_inc(done, 1)


def project_natural(g):
    nc = g.nc
    room = Room(nc, R2, R_CQ)
    w_st = room("wn_st", [P, KD, 512])
    w_hi = room("wn_hi", [P, 2, KD, 512], F32R)
    w_lo = room("wn_lo", [P, 2, KD, 512], F32R)
    nat = room("nat", [P, 3, 512])
    ra = room("rope_a", [P, 2, H, 8])
    rb = room("rope_b", [P, 2, H, 8])
    cos_a = room("cos_a", [P, NT, 8])
    sin_a = room("sin_a", [P, NT, 8])
    wn_in, wn_hi, wn_lo, n_full, n_got, roped, tabs, copies, ra_s = map(
        g.sem, ("wn_in", "wn_hi", "wn_lo", "n_full", "n_got", "roped", "tabs", "copies", "ra_s"))
    nat_out = [g.sem(f"nat_out{j}") for j in range(3)]
    dest = {2: (g.q_d, None), 3: (g.k_d, g.win_k_prompt), 4: (g.v_d, g.win_v_prompt)}
    steps = [(b, t) for b in range(5) for t in range(NT)]
    stored = [s for s in steps if s[0] >= 2]

    def written(m, place):
        return 16 * sum(1 if stored[n][0] == 2 else 2 for n in range(place, m, 3))

    with nc.Block() as block:

        @block.sync
        def _(sp):
            for tab, src in ((cos_a, g.cos_a_c), (sin_a, g.sin_a_c)):
                sp.dma_start(tab[:, :, :], src).then_inc(tabs, 16)
            for b, (c0, n) in enumerate(BLK_COLS):
                if b >= 1:
                    sp.wait_ge(wn_lo, b)
                sp.dma_start(w_st[:, :, :n], g.w_in[0, :, c0:c0 + n].rearrange("(k p) n -> p k n", p=P)).then_inc(wn_in, 16)
                if b == 0:
                    for cache, out in ((g.cache_win_k, g.win_k_sample), (g.cache_win_v, g.win_v_sample)):
                        sp.dma_start(out[0, :, 0:PAST, :, :].rearrange("n s h e -> n s (h e)"),
                                     cache[0].rearrange("n s h e -> n s (h e)")).then_inc(copies, 16)
            sp.wait_ge(copies, 32)

        @block.gpsimd
        def _(pool):
            for b, (c0, n) in enumerate(BLK_COLS):
                pool.wait_ge(wn_in, 16 * (b + 1))
                if b >= 2:
                    pool.wait_ge(n_full, NT * (b - 1))
                pool.tensor_copy(w_hi[:, b % 2, :, :n], w_st[:, :, :n]).then_inc(wn_hi, 1)
                pool.wait_ge(wn_hi, b + 1)
                pool.tensor_tensor(w_lo[:, b % 2, :, :n], w_st[:, :, :n], w_hi[:, b % 2, :, :n].bitcast(F32),
                                   ALU.subtract).then_inc(wn_lo, 1)

        @block.tensor
        def _(pe):
            for s, (b, t) in enumerate(steps):
                n = BLK_COLS[b][1]
                if t == 0:
                    pe.wait_ge(wn_lo, b + 1)
                if s >= 4:
                    pe.wait_ge(n_got, s - 3)
                toks = slice(t * P, t * P + ROWS[t])
                out = g.bank[:ROWS[t], s % 4, :n]
                for k in range(KD):
                    a, c = g.h_hi[:, k, toks], g.h_lo[:, k, toks]
                    w, v = w_hi[:, b % 2, k, :n], w_lo[:, b % 2, k, :n]
                    pe.matmul(out, a, w, start=k == 0, stop=False)
                    pe.matmul(out, a, v, start=False, stop=False)
                    last = pe.matmul(out, c, w, start=False, stop=k == KD - 1)
                last.then_inc(n_full, 1)

        @block.scalar
        def _(act):
            for s, (b, t) in enumerate(steps):
                r, n = ROWS[t], BLK_COLS[b][1]
                act.wait_ge(n_full, s + 1)
                if b < 2:
                    out = (g.cq, g.ckv)[b][:r, t, :]
                else:
                    m = s - 2 * NT
                    if m >= 3:
                        act.wait_ge(nat_out[m % 3], written(m, m % 3))
                    out = nat[:r, m % 3, :]
                factor = g.rstd8 if b == 2 else g.rstd
                act.activation(out, g.bank[:r, s % 4, :n], ACT.Copy, scale=factor[:r, t:t + 1]).then_inc(n_got, 1)
                if b >= 2:
                    if b < 4:
                        act.wait_ge(roped, m + 1)
                    else:
                        act.wait_ge(n_got, s + 1)
                    scratch, result = dest[b]
                    act.dma_start(scratch[t * P:t * P + r, :], out).then_inc(nat_out[m % 3], 16)
                    if result is not None:
                        o = result[0, 0, t * P:t * P + r, :, :].rearrange("s h e -> s (h e)") if t < NT - 1 else None
                        if o is not None:
                            act.dma_start(o, out).then_inc(nat_out[m % 3], 16)
                        else:
                            last = (g.win_k_sample if b == 3 else g.win_v_sample)
                            act.dma_start(last[0, :, PAST:PAST + TDEC, :, :].rearrange("n s h e -> n s (h e)"),
                                          out).then_inc(nat_out[m % 3], 16)
            for j in range(3):
                act.wait_ge(nat_out[j], written(len(stored), j))

        @block.vector
        def _(dve):
            dve.wait_ge(tabs, 32)
            for m, (b, t) in enumerate(stored):
                if b == 4:
                    break
                r = ROWS[t]
                dve.wait_ge(n_got, 2 * NT + m + 1)
                rotate(dve, nat[:r, m % 3, :].rearrange("p (h e) -> p h e", e=E), 8,
                       cos_a[:r, t, :], sin_a[:r, t, :], ra[:r], rb[:r], H, ra_s, 2 * m, roped, m)


def rotate(dve, x, half, cos, sin, ra, rb, heads, step, at, done, turn):
    shape = [x.shape[0], heads, half]
    c, s = cos.unsqueeze(1).to_broadcast(shape), sin.unsqueeze(1).to_broadcast(shape)
    x1, x2 = x[:, :, 0:half], x[:, :, half:2 * half]
    if turn:
        dve.wait_ge(done, turn)
    dve.tensor_tensor(ra[:, 0], x1, c, ALU.mult)
    dve.tensor_tensor(ra[:, 1], x2, c, ALU.mult)
    dve.tensor_tensor(rb[:, 0], x2, s, ALU.mult)
    dve.tensor_tensor(rb[:, 1], x1, s, ALU.mult).then_inc(step, 1)
    dve.wait_ge(step, at + 1)
    dve.tensor_tensor(x1, ra[:, 0], rb[:, 0], ALU.subtract).then_inc(step, 1)
    dve.wait_ge(step, at + 2)
    dve.tensor_tensor(x2, ra[:, 1], rb[:, 1], ALU.add).then_inc(done, 1)


def multiply_chunk(pe, g, bank, j, c, ks, act_hi, act_lo):
    out = g.bank[:, bank, :CH]
    cols = slice(c * CH, (c + 1) * CH)
    for n, (kw, ka) in enumerate(ks):
        w, v = g.wu_hi[:, j, kw], g.wu_lo[:, j, kw]
        a, b = act_hi[:, ka, cols], act_lo[:, ka, cols]
        pe.matmul(out, w, a, start=n == 0, stop=False)
        pe.matmul(out, w, b, start=False, stop=False)
        last = pe.matmul(out, v, a, start=False, stop=n == len(ks) - 1)
    last.then_inc(g.full, 1)


def unit_room(g, room, tag):
    g.w_stage = room(f"w_stage_{tag}", [P, 2, KD, P])
    g.wu_hi = room(f"wu_hi_{tag}", [P, 2, KD, P], F32R)
    g.wu_lo = room(f"wu_lo_{tag}", [P, 2, KD, P], F32R)


def columns(w, m):
    return w.rearrange("(k p) c -> p k c", p=P)[:, :, bass.ds(m * P, P)]


def in_pairs(eng, n, body, peel=True):
    if peel:
        body(0)
    with eng.Fori(1 if peel else 0, n // 2) as i:
        body(i)


def first(i):
    return isinstance(i, int) and i == 0


def project_gates(g):
    nc = g.nc
    room = Room(nc, R2, R_CQ)
    unit_room(g, room, "gates")
    scaled = room("gt_scaled", [P, 2, CH])
    gate = room("gate_out", [P, 2, T])
    n = 2 * KD
    U, C = g.units, g.chunks
    scaled_ready, gate_ready = g.sem("gt_scaled_s"), g.sem("gt_ready")
    gate_out = [g.sem(f"gt_out{j}") for j in range(2)]
    gates = g.w_in[0].rearrange("(k p) c -> p k c", p=P)
    dst = g.gate_d.rearrange("a k p t -> (a k) p t")
    with nc.Block() as block:

        @block.sync
        def _(sp):
            def pair(i):
                for j in range(2):
                    if not first(i):
                        sp.wait_ge(g.w_split, i * 2 + U + j - 1)
                    sp.dma_start(g.w_stage[:, j], gates[:, :, bass.ds(i * 256 + GATE_COL + j * P, P)]).then_inc(g.w_loaded[j], 16)
            in_pairs(sp, n, pair)

        @block.gpsimd
        def _(pool):
            def pair(i):
                for j in range(2):
                    pool.wait_ge(g.w_loaded[j], i * 16 + 16)
                    if not first(i):
                        pool.wait_ge(g.full, i * 6 + C + 3 * j - 3)
                    split_weights(pool, g, j, i * 2 + U + j + 1)
            in_pairs(pool, n, pair)

        @block.tensor
        def _(pe):
            def pair(i):
                for j in range(2):
                    pe.wait_ge(g.w_split, i * 2 + U + j + 1)
                    for c in range(NCH):
                        if not first(i):
                            pe.wait_ge(g.free, i * 6 + C + 3 * j + c - 5)
                        multiply_chunk(pe, g, 3 * j + c, j, c, [(k, k) for k in range(KD)], g.h_hi, g.h_lo)
            in_pairs(pe, n, pair)

        @block.vector
        def _(dve):
            def pair(i):
                for q in range(6):
                    c = q % 3
                    dve.wait_ge(g.full, i * 6 + C + q + 1)
                    if not (first(i) and q < 2):
                        dve.wait_ge(gate_ready, i * 6 + q - 1)
                    dve.tensor_tensor(scaled[:, q % 2, :], g.bank[:, q, :CH], g.rstd_bc[:, c * CH:(c + 1) * CH],
                                      ALU.mult).then_inc(g.free, 1)
            in_pairs(dve, n, pair)

        @block.scalar
        def _(act):
            def pair(i):
                for q in range(6):
                    j, c = divmod(q, 3)
                    act.wait_ge(g.free, i * 6 + C + q + 1)
                    if not first(i) and c == 0:
                        act.wait_ge(gate_out[j], i * 16)
                    act.activation(gate[:, j, c * CH:(c + 1) * CH], scaled[:, q % 2, :], ACT.Sigmoid).then_inc(gate_ready, 1)
                    if c == NCH - 1:
                        act.wait_ge(gate_ready, i * 6 + q + 1)
                        act.dma_start(dst[bass.ds(i * 2 + j, 1)].rearrange("a p t -> p (a t)"), gate[:, j, :]).then_inc(gate_out[j], 16)
            in_pairs(act, n, pair)
            for j in range(2):
                act.wait_ge(gate_out[j], 16 * (n // 2))
    g.units += n
    g.turns += n // 2
    g.chunks += 3 * n


def project_latents(g):
    nc = g.nc
    room = Room(nc, R1, R2)
    w_uq = room("w_uq_sb", [P, 3, H * BH])
    w_uk = room("w_uk_sb", [P, 2, H * E])
    cq_t = room("cq_t", [P, 3, T])
    q_nat = room("q_nat", [P, 2, H * BH])
    cos_b = room("cos_b", [P, NT, 16])
    sin_b = room("sin_b", [P, NT, 16])
    ra = room("lat_ra", [P, 2, H, 16])
    rb = room("lat_rb", [P, 2, H, 16])
    g_kv = room("g_kv_sb", [P, KL])
    g_q = room("g_q_sb", [P, 3])
    square = room("lat_square", [P, QL])
    stat = room("lat_stat", [P, 2, NT])
    root = room("lat_root", [P, 2, NT])
    root_q = room("lat_root_q", [P, NT])
    w_ukt = room("w_ukt", [E, H, 2, P])
    (l_in, l_set, squared, scaled, rooted, rq_done, normed, turned, l_step, out_s, cq_full, cq_got,
     ck_full, ck_got, uk_full, uk_got, qf, qg, qr, qt, qtg, kf, kg, vf, vg, lf) = map(g.sem, (
         "l_in", "l_set", "l_squared", "l_scaled", "l_rooted", "l_rq", "l_normed", "l_turned", "l_step", "l_out",
         "cq_full", "cq_got", "ck_full", "ck_got", "uk_full", "uk_got", "qb_full", "qb_got", "qb_turned",
         "qb_tr", "qb_tgot", "kn_full", "kn_got", "vb_full", "vb_got", "ql_full"))

    with nc.Block() as block:

        @block.sync
        def _(sp):
            sp.dma_start(w_uq[:, :, :], g.w_uq[0].rearrange("(k p) n -> p k n", p=P)).then_inc(l_in, 16)
            sp.dma_start(w_uk[:, :, :], g.w_uk[0].rearrange("(k p) h e -> p k (h e)", p=P)).then_inc(l_in, 16)
            sp.dma_start(g.w_uv_sb[:, :, :], g.w_uv[0].rearrange("(k p) h e -> p k (h e)", p=P)).then_inc(l_in, 16)
            sp.dma_start(cos_b[:, :, :], g.cos_b_c).then_inc(l_in, 16)
            sp.dma_start(sin_b[:, :, :], g.sin_b_c).then_inc(l_in, 16)
            sp.dma_start(g_kv[:, :], g.g_kv[0:1, :].to_broadcast([P, KL])).then_inc(l_in, 16)
            sp.dma_start(g_q[:, :], g.g_q[0].rearrange("(k p) -> p k", p=P), allow_slow_non_contiguous=True).then_inc(l_in, 16)
            for t in range(NT):
                sp.wait_ge(normed, t + 1)
                sp.wait_ge(turned, t + 1)
                if t < NT - 1:
                    sp.dma_start(g.ckv_prompt[0, 0, t * P:(t + 1) * P, :], g.ckv[:, t, :KL]).then_inc(out_s, 16)
                    sp.dma_start(g.kpe_prompt[0, 0, t * P:(t + 1) * P, :], g.ckv[:, t, KL:]).then_inc(out_s, 16)
                else:
                    sp.dma_start(g.ckv_sample[0].rearrange("n t c -> (n t) c"), g.ckv[:NS, t, :KL]).then_inc(out_s, 16)
                    sp.dma_start(g.kpe_sample[0].rearrange("n t c -> (n t) c"), g.ckv[:NS, t, KL:]).then_inc(out_s, 16)
            sp.wait_ge(out_s, 32 * NT)

        @block.scalar
        def _(act):
            act.wait_ge(l_set, 1)
            for t in range(NT):
                r = ROWS[t]
                for which, (x, w) in enumerate(((g.cq, QL), (g.ckv, KL))):
                    if t or which:
                        act.wait_ge(squared, 2 * t + which)
                    act.activation(square[:r, :w], x[:r, t, :w], ACT.Square,
                                   accum_out=stat[:r, which, t:t + 1]).then_inc(squared, 1)

        @block.gpsimd
        def _(pool):
            pool.wait_ge(squared, 2 * NT)
            inverse_root(pool, g, root[:, 0, :], stat[:, 0, :], 1.0 / QL, scaled, 1, rooted)
            inverse_root(pool, g, root[:, 1, :], stat[:, 1, :], 1.0 / KL, scaled, 2, rooted)

        @block.vector
        def _(dve):
            dve.memset(stat[:, :, :], float(QL)).then_inc(l_set, 1)
            dve.wait_ge(l_in, 7 * 16)
            for t in range(NT):
                r = ROWS[t]
                rotate(dve, g.ckv[:r, t, KL:].rearrange("p (h e) -> p h e", h=1), 16, cos_b[:r, t, :],
                       sin_b[:r, t, :], ra[:r, :, 0:1], rb[:r, :, 0:1], 1, l_step, 2 * t, turned, t)
            dve.wait_ge(rooted, 2)
            dve.tensor_scalar(root_q[:, :], root[:, 0, :], BH ** -0.5, None, ALU.mult).then_inc(rq_done, 1)
            for t in range(NT):
                r = ROWS[t]
                dve.scalar_tensor_tensor(g.ckv[:r, t, :KL], g.ckv[:r, t, :KL], root[:r, 1, t:t + 1],
                                         g_kv[:r, :], ALU.mult, ALU.mult).then_inc(normed, 1)
            for t in range(NT):
                r = ROWS[t]
                toks = slice(t * P, t * P + r)
                dve.wait_ge(cq_full, t + 1)
                dve.tensor_tensor(cq_t[:, :, toks], g.bank[:, t % 2, :3 * P].rearrange("p (k c) -> p k c", k=3)[:, :, :r],
                                  g_q[:, :].unsqueeze(2).to_broadcast([P, 3, r]), ALU.mult).then_inc(cq_got, 1)
            for t in range(NT):
                r = ROWS[t]
                toks = slice(t * P, t * P + r)
                dve.wait_ge(ck_full, t + 1)
                b = g.bank[:, 2 + t % 2, :].rearrange("p (k c) -> p k c", k=4)
                if t < NT - 1:
                    dve.tensor_copy(g.kb_t[E:BH, :, toks], b[E:BH, 2:3, :].to_broadcast([RD, H, P]))
                else:
                    dve.tensor_copy(g.kpe_t[:, :], b[:RD, 2, :r])
                dve.tensor_copy(g.ckv_t[:, :, toks], b[:, 0:2, :r]).then_inc(ck_got, 1)
            for n in range(4):
                dve.wait_ge(uk_full, n + 1)
                dve.tensor_copy(w_ukt[:, 2 * n:2 * n + 2, :, :].rearrange("e h c p -> e (h c p)"), g.bank[:E, 4 + n, :]).then_inc(uk_got, 1)

        @block.tensor
        def _(pe):
            for t in range(NT):
                r = ROWS[t]
                if t >= 2:
                    pe.wait_ge(cq_got, t - 1)
                for k in range(3):
                    last = pe.transpose(g.bank[:, t % 2, k * P:k * P + r], g.cq[:r, t, k * P:(k + 1) * P], g.ident[:r, :r])
                last.then_inc(cq_full, 1)
            pe.wait_ge(l_in, 7 * 16)
            for n in range(4):
                for m in range(4):
                    h, c = 2 * n + m // 2, m % 2
                    last = pe.transpose(g.bank[:E, 4 + n, m * P:(m + 1) * P], w_uk[:, c, h * E:(h + 1) * E], g.ident[:, :])
                last.then_inc(uk_full, 1)
            for t in range(NT):
                r = ROWS[t]
                pe.wait_ge(normed, t + 1)
                if t >= 2:
                    pe.wait_ge(ck_got, t - 1)
                for k in range(2):
                    pe.transpose(g.bank[:, 2 + t % 2, k * P:k * P + r], g.ckv[:r, t, k * P:(k + 1) * P], g.ident[:r, :r])
                w, c0 = (BH, KL - E) if t < NT - 1 else (RD, KL)
                pe.transpose(g.bank[:w, 2 + t % 2, 2 * P:2 * P + r], g.ckv[:r, t, c0:], g.ident[:r, :r]).then_inc(ck_full, 1)

    with nc.Block() as block:

        @block.tensor
        def _(pe):
            def turn(t):
                r = ROWS[t]
                pe.wait_ge(qr, t + 1)
                for half in range(2):
                    n = 2 * t + half
                    if n >= 2:
                        pe.wait_ge(qtg, n - 1)
                    for m in range(4):
                        h = 4 * half + m
                        last = pe.transpose(g.bank[:BH, 4 + half, m * P:m * P + r], q_nat[:r, t % 2, h * BH:(h + 1) * BH], g.ident[:r, :r])
                    last.then_inc(qt, 1)

            for t in range(NT):
                r = ROWS[t]
                for half in range(2):
                    n = 2 * t + half
                    if n >= 4:
                        pe.wait_ge(qg, n - 3)
                    for k in range(3):
                        last = pe.matmul(g.bank[:r, n % 4, :QL], cq_t[:, k, t * P:t * P + r], w_uq[:, k, half * QL:(half + 1) * QL],
                                         start=k == 0, stop=k == 2)
                    last.then_inc(qf, 1)
                if t >= 1:
                    turn(t - 1)
            for n in range(2 * H):
                h, half = divmod(n, 2)
                if n >= 2:
                    pe.wait_ge(kg, n - 1)
                for c in range(2):
                    last = pe.matmul(g.bank[:E, 6 + n % 2, :], w_uk[:, c, h * E:(h + 1) * E], g.ckv_t[:, c, half * 512:(half + 1) * 512],
                                     start=c == 0, stop=c == 1)
                last.then_inc(kf, 1)
                if n == 0:
                    turn(NT - 1)
            pe.wait_ge(qg, 2 * NT)
            for j in range(NT - 1):
                if j >= 4:
                    pe.wait_ge(vg, j - 3)
                for c in range(2):
                    last = pe.matmul(g.bank[:, j % 4, :], g.ckv_t[:, c, j * P:(j + 1) * P], g.w_uv_sb[:, c, :], start=c == 0, stop=c == 1)
                last.then_inc(vf, 1)
            pe.wait_ge(qtg, 2 * NT)
            for h in range(H):
                last = pe.transpose(g.bank[:RD, 4, h * NS:(h + 1) * NS], q_nat[:NS, (NT - 1) % 2, h * BH + E:(h + 1) * BH], g.ident[:NS, :NS])
            last.then_inc(lf, 1)
            for c in range(2):
                for h in range(H):
                    at = (c * H + h) * NS
                    last = pe.matmul(g.bank[:, 5, at:at + NS], w_ukt[:, h, c, :], g.qb_t[:E, h, SEQ:], start=True, stop=True)
            last.then_inc(lf, 1)

        @block.scalar
        def _(act):
            def turned_out(t):
                r = ROWS[t]
                for half in range(2):
                    act.wait_ge(qt, 2 * t + half + 1)
                    act.activation(g.qb_t[:, 4 * half:4 * half + 4, t * P:t * P + r],
                                   g.bank[:BH, 4 + half, :].rearrange("p (h c) -> p h c", h=4)[:, :, :r], ACT.Copy).then_inc(qtg, 1)

            for t in range(NT):
                r = ROWS[t]
                for half in range(2):
                    n = 2 * t + half
                    act.wait_ge(qf, n + 1)
                    if t >= 2:
                        act.wait_ge(qt, 2 * t - 2)
                    act.activation(q_nat[:r, t % 2, half * QL:(half + 1) * QL], g.bank[:r, n % 4, :QL], ACT.Copy,
                                   scale=root_q[:r, t:t + 1]).then_inc(qg, 1)
                if t >= 1:
                    turned_out(t - 1)
            turned_out(NT - 1)
            for j in range(NT - 1):
                act.wait_ge(vf, j + 1)
                act.activation(g.vb[:, j, :], g.bank[:, j % 4, :], ACT.Copy).then_inc(vg, 1)

        @block.vector
        def _(dve):
            for t in range(NT):
                r = ROWS[t]
                dve.wait_ge(qg, 2 * t + 2)
                rotate(dve, q_nat[:r, t % 2, :].rearrange("p (h e) -> p h e", e=BH)[:, :, E:], 16, cos_b[:r, t, :],
                       sin_b[:r, t, :], ra[:r], rb[:r], H, l_step, 2 * NT + 2 * t, qr, t)
            for n in range(2 * H):
                h, half = divmod(n, 2)
                dve.wait_ge(kf, n + 1)
                dve.tensor_copy(g.kb_t[:E, h, half * 512:(half + 1) * 512], g.bank[:E, 6 + n % 2, :]).then_inc(kg, 1)
            dve.wait_ge(lf, 1)
            dve.tensor_copy(g.qpe_t[:, :, :, :].rearrange("r s h t -> r h s t"),
                            g.bank[:RD, 4, :H * NS].rearrange("r (h s t) -> r h s t", h=H, s=NSEQ))
            dve.wait_ge(lf, 2)
            for c in range(2):
                dve.tensor_copy(g.ql_t[:, c].rearrange("p s h t -> p h s t"),
                                g.bank[:, 5, c * H * NS:(c + 1) * H * NS].rearrange("p (h s t) -> p h s t", h=H, s=NSEQ))


def attend_prompt(g, kind):
    nc = g.nc
    window = kind == "window"
    room = Room(nc, R2 if window else g.room_b)
    sem = lambda name: g.sem(f"{kind[0]}_{name}")
    if window:
        q_t = room("qw_t", [P, H // 2, SEQ])
        k_t = room("kw_t", [P, H // 2, SEQ])
        v = room("vw", [P, NT - 1, H * E])
        load_window(g, room, q_t, k_t, v)
        head = lambda x, h: x[E * (h % 2):E * (h % 2) + E, h // 2, :]
    else:
        q_t, k_t, v = g.qb_t, g.kb_t, g.vb
        head = lambda x, h: x[:, h, :]
    mask = room(f"{kind}_mask", [P, NT - 1, P])
    masked = room(f"{kind}_masked", [P, 2, SEQ])
    prob = room(f"{kind}_prob", [P, 2, SEQ])
    prob_t = room(f"{kind}_prob_t", [P, 2, NT - 1, P])
    top = room(f"{kind}_top", [P, 2, 4])
    mask_in, s_full, s_got, negated, e_done, inv_done, p_ready, t_full, t_got, o_full, o_hi_s, o_got = map(sem, (
        "mask_in", "s_full", "s_got", "negated", "e_done", "inv_done", "p_ready", "t_full", "t_got", "o_full", "o_hi", "o_got"))
    steps = [(h, i) for h in range(H) for i in range(NT - 1)]
    groups = []
    n = 0
    for h, i in steps:
        mine = []
        for j in range(0, i + 1, 4):
            mine.append((n, j, min(j + 4, i + 1)))
            n += 1
        groups.append(mine)
    N = len(steps)
    with nc.Block() as block:

        @block.sync
        def _(sp):
            sp.dma_start(mask[:, :, :], g.mask_w_c if window else g.mask_b_c).then_inc(mask_in, 16)

        @block.tensor
        def _(pe):
            def scores(s):
                h, i = steps[s]
                if s >= 2:
                    pe.wait_ge(s_got, s - 1)
                for at in range(0, (i + 1) * P, 512):
                    w = min(512, (i + 1) * P - at)
                    last = pe.matmul(g.bank[:, 2 * (s % 2) + at // 512, :w], head(q_t, h)[:, i * P:(i + 1) * P],
                                     head(k_t, h)[:, at:at + w], start=True, stop=True)
                last.then_inc(s_full, 1)

            def transposes(s):
                pe.wait_ge(p_ready, s + 1)
                for n, a, b in groups[s]:
                    if n >= 2:
                        pe.wait_ge(t_got, n - 1)
                    for j in range(a, b):
                        last = pe.transpose(g.bank[:, 4 + n % 2, (j - a) * P:(j - a + 1) * P],
                                            prob[:, s % 2, j * P:(j + 1) * P], g.ident[:, :])
                    last.then_inc(t_full, 1)

            def values(s):
                h, i = steps[s]
                if s >= 2:
                    pe.wait_ge(o_got, s - 1)
                lo = E * (h % 2)
                for n, a, b in groups[s]:
                    pe.wait_ge(t_got, n + 1)
                    for j in range(a, b):
                        last = pe.matmul(g.bank[lo:lo + E, 6 + s % 2, :P], v[:, j, h * E:(h + 1) * E],
                                         prob_t[:, s % 2, j, :], start=j == 0, stop=j == i)
                last.then_inc(o_full, 1)

            scores(0)
            scores(1)
            for s in range(N):
                if s + 2 < N:
                    scores(s + 2)
                transposes(s)
                if s >= 1:
                    values(s - 1)
            values(N - 1)

        @block.vector
        def _(dve):
            def largest(s):
                h, i = steps[s]
                w = (i + 1) * P
                dve.wait_ge(s_full, s + 1)
                if s >= 2:
                    dve.wait_ge(e_done, s - 1)
                dve.tensor_tensor_reduce(out=masked[:, s % 2, :w],
                                         in0=g.bank[:, 2 * (s % 2):2 * (s % 2) + 2, :].rearrange("p a b -> p (a b)")[:, :w],
                                         in1=mask[:, NT - 2 - i:, :].rearrange("p a b -> p (a b)"),
                                         scale=1.0, scalar=FLOOR, op0=ALU.add, op1=ALU.max,
                                         accum_out=top[:, s % 2, 0:1]).then_inc(s_got, 1)
                dve.wait_ge(s_got, s + 1)
                dve.tensor_scalar(top[:, s % 2, 1:2], top[:, s % 2, 0:1], -1.0, None, ALU.mult).then_inc(negated, 1)

            def divide(s):
                h, i = steps[s]
                w = (i + 1) * P
                dve.wait_ge(e_done, s + 1)
                dve.reciprocal(top[:, s % 2, 3:4], top[:, s % 2, 2:3]).then_inc(inv_done, 1)
                dve.wait_ge(inv_done, s + 1)
                dve.tensor_scalar(prob[:, s % 2, :w], prob[:, s % 2, :w], top[:, s % 2, 3:4], None, ALU.mult).then_inc(p_ready, 1)

            def take(s):
                h, i = steps[s]
                lo = E * (h % 2)
                tile = h // 2 + (0 if window else H // 2)
                place = (slice(lo, lo + E), tile, slice(i * P, (i + 1) * P))
                dve.wait_ge(o_full, s + 1)
                dve.tensor_copy(g.o_hi[place], g.bank[lo:lo + E, 6 + s % 2, :P]).then_inc(o_hi_s, 1)
                dve.wait_ge(o_hi_s, s + 1)
                dve.tensor_tensor(g.o_lo[place], g.bank[lo:lo + E, 6 + s % 2, :P], g.o_hi[place].bitcast(F32),
                                  ALU.subtract).then_inc(o_got, 1)

            dve.wait_ge(mask_in, 16)
            largest(0)
            for s in range(N):
                if s + 1 < N:
                    largest(s + 1)
                divide(s)
                if s >= 2:
                    take(s - 2)
            take(N - 2)
            take(N - 1)

        @block.scalar
        def _(act):
            def exponent(s):
                h, i = steps[s]
                w = (i + 1) * P
                act.wait_ge(negated, s + 1)
                if s >= 2:
                    act.wait_ge(t_full, groups[s - 2][-1][0] + 1)
                act.activation(prob[:, s % 2, :w], masked[:, s % 2, :w], ACT.Exp, bias=top[:, s % 2, 1:2],
                               accum_out=top[:, s % 2, 2:3]).then_inc(e_done, 1)

            exponent(0)
            for s in range(N):
                if s + 1 < N:
                    exponent(s + 1)
                if s >= 2:
                    act.wait_ge(o_full, s - 1)
                for n, a, b in groups[s]:
                    act.wait_ge(t_full, n + 1)
                    act.activation(prob_t[:, s % 2, a:b, :].rearrange("p a b -> p (a b)"),
                                   g.bank[:, 4 + n % 2, :(b - a) * P], ACT.Copy).then_inc(t_got, 1)


def load_window(g, room, q_t, k_t, v):
    nc = g.nc
    nat = room("win_nat", [P, 2, NT - 1, H * E // 2])
    wq_in, wv_in, wt_full, wt_got = map(g.sem, ("wq_in", "wv_in", "wt_full", "wt_got"))
    jobs = [(x, half) for x in range(2) for half in range(2)]
    with nc.Block() as block:

        @block.sync
        def _(sp):
            for m, (x, half) in enumerate(jobs):
                if m >= 2:
                    sp.wait_ge(wt_full, 4 * (m - 1))
                src = (g.q_d, g.k_d)[x][:SEQ, half * 256:(half + 1) * 256]
                sp.dma_start(nat[:, m % 2], src.rearrange("(t p) c -> p t c", p=P)).then_inc(wq_in, 16)
                sp.wait_ge(wq_in, 16 * (m + 1))
            sp.dma_start(v[:, :, :], g.v_d[:SEQ, :].rearrange("(t p) c -> p t c", p=P)).then_inc(wv_in, 16)
            sp.wait_ge(wv_in, 16)

        @block.tensor
        def _(pe):
            n = 0
            for m, (x, half) in enumerate(jobs):
                pe.wait_ge(wq_in, 16 * (m + 1))
                for tile in range(2):
                    for quad in range(2):
                        if n >= 4:
                            pe.wait_ge(wt_got, n - 3)
                        for t in range(4):
                            last = pe.transpose(g.bank[:, n % 4, t * P:(t + 1) * P],
                                                nat[:, m % 2, 4 * quad + t, tile * P:(tile + 1) * P], g.ident[:, :])
                        last.then_inc(wt_full, 1)
                        n += 1

        def take(eng, n, copy):
            m, tile, quad = n // 4, n // 2 % 2, n % 2
            x, half = jobs[m]
            eng.wait_ge(wt_full, n + 1)
            copy((q_t, k_t)[x][:, 2 * half + tile, quad * 512:(quad + 1) * 512], g.bank[:, n % 4, :]).then_inc(wt_got, 1)

        @block.vector
        def _(dve):
            for n in range(16):
                take(dve, n, dve.tensor_copy)


def attend_sample(g, kind):
    nc = g.nc
    window = kind == "window"
    tag = "ws" if window else "ls"
    tiles = SK if window else NPAGE
    width = tiles * P + TDEC
    vcols = H * E if window else KL
    room = Room(nc, R2, TOP if window else g.room_kept)
    sem = lambda name: g.sem(f"{tag}_{name}")
    if window:
        keys = room("ws_keys", [P, 2, SK, H * E])
        vals = room("ws_vals", [P, 2, SK, H * E])
        key_t = room("ws_key_t", [P, 2, H // 2, width])
        q_new = room("ws_q_new", [NS, H * E])
        k_new = room("ws_k_new", [NS, H * E])
        k_new_t = room("ws_k_new_t", [P, H // 2, NS])
        q_rows = room("ws_q_rows", [P, H // 2, NSEQ, H, TDEC])
        v_new = room("ws_v_new", [TDEC, NSEQ, H * E])
    else:
        keys = vals = room("ls_keys", [P, 2, NPAGE, KL + RD])
        key_t = room("ls_key_t", [P, 1, 2, width])
        pe_t = room("ls_pe_t", [RD, 1, width])
        v_new = room("ls_v_new", [TDEC, NSEQ, KL])
        o_t = room("ls_o_t", [P, 2, H, NSEQ, TDEC])
        pages = nc.alloc_sbuf_tensor_at("ls_pages", [1, NSEQ * NPAGE], I32, offset=room.next)
        room.next += NSEQ * NPAGE * BYTES
    buffers = 2 if window else 1
    mask = room(f"{tag}_mask", [NS, width])
    masked = room(f"{tag}_masked", [NS, width])
    prob = room(f"{tag}_prob", [NS, width])
    prob_t = room(f"{tag}_prob_t", [P, tiles + 1, NS])
    top = room(f"{tag}_top", [NS, 4])
    o_nat = room(f"{tag}_o_nat", [NS, vcols])
    (c_in, new_full, new_got, q_set, k_full, k_got, s_full, s_got, negated, e_done, inv_done, p_ready,
     pt_full, pt_got, o_full, o_taken, ot_full, ot_got, o_hi_s, o_lo_s) = map(sem, (
         "c_in", "new_full", "new_got", "q_set", "k_full", "k_got", "s_full", "s_got", "negated", "e_done",
         "inv_done", "p_ready", "pt_full", "pt_got", "o_full", "o_taken", "ot_full", "ot_got", "o_hi", "o_lo"))
    kv_in = [sem(f"kv_in{j}") for j in range(2)]
    kv_count = 160 if window else 32 * NPAGE
    n_const = (4 if window else 3) * 16
    scores_flat = g.bank[:NS, 0:3, :].rearrange("p a b -> p (a b)")[:, :width]
    with nc.Block() as block:

        @block.sync
        def _(sp):
            sp.dma_start(mask[:, :], g.mask_ws_c if window else g.mask_ls_c).then_inc(c_in, 16)
            if window:
                sp.dma_start(q_new[:, :], g.q_d[SEQ:, :]).then_inc(c_in, 16)
                sp.dma_start(k_new[:, :], g.k_d[SEQ:, :]).then_inc(c_in, 16)
                sp.dma_start(v_new[:, :, :], g.v_d[SEQ:, :].rearrange("(s t) c -> t s c", t=TDEC)).then_inc(c_in, 16)
            else:
                sp.dma_start(v_new[:, :, :], g.ckv_sample[0].rearrange("s t c -> t s c")).then_inc(c_in, 16)
                sp.dma_start(pages[:, :], g.page_table.rearrange("(a s) n -> a (s n)", a=1)).then_inc(c_in, 16)
                sp.wait_ge(c_in, n_const)
            for s in range(NSEQ):
                if s >= 2:
                    sp.wait_ge(o_full, s - 1)
                if window:
                    for cache, dst in ((g.cache_win_k, keys), (g.cache_win_v, vals)):
                        far = cache[0, s, 0:PAST // 2].rearrange("(m r) h e -> m r (h e)", r=16)
                        for r in range(4):
                            sp.dma_start(dst[32 * r:32 * r + 32, s % 2, 0, :], far[:, r, :]).then_inc(kv_in[s % 2], 16)
                        sp.dma_start(dst[:, s % 2, 1:, :], cache[0, s, PAST // 2:].rearrange("(a p) h e -> p a (h e)", p=P)).then_inc(kv_in[s % 2], 16)
                else:
                    for n in range(NPAGE):
                        page = sp.value_load(pages[0:1, s * NPAGE + n:s * NPAGE + n + 1], min_val=0, max_val=NPHYS - 1)
                        sp.dma_start(keys[:, s % 2, n, :KL], g.cache_ckv[0, bass.ds(page, 1)].rearrange("a p c -> p (a c)")).then_inc(kv_in[s % 2], 16)
                        sp.dma_start(keys[:, s % 2, n, KL:], g.cache_kpe[0, bass.ds(page, 1)].rearrange("a p c -> p (a c)")).then_inc(kv_in[s % 2], 16)

        @block.tensor
        def _(pe):
            def turn_keys(s):
                pe.wait_ge(kv_in[s % 2], kv_count * (s // 2 + 1))
                for n in range(tiles):
                    m = s * tiles + n
                    if m >= 2:
                        pe.wait_ge(k_got, m - 1)
                    b = 3 + m % 2
                    for k in range(4 if window else 2):
                        last = pe.transpose(g.bank[:, b, k * P:(k + 1) * P], keys[:, s % 2, n, k * P:(k + 1) * P], g.ident[:, :])
                    if not window:
                        last = pe.transpose(g.bank[:RD, b, 2 * P:3 * P], keys[:, s % 2, n, KL:], g.ident[:, :])
                    last.then_inc(k_full, 1)

            if window:
                pe.wait_ge(c_in, n_const)
                for x in (q_new, k_new):
                    for k in range(4):
                        at = (0 if x is q_new else P) + k * NS
                        last = pe.transpose(g.bank[:, 7, at:at + NS], x[:, k * P:(k + 1) * P], g.ident[:NS, :NS])
                last.then_inc(new_full, 1)
            turn_keys(0)
            for s in range(NSEQ):
                pe.wait_ge(q_set, 1)
                pe.wait_ge(k_got, (s + 1) * tiles)
                pe.wait_ge(new_got, s + 1)
                if s >= 1:
                    pe.wait_ge(s_got, s)
                for at in range(0, width, 512):
                    w = min(512, width - at)
                    out = g.bank[:NS, at // 512, :w]
                    if window:
                        for k in range(4):
                            last = pe.matmul(out, q_rows[:, k, s].rearrange("p h t -> p (h t)"), key_t[:, s % 2, k, at:at + w],
                                             start=k == 0, stop=k == 3)
                    else:
                        for k in range(2):
                            pe.matmul(out, g.ql_t[:, k, s].rearrange("p h t -> p (h t)"), key_t[:, 0, k, at:at + w],
                                      start=k == 0, stop=False)
                        last = pe.matmul(out, g.qpe_t[:, s].rearrange("p h t -> p (h t)"), pe_t[:, 0, at:at + w],
                                         start=False, stop=True)
                last.then_inc(s_full, 1)
                if s + 1 < NSEQ:
                    turn_keys(s + 1)
                pe.wait_ge(p_ready, s + 1)
                for n in range(tiles):
                    pe.transpose(g.bank[:, 5, n * NS:(n + 1) * NS], prob[:, n * P:(n + 1) * P], g.ident[:NS, :NS])
                pe.transpose(g.bank[:TDEC, 5, tiles * NS:(tiles + 1) * NS], prob[:, tiles * P:], g.ident[:NS, :NS]).then_inc(pt_full, 1)
                pe.wait_ge(pt_got, s + 1)
                if s >= 1:
                    pe.wait_ge(o_taken, s)
                for n in range(tiles):
                    pe.matmul(g.bank[:NS, 6, :vcols], prob_t[:, n, :], vals[:, s % 2, n, :vcols], start=n == 0, stop=False)
                pe.matmul(g.bank[:NS, 6, :vcols], prob_t[:TDEC, tiles, :], v_new[:, s, :], start=False, stop=True).then_inc(o_full, 1)
                pe.wait_ge(o_taken, s + 1)
                if s >= 1:
                    pe.wait_ge(ot_got, s)
                for k in range(vcols // P):
                    last = pe.transpose(g.bank[:, 7, k * NS:(k + 1) * NS], o_nat[:, k * P:(k + 1) * P], g.ident[:NS, :NS])
                last.then_inc(ot_full, 1)
            if not window:
                pe.wait_ge(ot_got, NSEQ)
                for h in range(H):
                    lo = E * (h % 2)
                    for c in range(2):
                        last = pe.matmul(g.bank[lo:lo + E, 5 + h % 2, (h // 2) * NS:(h // 2 + 1) * NS], g.w_uv_sb[:, c, h * E:(h + 1) * E],
                                         o_t[:, c, h].rearrange("p s t -> p (s t)"), start=c == 0, stop=c == 1)
                last.then_inc(ot_full, 1)

        @block.scalar
        def _(act):
            def take_keys(s):
                for n in range(tiles):
                    m = s * tiles + n
                    b = 3 + m % 2
                    act.wait_ge(k_full, m + 1)
                    if s >= buffers:
                        act.wait_ge(s_full, s - buffers + 1)
                    if window:
                        act.activation(key_t[:, s % 2, :, n * P:(n + 1) * P],
                                       g.bank[:, b, :].rearrange("p (k c) -> p k c", k=4), ACT.Copy).then_inc(k_got, 1)
                    else:
                        act.activation(key_t[:, 0, :, n * P:(n + 1) * P],
                                       g.bank[:, b, :2 * P].rearrange("p (k c) -> p k c", k=2), ACT.Copy)
                        act.activation(pe_t[:, 0, n * P:(n + 1) * P], g.bank[:RD, b, 2 * P:3 * P], ACT.Copy).then_inc(k_got, 1)

            take_keys(0)
            for s in range(NSEQ):
                act.wait_ge(negated, s + 1)
                if s >= 1:
                    act.wait_ge(pt_full, s)
                act.activation(prob[:, :], masked[:, :], ACT.Exp, bias=top[:, 1:2], accum_out=top[:, 2:3]).then_inc(e_done, 1)
                if s + 1 < NSEQ:
                    take_keys(s + 1)

        @block.vector
        def _(dve):
            def add_new(s):
                if s >= buffers:
                    dve.wait_ge(s_full, s - buffers + 1)
                if window:
                    dve.tensor_copy(key_t[:, s % 2, :, SK * P:], k_new_t[:, :, s * TDEC:(s + 1) * TDEC]).then_inc(new_got, 1)
                else:
                    dve.tensor_copy(key_t[:, 0, :, PAST:], g.ckv_t[:, :, SEQ + s * TDEC:SEQ + (s + 1) * TDEC])
                    dve.tensor_copy(pe_t[:, 0, PAST:], g.kpe_t[:, s * TDEC:(s + 1) * TDEC]).then_inc(new_got, 1)

            if window:
                dve.memset(q_rows[:, :, :, :, :].rearrange("p k s h t -> p (k s h t)"), 0.0).then_inc(q_set, 1)
                dve.wait_ge(new_full, 1)
                dve.wait_ge(q_set, 1)
                for h in range(H):
                    lo, k = E * (h % 2), h // 2
                    dve.tensor_copy(q_rows[lo:lo + E, k, :, h, :],
                                    g.bank[lo:lo + E, 7, k * NS:(k + 1) * NS].rearrange("p (s t) -> p s t", s=NSEQ))
                dve.tensor_copy(k_new_t[:, :, :], g.bank[:, 7, P:2 * P].rearrange("p (k c) -> p k c", k=4)).then_inc(q_set, 1)
                dve.wait_ge(q_set, 2)
            else:
                dve.memset(masked[:, :], 0.0).then_inc(q_set, 1)
            add_new(0)
            dve.wait_ge(c_in, n_const)
            for s in range(NSEQ):
                dve.wait_ge(s_full, s + 1)
                if s >= 1:
                    dve.wait_ge(e_done, s)
                dve.tensor_tensor_reduce(out=masked[:, :], in0=scores_flat, in1=mask[:, :], scale=1.0, scalar=FLOOR,
                                         op0=ALU.add, op1=ALU.max, accum_out=top[:, 0:1]).then_inc(s_got, 1)
                dve.wait_ge(s_got, s + 1)
                dve.tensor_scalar(top[:, 1:2], top[:, 0:1], -1.0, None, ALU.mult).then_inc(negated, 1)
                if s + 1 < NSEQ:
                    add_new(s + 1)
                dve.wait_ge(e_done, s + 1)
                dve.reciprocal(top[:, 3:4], top[:, 2:3]).then_inc(inv_done, 1)
                dve.wait_ge(inv_done, s + 1)
                dve.tensor_scalar(prob[:, :], prob[:, :], top[:, 3:4], None, ALU.mult).then_inc(p_ready, 1)
                dve.wait_ge(pt_full, s + 1)
                if s >= 1:
                    dve.wait_ge(o_full, s)
                dve.tensor_copy(prob_t[:, :tiles, :].rearrange("p a b -> p (a b)"), g.bank[:, 5, :tiles * NS])
                dve.tensor_copy(prob_t[:TDEC, tiles, :], g.bank[:TDEC, 5, tiles * NS:(tiles + 1) * NS]).then_inc(pt_got, 1)
                dve.wait_ge(o_full, s + 1)
                if s >= 1:
                    dve.wait_ge(ot_full, s)
                dve.tensor_copy(o_nat[:, :], g.bank[:NS, 6, :vcols]).then_inc(o_taken, 1)
                dve.wait_ge(ot_full, s + 1)
                if window:
                    at = SEQ + s * TDEC
                    for odd in range(2):
                        lo = E * odd
                        src = g.bank[lo:lo + E, 7, 0:160].rearrange("p (a c) -> p a c", c=NS + 2 * TDEC)[:, :, odd * TDEC:(odd + 1) * TDEC]
                        place = (slice(lo, lo + E), slice(0, H // 2), slice(at, at + TDEC))
                        dve.tensor_copy(g.o_hi[place], src).then_inc(o_hi_s, 1)
                        dve.wait_ge(o_hi_s, 2 * s + odd + 1)
                        last = dve.tensor_tensor(g.o_lo[place], src, g.o_hi[place].bitcast(F32), ALU.subtract)
                    last.then_inc(ot_got, 1)
                else:
                    dve.tensor_copy(o_t[:, :, :, s, :], g.bank[:, 7, :2 * NS].rearrange("p (c h t) -> p c h t", c=2, h=H)).then_inc(ot_got, 1)
            if not window:
                dve.wait_ge(ot_full, NSEQ + 1)
                for odd in range(2):
                    lo = E * odd
                    src = g.bank[lo:lo + E, 5 + odd, :P].rearrange("p (a c) -> p a c", a=4)
                    place = (slice(lo, lo + E), slice(H // 2, H), slice(SEQ, T))
                    dve.tensor_copy(g.o_hi[place], src).then_inc(o_hi_s, 1)
                    dve.wait_ge(o_hi_s, odd + 1)
                    dve.tensor_tensor(g.o_lo[place], src, g.o_hi[place].bitcast(F32), ALU.subtract)


class Step:

    def __init__(self, g, kind, w, act, out=None, gain=None, per_unit=3):
        self.kind, self.w, self.act, self.out, self.gain, self.per_unit = kind, w, act, out, gain, per_unit
        self.prev = g.steps[-1] if g.steps else None
        self.unit, self.chunk, self.turn, self.part, self.square = g.units, g.chunks, g.turns, g.parts, g.squares
        g.steps.append(self)
        g.units += KD
        g.chunks += per_unit * KD
        g.turns += KD // 2 * (2 if kind == "merge" else 1)
        g.parts += NCH * KD if out else 0
        g.squares += NCH * KD if gain is not None or kind == "ple" else 0


def run_tail(g):
    nc = g.nc
    unit_room(g, Room(nc, RW, RM), "fin")
    room = Room(nc, RM)
    g.hg, g.tmp = room("f_hg", [P, 2, CH]), room("f_tmp", [P, 2, CH])
    g.gate_in_sb = room("f_gates", [P, 2, 2, CH])
    room = Room(nc, R1, R2)
    h = (room("h2_hi", [P, KD, T], F32R), room("h2_lo", [P, KD, T], F32R))
    room = Room(nc, R2, RX)
    z = (room("z_hi", [P, KD, T], F32R), room("z_lo", [P, KD, T], F32R))
    room = Room(nc, R2, RX)
    a = (room("a_hi", [P, KD, T], F32R), room("a_lo", [P, KD, T], F32R))
    room = Room(nc, R2, RX)
    g.diag = room("f_diag", [P, NT, P])
    g.stat = room("f_stat", [P, NT])
    g.p_t = room("p_t_sb", [P, 2, T])
    g.p_hi, g.p_lo = room("p_hi", [P, 2, T], F32R), room("p_lo", [P, 2, T], F32R)
    g.wp = room("w_ple_sb", [P, 2, D])
    g.wp_hi, g.wp_lo = room("w_ple_hi", [P, 2, D], F32R), room("w_ple_lo", [P, 2, D], F32R)
    g.total = room("final_total", [P, T])
    g.sig = room("ple_sig", [P, 2, CH])
    g.root = room("y_root", [P, NT])
    g.x = Room(nc, RX, RW)("x_res", [P, KD, T])
    g.y = Room(nc, R1, R2)("y_nat", [P, 3, D])
    (g.hg_s, g.hi_s, g.lo_s, g.sq_s, g.acc_s, g.clear_s, g.x_in, g.sum_s, g.stat_s, g.mean_s, g.root_s,
     g.diag_s, g.bc_s, g.bc_got, g.p_in, g.p_hi_s, g.p_lo_s, g.sig_s, g.px_s, g.pdone_s, g.y_full, g.y_got) = map(g.sem, (
         "t_hg", "t_hi", "t_lo", "t_sq", "t_acc", "t_clear", "t_x_in", "t_sum", "t_stat", "t_mean", "t_root",
         "t_diag", "t_bc", "t_bc_got", "t_p_in", "t_p_hi", "t_p_lo", "t_sig", "t_px", "t_pdone", "t_y_full", "t_y_got"))
    g.gates_in = [g.sem(f"t_gates_in{j}") for j in range(2)]
    y_out = [g.sem(f"y_out{j}") for j in range(3)]
    g.parts = g.squares = 0
    g.steps = []
    Step(g, "merge", None, (g.o_hi, g.o_lo), z, per_unit=6)
    Step(g, "residual", g.w_o[0], z, h, gain=1)
    for f in range(NF):
        Step(g, "up", g.w_up[0, :, f * D:(f + 1) * D], h, a)
        out, gain = (h, 2) if f == NF - 1 else (None, None)
        Step(g, "residual", g.w_down[0, f * D:(f + 1) * D, :], a, out, gain)
    Step(g, "ple", g.w_ple_gate[0], h, per_unit=6)
    factors = [g.steps[2], g.steps[-1]]
    steps = g.steps

    with nc.Block() as block:

        @block.sync
        def _(sp):
            sp.dma_start(g.x[:, :, :], g.xt_d).then_inc(g.x_in, 16)
            for st in steps:
                def pair(i, st=st):
                    for j in range(2):
                        sp.wait_ge(g.w_split, i * 2 + st.unit + j - 1)
                        if st.kind == "merge":
                            for half, w in enumerate((g.w_oa, g.w_ob)):
                                sp.dma_start(g.w_stage[:, j, 4 * half:4 * half + 4, :], columns(w[0], i * 2 + j)).then_inc(g.w_loaded[j], 16)
                        else:
                            sp.dma_start(g.w_stage[:, j], columns(st.w, i * 2 + j)).then_inc(g.w_loaded[j], 16)
                in_pairs(sp, KD, pair, peel=False)
                if st is steps[-2]:
                    sp.wait_ge(g.full, steps[-1].chunk)
                    sp.dma_start(g.p_t[:, :, :], g.p_t_d).then_inc(g.p_in, 16)
                    sp.dma_start(g.wp[:, :, :], g.w_ple[0].rearrange("(k p) c -> p k c", p=P)).then_inc(g.p_in, 16)
            for t in range(NT):
                sp.wait_ge(g.y_got, t + 1)
                dst = g.y_prompt[0, t * P:(t + 1) * P, :] if t < NT - 1 else g.y_sample.rearrange("s t d -> (s t) d")
                sp.dma_start(dst, g.y[:ROWS[t], t % 3, :]).then_inc(y_out[t % 3], 16)
            for j in range(3):
                sp.wait_ge(y_out[j], 16 * len(range(j, NT, 3)))

        @block.gpsimd
        def _(pool):
            for st in steps:
                def pair(i, st=st):
                    for j in range(2):
                        per = 2 if st.kind == "merge" else 1
                        pool.wait_ge(g.w_loaded[j], (i * per + st.turn + per) * 16)
                        before = st.prev.per_unit if first(i) and st.prev else st.per_unit
                        pool.wait_ge(g.full, i * (2 * st.per_unit) + st.chunk - (before if j == 0 else 0))
                        split_weights(pool, g, j, i * 2 + st.unit + j + 1)
                        if j == 1:
                            low_parts(pool, g, st, i, 0)
                        elif not first(i):
                            low_parts(pool, g, st, i - 1, 1)
                        else:
                            if st.prev:
                                low_parts(pool, g, st.prev, KD // 2 - 1, 1)
                            if st in factors:
                                pool.wait_ge(g.stat_s, 2 * factors.index(st) + 2)
                                inverse_root(pool, g, g.stat[:, :], g.stat[:, :], 1.0 / D, g.mean_s, factors.index(st) + 1, g.root_s)
                in_pairs(pool, KD, pair)
            pool.wait_ge(g.stat_s, 6)
            inverse_root(pool, g, g.root[:, :], g.stat[:, :], 1.0 / D, g.mean_s, 3, g.root_s)

        @block.tensor
        def _(pe):
            for st in steps:
                if st.kind == "ple":
                    for m in range(KD):
                        embed_unit(pe, g, st, m, factors)
                    continue

                def pair(i, st=st):
                    for j in range(2):
                        pe.wait_ge(g.w_split, i * 2 + st.unit + j + 1)
                        for n in range(st.per_unit):
                            c, half = (n // 2, n % 2) if st.kind == "merge" else (n, 0)
                            if first(i) and j == 0 and st.prev and half == 0:
                                pe.wait_ge(g.lo_s, st.part - 2 + c)
                            pe.wait_ge(g.free, i * (2 * st.per_unit) + st.chunk + st.per_unit * j + n - 5)
                            ks = [(4 * half + k, 4 * half + k) for k in range(4)] if st.kind == "merge" else [(k, k) for k in range(KD)]
                            multiply_chunk(pe, g, (st.per_unit * j + n) % 6, j, c, ks, *st.act)
                            if first(i) and st in factors:
                                factor_products(pe, g, factors.index(st), [(0, 0), (0, 2), (1, 0)], (j, n))
                in_pairs(pe, KD, pair)
            write_products(pe, g)

        @block.vector
        def _(dve):
            dve.memset(g.rstd_bc[:, :], 0.0).then_inc(g.clear_s, 1)
            for st in steps:
                if st.kind == "ple":
                    dve.memset(g.total[:, :], 0.0).then_inc(g.clear_s, 1)
                    dve.wait_ge(g.p_hi_s, 2)
                    dve.tensor_tensor(g.p_lo[:, :, :], g.p_t[:, :, :], g.p_hi[:, :, :].bitcast(F32), ALU.subtract).then_inc(g.p_lo_s, 1)
                    dve.tensor_tensor(g.wp_lo[:, :, :], g.wp[:, :, :], g.wp_hi[:, :, :].bitcast(F32), ALU.subtract).then_inc(g.p_lo_s, 1)
                    dve.wait_ge(g.clear_s, 3)
                if st in factors:
                    spread_factors(dve, g, factors.index(st))
                if st.kind == "residual" and st.prev.kind == "merge":
                    dve.wait_ge(g.x_in, 16)
                    dve.wait_ge(g.clear_s, 1)
                if st is steps[-2]:
                    dve.memset(g.rstd_bc[:, :], 0.0).then_inc(g.clear_s, 1)
                    dve.wait_ge(g.clear_s, 2)
                take = {"merge": take_merge, "residual": take_residual, "up": take_up, "ple": take_embedding}[st.kind]
                in_pairs(dve, KD, lambda i, st=st, take=take: take(dve, g, st, i), peel=st.prev is None)
            dve.memset(g.stat[:, :], float(D)).then_inc(g.stat_s, 1)
            copy_sums(dve, g, 3)

        @block.scalar
        def _(act):
            for q in range(2):
                load_gates(act, g, 0, q)
            for st in steps:
                if st.kind == "ple":
                    act.wait_ge(g.p_in, 32)
                    act.activation(g.p_hi[:, :, :], g.p_t[:, :, :], ACT.Copy).then_inc(g.p_hi_s, 1)
                    act.activation(g.wp_hi[:, :, :], g.wp[:, :, :], ACT.Copy).then_inc(g.p_hi_s, 1)

                def pair(i, st=st, last=False):
                    for q in range(6):
                        if st.kind == "ple":
                            act.wait_ge(g.free, i * 12 + st.chunk + 2 * q + 1)
                            act.activation(g.sig[:, q % 2, :], g.tmp[:, q % 2, :], ACT.Sigmoid).then_inc(g.sig_s, 1)
                            act.wait_ge(g.px_s, i * 6 + q + 1)
                        if st.gain is not None:
                            act.wait_ge(g.free, i * 6 + st.chunk + q + 1)
                        if st.gain is not None or st.kind == "ple":
                            if not (st is steps[1] and first(i) and q == 0):
                                act.wait_ge(g.acc_s, i * 6 + st.square + q)
                            act.activation(g.sq[:, :].unsqueeze(1), chunk_of(g.x, i, q), ACT.Square).then_inc(g.sq_s, 1)
                        if st.out:
                            act.wait_ge(g.hg_s, i * 6 + st.part + q + 1)
                            act.activation(chunk_of(st.out[0], i, q), g.hg[:, q % 2:q % 2 + 1, :], ACT.Copy).then_inc(g.hi_s, 1)
                        if st.kind == "merge" and not (last and q >= 4):
                            load_gates(act, g, i + (q + 2) // 6, (q + 2) % 6, i * 6 + q + 1)
                if st.kind == "merge":
                    pair(0)
                    with act.Fori(1, KD // 2 - 1) as i:
                        pair(i)
                    pair(KD // 2 - 1, last=True)
                elif st.out or st.kind == "ple":
                    in_pairs(act, KD, pair, peel=st is steps[1])
            act.wait_ge(g.root_s, 3)
            for t in range(NT):
                r = ROWS[t]
                act.wait_ge(g.y_full, t + 1)
                if t >= 3:
                    act.wait_ge(y_out[t % 3], 16 * (t // 3))
                act.activation(g.y[:r, t % 3, :], g.bank[:r, 2 * (t % 3):2 * (t % 3) + 2, :].rearrange("p a b -> p (a b)"),
                               ACT.Copy, scale=g.root[:r, t:t + 1]).then_inc(g.y_got, 1)


def chunk_of(x, i, q):
    c = q % 3
    return x[:, bass.ds(i * 2 + q // 3, 1), c * CH:(c + 1) * CH]


def split_weights(pool, g, j, n):
    one = g.ones[:, 0:1].unsqueeze(2).to_broadcast([P, KD, P])
    pool.tensor_tensor(g.wu_hi[:, j], g.w_stage[:, j], one, ALU.mult).then_inc(g.w_hi, 1)
    pool.wait_ge(g.w_hi, n)
    pool.tensor_tensor(g.wu_lo[:, j], g.w_stage[:, j], g.wu_hi[:, j].bitcast(F32), ALU.subtract).then_inc(g.w_split, 1)


def low_parts(pool, g, st, i, j):
    if not st.out:
        return
    for c in range(NCH):
        q = 3 * j + c
        pool.wait_ge(g.hi_s, i * 6 + st.part + q + 1)
        pool.tensor_tensor(chunk_of(st.out[1], i, q), g.hg[:, q % 2:q % 2 + 1, :], chunk_of(st.out[0], i, q).bitcast(F32),
                           ALU.subtract).then_inc(g.lo_s, 1)


def load_gates(act, g, i, q, free=None):
    if free is not None:
        act.wait_ge(g.hg_s, free)
    c = q % 3
    src = g.gate_d.rearrange("a k p t -> k p a t")[bass.ds(i * 2 + q // 3, 1), :, :, c * CH:(c + 1) * CH]
    act.dma_start(g.gate_in_sb[:, q % 2], src.rearrange("k p a t -> p (k a) t")).then_inc(g.gates_in[q % 2], 16)


def take_merge(dve, g, st, i):
    for q in range(6):
        dve.wait_ge(g.gates_in[q % 2], (i * 3 + q // 2 + 1) * 16)
        for half in range(2):
            n = 2 * q + half
            dve.wait_ge(g.full, i * 12 + st.chunk + n + 1)
            if half == 0 and not (first(i) and q == 0):
                dve.wait_ge(g.hg_s, i * 6 + q)
            dve.tensor_tensor(g.tmp[:, half, :], g.bank[:, n % 6, :CH], g.gate_in_sb[:, q % 2, half, :], ALU.mult).then_inc(g.free, 1)
        dve.wait_ge(g.free, i * 12 + st.chunk + 2 * q + 2)
        if not (first(i) and q < 2):
            dve.wait_ge(g.lo_s, i * 6 + st.part + q - 1)
        dve.tensor_tensor(g.hg[:, q % 2, :], g.tmp[:, 0, :], g.tmp[:, 1, :], ALU.add).then_inc(g.hg_s, 1)


def take_residual(dve, g, st, i):
    for q in range(6):
        x = chunk_of(g.x, i, q)
        dve.wait_ge(g.full, i * 6 + st.chunk + q + 1)
        dve.tensor_tensor(x, g.bank[:, q:q + 1, :CH], x, ALU.add).then_inc(g.free, 1)
        if st.gain is not None:
            dve.wait_ge(g.free, i * 6 + st.chunk + q + 1)
            dve.wait_ge(g.lo_s, i * 6 + st.part + q - 1)
            dve.tensor_scalar(g.hg[:, q % 2:q % 2 + 1, :], x, g.gains[:, st.gain, bass.ds(i * 2 + q // 3, 1)], None,
                              ALU.mult).then_inc(g.hg_s, 1)
            add_square(dve, g, g.rstd_bc, q % 3, i * 6 + st.square + q + 1)


def take_up(dve, g, st, i):
    for q in range(6):
        c = q % 3
        dve.wait_ge(g.full, i * 6 + st.chunk + q + 1)
        dve.tensor_tensor(g.tmp[:, q % 2, :], g.bank[:, q, :CH], g.rstd_bc[:, c * CH:(c + 1) * CH], ALU.mult).then_inc(g.free, 1)
        dve.wait_ge(g.free, i * 6 + st.chunk + q + 1)
        dve.wait_ge(g.lo_s, i * 6 + st.part + q - 1)
        dve.scalar_tensor_tensor(g.hg[:, q % 2, :], g.tmp[:, q % 2, :], 0.0, g.tmp[:, q % 2, :], ALU.max, ALU.mult).then_inc(g.hg_s, 1)


def take_embedding(dve, g, st, i):
    for q in range(6):
        c = q % 3
        x = chunk_of(g.x, i, q)
        dve.wait_ge(g.full, i * 12 + st.chunk + 2 * q + 1)
        dve.tensor_tensor(g.tmp[:, q % 2, :], g.bank[:, 2 * c, :CH], g.rstd_bc[:, c * CH:(c + 1) * CH], ALU.mult).then_inc(g.free, 1)
        dve.wait_ge(g.full, i * 12 + st.chunk + 2 * q + 2)
        dve.wait_ge(g.sig_s, i * 6 + q + 1)
        dve.tensor_tensor(g.hg[:, q % 2, :], g.bank[:, 2 * c + 1, :CH], g.sig[:, q % 2, :], ALU.mult).then_inc(g.free, 1)
        dve.wait_ge(g.free, i * 12 + st.chunk + 2 * q + 2)
        dve.tensor_tensor(x, x, g.hg[:, q % 2:q % 2 + 1, :], ALU.add).then_inc(g.px_s, 1)
        add_square(dve, g, g.total, c, i * 6 + st.square + q + 1)
        dve.tensor_scalar(x, x, g.gains[:, 3, bass.ds(i * 2 + q // 3, 1)], None, ALU.mult).then_inc(g.pdone_s, 1)


def add_square(dve, g, total, c, at):
    dve.wait_ge(g.sq_s, at)
    cols = slice(c * CH, (c + 1) * CH)
    dve.tensor_tensor(total[:, cols], total[:, cols], g.sq[:, :], ALU.add).then_inc(g.acc_s, 1)


def embed_unit(pe, g, st, m, factors):
    pe.wait_ge(g.w_split, st.unit + m + 1)
    for c in range(NCH):
        n = 6 * m + 2 * c
        if m == 0:
            pe.wait_ge(g.lo_s, st.part - 2 + c)
        pe.wait_ge(g.free, st.chunk + n - 5)
        multiply_chunk(pe, g, 2 * c, m % 2, c, [(k, k) for k in range(KD)], *st.act)
        if m == 0:
            factor_products(pe, g, factors.index(st), [(0, 0), (0, 2), (0, 4)], (0, 2 * c))
        if n == 0:
            pe.wait_ge(g.p_lo_s, 2)
        pe.wait_ge(g.free, st.chunk + n - 4)
        out = g.bank[:, 2 * c + 1, :CH]
        for k in range(2):
            w, v = g.wp_hi[:, k, m * P:(m + 1) * P], g.wp_lo[:, k, m * P:(m + 1) * P]
            a, b = g.p_hi[:, k, c * CH:(c + 1) * CH], g.p_lo[:, k, c * CH:(c + 1) * CH]
            pe.matmul(out, w, a, start=k == 0, stop=False)
            pe.matmul(out, w, b, start=False, stop=False)
            last = pe.matmul(out, v, a, start=False, stop=k == 1)
        last.then_inc(g.full, 1)


def factor_products(pe, g, n, places, at):
    if at == places[0]:
        pe.wait_ge(g.acc_s, NCH * KD * (n + 1))
        sum_features(pe, g, g.rstd_bc)
    elif at == places[1]:
        pe.wait_ge(g.diag_s, n + 1)
        for b in range(2):
            for t in range(4):
                last = pe.matmul(g.bank[:, 6 + b, t * P:(t + 1) * P], g.ones[:, :], g.diag[:, 4 * b + t, :], start=True, stop=True)
            last.then_inc(g.bc_s, 1)
    elif at == places[2]:
        pe.wait_ge(g.bc_got, 3 * n + 1)
        pe.matmul(g.bank[:, 6, :NS], g.ones[:NS, :], g.diag[:NS, NT - 1, :NS], start=True, stop=True).then_inc(g.bc_s, 1)


def sum_features(pe, g, total):
    for t in range(NT):
        last = pe.matmul(g.bank[:ROWS[t], 7, t:t + 1], total[:, t * P:t * P + ROWS[t]], g.ones[:, 0:1], start=True, stop=True)
    last.then_inc(g.sum_s, 1)


def copy_sums(dve, g, n):
    dve.wait_ge(g.stat_s, 2 * n - 1)
    dve.wait_ge(g.sum_s, n)
    dve.tensor_copy(g.stat[:, :NT - 1], g.bank[:, 7, :NT - 1])
    dve.tensor_copy(g.stat[:NS, NT - 1:], g.bank[:NS, 7, NT - 1:NT]).then_inc(g.stat_s, 1)


def spread_factors(dve, g, n):
    dve.memset(g.stat[:, :], float(D)).then_inc(g.stat_s, 1)
    copy_sums(dve, g, n + 1)
    dve.wait_ge(g.root_s, n + 1)
    shape = [P, NT, P]
    dve.tensor_tensor(g.diag[:, :, :], g.ident[:, :].unsqueeze(1).to_broadcast(shape),
                      g.stat[:, :].unsqueeze(2).to_broadcast(shape), ALU.mult).then_inc(g.diag_s, 1)
    for b, (bank, a, z) in enumerate(((6, 0, 512), (7, 512, 1024), (6, 1024, T))):
        dve.wait_ge(g.bc_s, 3 * n + b + 1)
        dve.tensor_copy(g.rstd_bc[:, a:z], g.bank[:, bank, :z - a]).then_inc(g.bc_got, 1)
    dve.wait_ge(g.bc_got, 3 * n + 3)


def write_products(pe, g):
    pe.wait_ge(g.acc_s, g.squares)
    sum_features(pe, g, g.total)
    pe.wait_ge(g.pdone_s, NCH * KD)
    pe.wait_ge(g.free, g.chunks)
    for t in range(NT):
        r = ROWS[t]
        if t >= 3:
            pe.wait_ge(g.y_got, t - 2)
        for k in range(KD):
            last = pe.transpose(g.bank[:r, 2 * (t % 3) + k // 4, (k % 4) * P:(k % 4 + 1) * P], g.x[:, k, t * P:t * P + r], g.ident[:, :])
        last.then_inc(g.y_full, 1)


_INS = ["x_prompt", "x_sample", "cache_win_k", "cache_win_v", "cache_ckv", "cache_kpe", "page_table", "p_prompt",
        "p_sample", "g_mix", "w_in", "g_q", "w_uq", "g_kv", "w_uk", "w_uv", "w_oa", "w_ob", "w_o", "g_ffn", "w_up",
        "w_down", "g_ple", "w_ple_gate", "w_ple", "g_final"]
_OUTS = {
    "y_prompt": (1, SEQ, D), "y_sample": (NSEQ, TDEC, D),
    "win_k_prompt": (1, 1, SEQ, H, E), "win_v_prompt": (1, 1, SEQ, H, E),
    "ckv_prompt": (1, 1, SEQ, KL), "kpe_prompt": (1, 1, SEQ, RD),
    "win_k_sample": (1, NSEQ, PAST + TDEC, H, E), "win_v_sample": (1, NSEQ, PAST + TDEC, H, E),
    "ckv_sample": (1, NSEQ, TDEC, KL), "kpe_sample": (1, NSEQ, TDEC, RD),
}


def _log_count(dist):
    count = sum(((dist >= 0) & (dist <= w) & (dist % d == 0)).astype(np.float32) for w, d in PATTERNS)
    return np.where(count > 0, np.log(np.maximum(count, 1)), NEG).astype(np.float32)


def _constants():
    pos = np.concatenate([np.arange(SEQ), np.tile(PAST + np.arange(TDEC), NSEQ), np.zeros(P - NS)]).astype(np.float32)
    out = {"ident_c": np.eye(P, dtype=np.float32)}
    for tag, rot in (("a", E // 4), ("b", RD)):
        half = rot // 2
        inv = np.float32(500000.0) ** (-np.arange(half, dtype=np.float32) * np.float32(2.0 / rot))
        ang = (pos[:, None] * inv[None, :].astype(np.float32)).astype(np.float32)
        for fn, name in ((np.cos, "cos"), (np.sin, "sin")):
            out[f"{name}_{tag}_c"] = np.ascontiguousarray(fn(ang).astype(np.float32).reshape(NT, P, half).transpose(1, 0, 2))
    q, k = np.arange(P)[:, None, None], np.arange(P)[None, None, :]
    dist = (NT - 2 - np.arange(NT - 1))[None, :, None] * P + q - k
    out["mask_w_c"] = _log_count(dist)
    out["mask_b_c"] = np.where(dist >= 0, 0.0, NEG).astype(np.float32)
    far = np.array([16 * m + r for r in range(4) for m in range(32)])
    keys = np.concatenate([far, np.arange(PAST // 2, PAST + TDEC)])
    t = np.tile(np.arange(TDEC), H)[:, None]
    out["mask_ws_c"] = _log_count(PAST + t - keys[None, :])
    out["mask_ls_c"] = np.where(np.arange(PAST + TDEC)[None, :] <= PAST + t, 0.0, NEG).astype(np.float32)
    return out


def kernel(**inputs):
    import concourse.bacc as _bacc
    from concourse.bass_utils import run_bass_kernel_spmd as _run

    nc = _bacc.Bacc("TRN2", target_bir_lowering=False, num_devices=1)
    arrays, io = {}, {}
    for name, a in [(n, np.asarray(inputs[n])) for n in _INS] + list(_constants().items()):
        a = np.ascontiguousarray(a)
        arrays[f"in_{name}"] = a
        io[name] = nc.dram_tensor(f"in_{name}", a.shape, mybir.dt.from_np(a.dtype), kind="ExternalInput").ap()
    for name, shape in _OUTS.items():
        io[name] = nc.dram_tensor(f"out_{name}", shape, F32, kind="ExternalOutput").ap()
    build(nc, io)
    r = _run(nc, [arrays], core_ids=[0])
    return tuple(r.results[0][f"out_{name}"] for name in _OUTS)
```

```python
from contextlib import ExitStack

import numpy as np

import concourse.bass as bass
from concourse import mybir

F32 = mybir.dt.float32
F32R = mybir.dt.float32r
I32 = mybir.dt.int32
ALU = mybir.AluOpType
ACT = mybir.ActivationFunctionType
AX_X = mybir.AxisListType.X

P = 128
D = 1024
SEQ = 1024
NSEQ, TDEC = 8, 4
NS = NSEQ * TDEC
T = SEQ + NS
NT = SEQ // P + 1
ROWS = [P] * (NT - 1) + [NS]
CH = 352
NCH = T // CH
KD = D // P
H = 8
E = 64
PATTERNS = ((128, 1), (512, 4), (2048, 16))
QL, KL, RD = 384, 256, 32
BH = E + RD
FF = 4 * D
NF = FF // D
PLE = 256
PAST, PAGE = 1024, 128
NPAGE = PAST // PAGE
NPHYS = (5 * NSEQ * NPAGE + 3) // 4
EPS = 1e-6
NEG = -1e30
BLK_COLS = [(1536, QL), (1920, KL + RD), (0, 512), (512, 512), (1024, 512)]
GATE_COL = 2208
SK = 5
SKEYS = SK * P + TDEC
FLOOR = -3e38



BYTES = 4
BASE = 16512
MAIN = BASE + 7168
R1 = MAIN
R2 = R1 + 2 * KD * T * BYTES
RX = R2 + 2 * KD * T * BYTES
RW = RX + KD * T * BYTES
RM = RW + 6 * KD * P * BYTES
TOP = 229368
R_CQ = (TOP - NT * (QL + KL + RD) * BYTES) // 32 * 32 - 64


class Room:

    def __init__(self, nc, start, end=TOP):
        self.nc, self.next, self.end = nc, start, end

    def __call__(self, name, shape, dt=F32):
        size = -(-int(np.prod(shape[1:])) * BYTES // 32) * 32
        assert self.next + size <= self.end, (name, self.next + size, self.end)
        made = self.nc.alloc_sbuf_tensor_at(name, list(shape), dt, offset=self.next)
        self.next += size
        return made


class Program:

    def __init__(self, nc, io):
        self.nc = nc
        self.x_prompt = io["x_prompt"]
        self.x_sample = io["x_sample"]
        self.cache_win_k = io["cache_win_k"]
        self.cache_win_v = io["cache_win_v"]
        self.cache_ckv = io["cache_ckv"]
        self.cache_kpe = io["cache_kpe"]
        self.page_table = io["page_table"]
        self.p_prompt = io["p_prompt"]
        self.p_sample = io["p_sample"]
        self.g_mix = io["g_mix"]
        self.w_in = io["w_in"]
        self.g_q = io["g_q"]
        self.w_uq = io["w_uq"]
        self.g_kv = io["g_kv"]
        self.w_uk = io["w_uk"]
        self.w_uv = io["w_uv"]
        self.w_oa = io["w_oa"]
        self.w_ob = io["w_ob"]
        self.w_o = io["w_o"]
        self.g_ffn = io["g_ffn"]
        self.w_up = io["w_up"]
        self.w_down = io["w_down"]
        self.g_ple = io["g_ple"]
        self.w_ple_gate = io["w_ple_gate"]
        self.w_ple = io["w_ple"]
        self.g_final = io["g_final"]
        self.ident_c = io["ident_c"]
        self.cos_a_c = io["cos_a_c"]
        self.sin_a_c = io["sin_a_c"]
        self.cos_b_c = io["cos_b_c"]
        self.sin_b_c = io["sin_b_c"]
        self.mask_w_c = io["mask_w_c"]
        self.mask_b_c = io["mask_b_c"]
        self.mask_ws_c = io["mask_ws_c"]
        self.mask_ls_c = io["mask_ls_c"]
        self.y_prompt = io["y_prompt"]
        self.y_sample = io["y_sample"]
        self.win_k_prompt = io["win_k_prompt"]
        self.win_v_prompt = io["win_v_prompt"]
        self.ckv_prompt = io["ckv_prompt"]
        self.kpe_prompt = io["kpe_prompt"]
        self.win_k_sample = io["win_k_sample"]
        self.win_v_sample = io["win_v_sample"]
        self.ckv_sample = io["ckv_sample"]
        self.kpe_sample = io["kpe_sample"]


def build(nc, io):
    with ExitStack() as ctx:
        g = Program(nc, io)
        g.stage_sems = []

        def sem(name):
            g.stage_sems.append(nc.alloc_semaphore(name=name))
            return g.stage_sems[-1]

        g.sem = sem
        g.bank = ctx.enter_context(nc.psum_tensor("bank", [P, 8, 512], F32))
        dram = lambda name, shape: nc.dram_tensor(name, shape, F32, kind="Internal").ap()
        g.xt_d = dram("xt_d", (P, KD, T))
        g.p_t_d = dram("p_t_d", (P, 2, T))
        g.gate_d = dram("gate_d", (2, KD, P, T))
        g.q_d = dram("q_d", (T, H * E))
        g.k_d = dram("k_d", (T, H * E))
        g.v_d = dram("v_d", (T, H * E))
        room = Room(nc, BASE, MAIN)
        g.ident = room("ident", [P, P])
        g.ones = room("ones", [P, P])
        g.nhalf = room("nhalf", [P, 1])
        g.gains = room("gains", [P, 4, KD])
        g.rstd_bc = room("rstd_bc", [P, T])
        g.rstd = room("rstd", [P, NT])
        g.rstd8 = room("rstd8", [P, NT])
        g.sq = room("tail_square", [P, CH])
        g.root = room("lat_root", [P, 2, NT])
        g.w_loaded = [ctx.enter_context(nc.semaphore(f"w_loaded{j}")) for j in range(2)]
        g.w_hi, g.w_split, g.full, g.free = (
            ctx.enter_context(nc.semaphore(n)) for n in ("w_hi", "w_split", "full", "free"))
        g.copied = ctx.enter_context(nc.semaphore("copied"))
        g.units = g.chunks = g.turns = 0
        room = Room(nc, R1, R2)
        g.h_hi = room("h_hi", [P, KD, T], F32R)
        g.h_lo = room("h_lo", [P, KD, T], F32R)
        room = Room(nc, R_CQ)
        g.cq = room("cq", [P, NT, QL])
        g.ckv_at = room.next
        g.ckv = room("ckv", [P, NT, KL + RD])
        room = Room(nc, R2)
        g.qb_t = room("qb_t", [BH, H, T])
        g.kb_t = room("kb_t", [BH, H, SEQ])
        g.vb = room("vb", [P, NT - 1, H * E])
        g.room_kept = room.next
        g.w_uv_sb = room("w_uv_sb", [P, 2, H * E])
        g.ckv_t = room("ckv_t", [P, 2, T])
        g.kpe_t = room("kpe_t", [RD, NS])
        g.ql_t = room("ql_t", [P, 2, NSEQ, H, TDEC])
        g.qpe_t = room("qpe_t", [RD, NSEQ, H, TDEC])
        g.room_b = room.next
        room = Room(nc, g.room_b, R_CQ)
        g.w_uq_sb = room("w_uq_sb", [P, 3, H * BH])
        g.w_uk_sb = room("w_uk_sb", [P, 2, H * E])
        g.cos_b_sb = room("cos_b_sb", [P, NT, 16])
        g.sin_b_sb = room("sin_b_sb", [P, NT, 16])
        g.g_q_sb = room("g_q_sb", [P, 3])
        g.l_in = g.sem("l_in")
        project_natural(g)
        project_gates(g)
        room = Room(nc, R1, R2)
        g.o_hi = room("o_hi", [P, KD, T], F32R)
        g.o_lo = room("o_lo", [P, KD, T], F32R)
        project_latents(g)
        renew_semaphores(g)
        for kind in ("latent", "window"):
            ahead = Ahead(g, kind)
            attend_prompt(g, kind, ahead)
            attend_sample(g, kind, ahead)
        renew_semaphores(g)
        run_tail(g)
        nc.clear_and_free_semaphores(g.stage_sems)


def renew_semaphores(g):
    g.nc.clear_and_free_semaphores(g.stage_sems)
    g.stage_sems.clear()
    g.nc.all_engine_barrier()


def inverse_root(pool, g, out, total, scale, scaled, at, done):
    pool.tensor_scalar(out, total, scale, EPS, ALU.mult, ALU.add).then_inc(scaled, 1)
    pool.wait_ge(scaled, at)
    half = g.nhalf[:out.shape[0], :].to_broadcast(list(out.shape))
    pool.tensor_tensor(out, out, half, ALU.pow).then_inc(done, 1)


def project_natural(g):
    nc = g.nc
    room = Room(nc, R2, R_CQ)
    g.gate_stage_at = room.next
    w_st = room("wn_st", [P, KD, 512])
    g.gate_split_at = room.next + KD * 512 * BYTES
    w_hi = room("wn_hi", [P, 2, KD, 512], F32R)
    w_lo = room("wn_lo", [P, 2, KD, 512], F32R)
    early = Room(nc, room.next)
    nat = early("nat", [P, 3, 512])
    room_after_nat = early.next
    x_nat = room("x_nat", [P, 3, D])
    x_nat_end = room.next
    x_t = room("x_t", [P, 2, KD, P])
    hg = room("hg", [P, 2, KD // 2, P])
    p_nat = room("p_nat", [P, 2, PLE])
    p_t = room("p_t", [P, 2, 2, P])
    diag = room("diag", [P, 2, P])
    gain_nat = room("gain_nat", [4 * KD, P])
    stat = room("stat", [P, NT])
    ra = room("rope_a", [P, 2, H, 8])
    rb = room("rope_b", [P, 2, H, 8])
    cos_a = room("cos_a", [P, NT, 8])
    sin_a = room("sin_a", [P, NT, 8])
    square = Room(nc, g.ckv_at)("square", [P, D])
    room = Room(nc, room_after_nat, x_nat_end)
    lat_square = room("lat_square", [P, QL])
    g_kv = room("g_kv_sb", [P, KL])
    cos_b = room("cos_b", [P, NT, 16])
    sin_b = room("sin_b", [P, NT, 16])
    la = room("lat_ra", [P, 2, 1, 16])
    lb = room("lat_rb", [P, 2, 1, 16])
    lat_stat = room("lat_stat", [P, 2, NT])
    squared, scaled, rooted, normed, turned, l_step, lat_out, lat_tabs, l_set = map(g.sem, (
        "l_squared", "l_scaled", "l_rooted", "l_normed", "l_turned", "l_step", "l_out", "l_tabs", "l_set"))
    (consts, x_squared, tr, t_copied, hg_ready, hi_done, lo_done, stat_ready, rstd_ready, diag_ready, bc_full,
     bc_got, gain_in, gain_t, set_up, got_gain, p_full, p_got, rstd8_set) = map(g.sem, (
         "consts", "x_squared", "tr", "t_copied", "hg_ready", "hi_done", "lo_done", "stat_ready", "rstd_ready",
         "diag_ready", "bc_full", "bc_got", "gain_in", "gain_t", "set_up", "got_gain", "p_full", "p_got", "rstd8_set"))
    x_in = [g.sem(f"x_in{j}") for j in range(3)]
    x_out = [g.sem(f"x_out{j}") for j in range(2)]
    p_in = [g.sem(f"p_in{j}") for j in range(2)]
    p_out = [g.sem(f"p_out{j}") for j in range(2)]
    wn_in, wn_hi, wn_lo, n_full, n_got, roped, tabs, ra_s = map(
        g.sem, ("wn_in", "wn_hi", "wn_lo", "n_full", "n_got", "roped", "tabs", "ra_s"))
    nat_out = [g.sem(f"nat_out{j}") for j in range(3)]
    g.w_stage = Room(nc, g.gate_stage_at)("w_stage_gates", [P, 2, KD, P])
    split_room(g, Room(nc, g.gate_split_at), "gates")
    gates = g.w_in[0].rearrange("(k p) c -> p k c", p=P)
    dest = {2: (g.q_d, None), 3: (g.k_d, g.win_k_prompt), 4: (g.v_d, g.win_v_prompt)}
    steps = [(b, t) for b in range(5) for t in range(NT)]
    stored = [s for s in steps if s[0] >= 2]

    def written(m, place):
        return 16 * sum(1 if stored[n][0] == 2 else 2 for n in range(place, m, 3))

    def low_block(eng, b):
        n = BLK_COLS[b][1]
        eng.tensor_tensor(w_lo[:, b % 2, :, :n], w_st[:, :, :n], w_hi[:, b % 2, :, :n].bitcast(F32),
                          ALU.subtract).then_inc(wn_lo, 1)

    with nc.Block() as block:

        @block.sync
        def _(sp):
            def load_x(t):
                if t >= 3:
                    sp.wait_ge(tr, 2 * (t - 2))
                    sp.wait_ge(x_squared, t - 2)
                src = g.x_prompt[0, t * P:(t + 1) * P, :] if t < NT - 1 else g.x_sample.rearrange("n t d -> (n t) d")
                sp.dma_start(x_nat[:ROWS[t], t % 3, :], src).then_inc(x_in[t % 3], 16)

            def load_p(t):
                if t >= 2:
                    sp.wait_ge(p_full, t - 1)
                src = g.p_prompt[0, 0, t * P:(t + 1) * P, :] if t < NT - 1 else g.p_sample[0].rearrange("s t c -> (s t) c")
                sp.dma_start(p_nat[:ROWS[t], t % 2, :], src).then_inc(p_in[t % 2], 16)

            def load_block(b):
                c0, n = BLK_COLS[b]
                if b >= 1:
                    sp.wait_ge(wn_lo, b)
                sp.dma_start(w_st[:, :, :n], g.w_in[0, :, c0:c0 + n].rearrange("(k p) n -> p k n", p=P)).then_inc(wn_in, 16)

            load_x(0)
            sp.dma_start(g.ident[:, :], g.ident_c).then_inc(consts, 16)
            for n, gain in enumerate((g.g_mix, g.g_ffn, g.g_ple, g.g_final)):
                row = gain if n == 3 else gain[0, :]
                sp.dma_start(gain_nat[n * KD:(n + 1) * KD, :], row.rearrange("(k p) -> k p", p=P)).then_inc(gain_in, 16)
            load_x(1)
            load_block(0)
            load_x(2)
            for tab, src in ((cos_a, g.cos_a_c), (sin_a, g.sin_a_c)):
                sp.dma_start(tab[:, :, :], src).then_inc(tabs, 16)
            for t in range(NT):
                sp.wait_ge(t_copied, 2 * t + 2)
                toks = slice(t * P, t * P + ROWS[t])
                sp.dma_start(g.xt_d[:, :, toks], x_t[:, t % 2, :, :ROWS[t]]).then_inc(x_out[t % 2], 16)
                if t + 3 < NT:
                    load_x(t + 3)
                if t == 3:
                    load_block(1)
            load_p(0)
            load_p(1)
            sp.wait_ge(tr, 2 * NT)
            sp.wait_ge(x_squared, NT)
            for tab, src in ((cos_b, g.cos_b_c), (sin_b, g.sin_b_c)):
                sp.dma_start(tab[:, :, :], src).then_inc(lat_tabs, 16)
            sp.dma_start(g_kv[:, :], g.g_kv[0:1, :].to_broadcast([P, KL])).then_inc(lat_tabs, 16)
            for t in range(NT):
                sp.wait_ge(p_got, t + 1)
                toks = slice(t * P, t * P + ROWS[t])
                sp.dma_start(g.p_t_d[:, :, toks], p_t[:, t % 2, :, :ROWS[t]]).then_inc(p_out[t % 2], 16)
                if t + 2 < NT:
                    load_p(t + 2)
                if t == 0:
                    load_block(2)
            load_block(3)
            load_block(4)
            sp.wait_ge(wn_lo, 5)
            for j in range(2):
                sp.dma_start(g.w_stage[:, j], gates[:, :, GATE_COL + j * P:GATE_COL + (j + 1) * P]).then_inc(g.w_loaded[j], 16)
            for t in range(NT):
                r = ROWS[t]
                sp.wait_ge(normed, t + 1)
                sp.wait_ge(turned, t + 1)
                for out, new, part in ((g.ckv_prompt, g.ckv_sample, slice(0, KL)), (g.kpe_prompt, g.kpe_sample, slice(KL, KL + RD))):
                    dst = out[0, 0, t * P:(t + 1) * P, :] if t < NT - 1 else new[0].rearrange("n t c -> (n t) c")
                    sp.dma_start(dst, g.ckv[:r, t, part]).then_inc(lat_out, 16)
            sp.wait_ge(lat_out, 32 * NT)
            for j in range(2):
                sp.wait_ge(x_out[j], 16 * len(range(j, NT, 2)))
                sp.wait_ge(p_out[j], 16 * len(range(j, NT, 2)))

        @block.gpsimd
        def _(pool):
            for n in range(2 * NT):
                t, half = divmod(n, 2)
                pool.wait_ge(hi_done, n + 1)
                where = (slice(None), slice(4 * half, 4 * half + 4), slice(t * P, t * P + ROWS[t]))
                pool.tensor_tensor(g.h_lo[where], hg[:, n % 2, :, :ROWS[t]], g.h_hi[where].bitcast(F32),
                                   ALU.subtract).then_inc(lo_done, 1)
                if n % 6 == 5:
                    pool.wait_ge(x_squared, t + 1)
                    inverse_root(pool, g, g.rstd[:, t - 2:t + 1], stat[:, t - 2:t + 1], 1.0 / D, stat_ready, t // 3 + 1, rstd_ready)
            for b in range(1, 5):
                pool.wait_ge(wn_hi, b + 1)
                low_block(pool, b)
                if b == 3:
                    pool.wait_ge(squared, 2 * NT)
                    inverse_root(pool, g, g.root[:, 0, :], lat_stat[:, 0, :], 1.0 / QL, scaled, 1, rooted)
                    inverse_root(pool, g, g.root[:, 1, :], lat_stat[:, 1, :], 1.0 / KL, scaled, 2, rooted)
            pool.wait_ge(n_full, 4 * NT)
            for j in range(2):
                pool.wait_ge(g.w_loaded[j], 16)
                split_weights(pool, g, j, j + 1)

        @block.tensor
        def _(pe):
            def turn_x(t):
                pe.wait_ge(x_in[t % 3], 16 * (t // 3 + 1))
                for half in range(2):
                    n = 2 * t + half
                    if n >= 2:
                        pe.wait_ge(t_copied, n - 1)
                    for k in range(4):
                        at = (4 * half + k) * P
                        last = pe.transpose(g.bank[:, 4 + n % 2, k * P:k * P + ROWS[t]],
                                            x_nat[:ROWS[t], t % 3, at:at + P], g.ident[:ROWS[t], :ROWS[t]])
                    last.then_inc(tr, 1)

            def product(s):
                b, t = steps[s]
                n = BLK_COLS[b][1]
                if t == 0:
                    pe.wait_ge(wn_lo, b + 1)
                if b == 0:
                    pe.wait_ge(lo_done, 2 * t + 2)
                if s >= 4:
                    pe.wait_ge(n_got, s - 3)
                toks = slice(t * P, t * P + ROWS[t])
                out = g.bank[:ROWS[t], s % 4, :n]
                for k in range(KD):
                    a, c = g.h_hi[:, k, toks], g.h_lo[:, k, toks]
                    w, v = w_hi[:, b % 2, k, :n], w_lo[:, b % 2, k, :n]
                    pe.matmul(out, a, w, start=k == 0, stop=False)
                    pe.matmul(out, a, v, start=False, stop=False)
                    last = pe.matmul(out, c, w, start=False, stop=k == KD - 1)
                last.then_inc(n_full, 1)

            pe.wait_ge(consts, 16)
            pe.wait_ge(gain_in, 64)
            pe.transpose(g.bank[:, 7, 0:4 * KD], gain_nat[:, :], g.ident[:4 * KD, :4 * KD]).then_inc(gain_t, 1)
            turn_x(0)
            turn_x(1)
            for t in range(NT):
                if t + 2 < NT:
                    turn_x(t + 2)
                product(t)
            for t in range(NT):
                r = ROWS[t]
                product(NT + t)
                pe.wait_ge(diag_ready, t + 1)
                if t == 0:
                    pe.wait_ge(got_gain, 1)
                if t >= 6:
                    pe.wait_ge(bc_got, 1)
                pe.matmul(g.bank[:, 6 + t // 3 % 2, (t % 3) * P:(t % 3) * P + r], g.ones[:r, :],
                          diag[:r, t % 2, :r], start=True, stop=True).then_inc(bc_full, 1)
                pe.wait_ge(p_in[t % 2], 16 * (t // 2 + 1))
                if t >= 2:
                    pe.wait_ge(p_got, t - 1)
                for k in range(2):
                    last = pe.transpose(g.bank[:, 4 + t % 2, k * P:k * P + r], p_nat[:r, t % 2, k * P:(k + 1) * P], g.ident[:r, :r])
                last.then_inc(p_full, 1)
            for s in range(2 * NT, 5 * NT):
                product(s)

        @block.scalar
        def _(act):
            def high_block(b):
                n = BLK_COLS[b][1]
                act.wait_ge(wn_in, 16 * (b + 1))
                if b >= 2:
                    act.wait_ge(n_full, NT * (b - 1))
                act.activation(w_hi[:, b % 2, :, :n], w_st[:, :, :n], ACT.Copy).then_inc(wn_hi, 1)

            def take(s):
                b, t = steps[s]
                r, n = ROWS[t], BLK_COLS[b][1]
                act.wait_ge(n_full, s + 1)
                if b == 0 and t % 3 == 0:
                    act.wait_ge(rstd_ready, t // 3 + 1)
                if s == NT:
                    act.wait_ge(x_squared, NT)
                if s == 2 * NT:
                    act.wait_ge(rstd8_set, 1)
                m = s - 2 * NT
                if b < 2:
                    out = (g.cq, g.ckv)[b][:r, t, :]
                else:
                    if m >= 3:
                        act.wait_ge(nat_out[m % 3], written(m, m % 3))
                    out = nat[:r, m % 3, :]
                factor = g.rstd8 if b == 2 else g.rstd
                act.activation(out, g.bank[:r, s % 4, :n], ACT.Copy, scale=factor[:r, t:t + 1]).then_inc(n_got, 1)
                if b >= 2:
                    if b < 4:
                        act.wait_ge(roped, m + 1)
                    else:
                        act.wait_ge(n_got, s + 1)
                    scratch, result = dest[b]
                    act.dma_start(scratch[t * P:t * P + r, :], out).then_inc(nat_out[m % 3], 16)
                    if result is not None:
                        if t < NT - 1:
                            o = result[0, 0, t * P:t * P + r, :, :].rearrange("s h e -> s (h e)")
                        else:
                            new = g.win_k_sample if b == 3 else g.win_v_sample
                            o = new[0, :, PAST:PAST + TDEC, :, :].rearrange("n s h e -> n s (h e)")
                        act.dma_start(o, out).then_inc(nat_out[m % 3], 16)

            act.wait_ge(set_up, 1)
            for t in range(NT):
                act.wait_ge(x_in[t % 3], 16 * (t // 3 + 1))
                if t >= 1:
                    act.wait_ge(x_squared, t)
                act.activation(square[:ROWS[t], :], x_nat[:ROWS[t], t % 3, :], ACT.Square,
                               accum_out=stat[:ROWS[t], t:t + 1]).then_inc(x_squared, 1)
                for half in range(2):
                    n = 2 * t + half
                    act.wait_ge(hg_ready, n + 1)
                    act.activation(g.h_hi[:, 4 * half:4 * half + 4, t * P:t * P + ROWS[t]], hg[:, n % 2, :, :ROWS[t]],
                                   ACT.Copy).then_inc(hi_done, 1)
                if t == 0:
                    high_block(0)
                if t >= 4:
                    take(t - 4)
            for s in range(NT - 4, 5 * NT):
                if s == NT - 3:
                    high_block(1)
                if s >= NT and s % NT == 4 and s // NT < 4:
                    high_block(s // NT + 1)
                take(s)
                if s == 2 * NT:
                    act.wait_ge(n_got, 2 * NT)
                    act.wait_ge(l_set, 1)
                if 2 * NT <= s < 3 * NT:
                    t = s - 2 * NT
                    for which, (x, w) in enumerate(((g.cq, QL), (g.ckv, KL))):
                        if t or which:
                            act.wait_ge(squared, 2 * t + which)
                        act.activation(lat_square[:ROWS[t], :w], x[:ROWS[t], t, :w], ACT.Square,
                                       accum_out=lat_stat[:ROWS[t], which, t:t + 1]).then_inc(squared, 1)
            for j in range(3):
                act.wait_ge(nat_out[j], written(len(stored), j))

        @block.vector
        def _(dve):
            dve.memset(g.ones[:, :], 1.0)
            dve.memset(g.nhalf[:, :], -0.5)
            dve.memset(stat[:, :], float(D)).then_inc(set_up, 1)
            dve.wait_ge(gain_t, 1)
            dve.tensor_copy(g.gains[:, :, :].rearrange("p a b -> p (a b)"), g.bank[:, 7, 0:4 * KD]).then_inc(got_gain, 1)
            dve.wait_ge(got_gain, 1)
            for t in range(NT):
                for half in range(2):
                    n = 2 * t + half
                    r = ROWS[t]
                    dve.wait_ge(tr, n + 1)
                    got = g.bank[:, 4 + n % 2, :].rearrange("p (k c) -> p k c", k=4)[:, :, :r]
                    ks = slice(4 * half, 4 * half + 4)
                    if n >= 2:
                        dve.wait_ge(lo_done, n - 1)
                    gain = g.gains[:, 0, ks].unsqueeze(2).to_broadcast([P, 4, r])
                    dve.tensor_tensor(hg[:, n % 2, :, :r], got, gain, ALU.mult).then_inc(hg_ready, 1)
                    if t >= 2:
                        dve.wait_ge(x_out[t % 2], 16 * (t // 2))
                    dve.tensor_copy(x_t[:, t % 2, ks, :r], got).then_inc(t_copied, 1)
                if t == 0:
                    dve.wait_ge(wn_hi, 1)
                    low_block(dve, 0)
            dve.wait_ge(rstd_ready, 3)
            dve.tensor_scalar(g.rstd8[:, :], g.rstd[:, :], E ** -0.5, None, ALU.mult).then_inc(rstd8_set, 1)
            for t in range(NT):
                r = ROWS[t]
                if t >= 2:
                    dve.wait_ge(bc_full, t - 1)
                dve.tensor_scalar(diag[:, t % 2, :], g.ident[:, :], g.rstd[:, t:t + 1], None, ALU.mult).then_inc(diag_ready, 1)
                if t % 3 == 2:
                    dve.wait_ge(bc_full, t + 1)
                    at, w = (t - 2) * P, 2 * P + r
                    dve.tensor_copy(g.rstd_bc[:, at:at + w], g.bank[:, 6 + t // 3 % 2, :w]).then_inc(bc_got, 1)
                dve.wait_ge(p_full, t + 1)
                if t >= 2:
                    dve.wait_ge(p_out[t % 2], 16 * (t // 2))
                dve.tensor_copy(p_t[:, t % 2, :, :r],
                                g.bank[:, 4 + t % 2, :2 * P].rearrange("p (k c) -> p k c", k=2)[:, :, :r]).then_inc(p_got, 1)
            dve.wait_ge(tabs, 32)
            dve.wait_ge(lat_tabs, 48)
            dve.memset(lat_stat[:, :, :], float(QL)).then_inc(l_set, 1)
            for m, (b, t) in enumerate(stored):
                if b == 4:
                    break
                r = ROWS[t]
                dve.wait_ge(n_got, 2 * NT + m + 1)
                rotate(dve, nat[:r, m % 3, :].rearrange("p (h e) -> p h e", e=E), 8,
                       cos_a[:r, t, :], sin_a[:r, t, :], ra[:r], rb[:r], H, ra_s, 2 * m, roped, m)
                if b == 2:
                    rotate(dve, g.ckv[:r, t, KL:].rearrange("p (h e) -> p h e", h=1), 16, cos_b[:r, t, :],
                           sin_b[:r, t, :], la[:r], lb[:r], 1, l_step, 2 * t, turned, t)
                else:
                    dve.wait_ge(rooted, 2)
                    dve.scalar_tensor_tensor(g.ckv[:r, t, :KL], g.ckv[:r, t, :KL], g.root[:r, 1, t:t + 1],
                                             g_kv[:r, :], ALU.mult, ALU.mult).then_inc(normed, 1)


def copy_cache(eng, g, cache, out, s, n):
    eng.dma_start(out[0, bass.ds(s, n), 0:PAST, :, :].rearrange("n s h e -> n s (h e)"),
                  cache[0, bass.ds(s, n)].rearrange("n s h e -> n s (h e)")).then_inc(g.copied, 16)


def rotate(dve, x, half, cos, sin, ra, rb, heads, step, at, done, turn):
    shape = [x.shape[0], heads, half]
    c, s = cos.unsqueeze(1).to_broadcast(shape), sin.unsqueeze(1).to_broadcast(shape)
    x1, x2 = x[:, :, 0:half], x[:, :, half:2 * half]
    if turn:
        dve.wait_ge(done, turn)
    dve.tensor_tensor(ra[:, 0], x1, c, ALU.mult)
    dve.tensor_tensor(ra[:, 1], x2, c, ALU.mult)
    dve.tensor_tensor(rb[:, 0], x2, s, ALU.mult)
    dve.tensor_tensor(rb[:, 1], x1, s, ALU.mult).then_inc(step, 1)
    dve.wait_ge(step, at + 1)
    dve.tensor_tensor(x1, ra[:, 0], rb[:, 0], ALU.subtract).then_inc(step, 1)
    dve.wait_ge(step, at + 2)
    dve.tensor_tensor(x2, ra[:, 1], rb[:, 1], ALU.add).then_inc(done, 1)


def multiply_chunk(pe, g, bank, j, c, ks, act_hi, act_lo):
    out = g.bank[:, bank, :CH]
    cols = slice(c * CH, (c + 1) * CH)
    for n, (kw, ka) in enumerate(ks):
        w, v = g.wu_hi[:, j, kw], g.wu_lo[:, j, kw]
        a, b = act_hi[:, ka, cols], act_lo[:, ka, cols]
        pe.matmul(out, w, a, start=n == 0, stop=False)
        pe.matmul(out, w, b, start=False, stop=False)
        last = pe.matmul(out, v, a, start=False, stop=n == len(ks) - 1)
    last.then_inc(g.full, 1)


def unit_room(g, room, tag):
    g.w_stage = room(f"w_stage_{tag}", [P, 2, KD, P])
    split_room(g, room, tag)


def split_room(g, room, tag):
    g.wu_hi = room(f"wu_hi_{tag}", [P, 2, KD, P], F32R)
    g.wu_lo = room(f"wu_lo_{tag}", [P, 2, KD, P], F32R)


def columns(w, m):
    return w.rearrange("(k p) c -> p k c", p=P)[:, :, bass.ds(m * P, P)]


def in_pairs(eng, n, body, peel=True):
    if peel:
        body(0)
    with eng.Fori(1 if peel else 0, n // 2) as i:
        body(i)


def first(i):
    return isinstance(i, int) and i == 0


def project_gates(g):
    nc = g.nc
    room = Room(nc, g.gate_split_at + KD * 512 * BYTES, g.room_kept)
    scaled = room("gt_scaled", [P, 2, CH])
    gate = room("gate_out", [P, 2, T])
    n = 2 * KD
    U, C = g.units, g.chunks
    scaled_ready, gate_ready = g.sem("gt_scaled_s"), g.sem("gt_ready")
    gate_out = [g.sem(f"gt_out{j}") for j in range(2)]
    gates = g.w_in[0].rearrange("(k p) c -> p k c", p=P)
    dst = g.gate_d.rearrange("a k p t -> (a k) p t")
    with nc.Block() as block:

        @block.sync
        def _(sp):
            def pair(i):
                for j in range(2):
                    sp.wait_ge(g.w_split, i * 2 + U + j - 1)
                    sp.dma_start(g.w_stage[:, j], gates[:, :, bass.ds(i * 256 + GATE_COL + j * P, P)]).then_inc(g.w_loaded[j], 16)
                copy_cache(sp, g, g.cache_win_k, g.win_k_sample, i, 1)

            copy_cache(sp, g, g.cache_win_k, g.win_k_sample, 0, 1)
            load_latent_weights(g, sp)
            with sp.Fori(1, n // 2) as i:
                pair(i)

        @block.gpsimd
        def _(pool):
            def pair(i):
                for j in range(2):
                    pool.wait_ge(g.w_loaded[j], i * 16 + 16)
                    pool.wait_ge(g.full, i * 6 + C + 3 * j - 3)
                    split_weights(pool, g, j, i * 2 + U + j + 1)

            with pool.Fori(1, n // 2) as i:
                pair(i)

        @block.tensor
        def _(pe):
            def pair(i):
                for j in range(2):
                    pe.wait_ge(g.w_split, i * 2 + U + j + 1)
                    for c in range(NCH):
                        if not first(i):
                            pe.wait_ge(g.free, i * 6 + C + 3 * j + c - 5)
                        multiply_chunk(pe, g, 3 * j + c, j, c, [(k, k) for k in range(KD)], g.h_hi, g.h_lo)
            in_pairs(pe, n, pair)

        @block.vector
        def _(dve):
            def pair(i):
                for q in range(6):
                    c = q % 3
                    dve.wait_ge(g.full, i * 6 + C + q + 1)
                    if not (first(i) and q < 2):
                        dve.wait_ge(gate_ready, i * 6 + q - 1)
                    dve.tensor_tensor(scaled[:, q % 2, :], g.bank[:, q, :CH], g.rstd_bc[:, c * CH:(c + 1) * CH],
                                      ALU.mult).then_inc(g.free, 1)
            in_pairs(dve, n, pair)

        @block.scalar
        def _(act):
            def pair(i):
                for q in range(6):
                    j, c = divmod(q, 3)
                    act.wait_ge(g.free, i * 6 + C + q + 1)
                    if not first(i) and c == 0:
                        act.wait_ge(gate_out[j], i * 16)
                    act.activation(gate[:, j, c * CH:(c + 1) * CH], scaled[:, q % 2, :], ACT.Sigmoid).then_inc(gate_ready, 1)
                    if c == NCH - 1:
                        act.wait_ge(gate_ready, i * 6 + q + 1)
                        act.dma_start(dst[bass.ds(i * 2 + j, 1)].rearrange("a p t -> p (a t)"), gate[:, j, :]).then_inc(gate_out[j], 16)
            in_pairs(act, n, pair)
            for j in range(2):
                act.wait_ge(gate_out[j], 16 * (n // 2))
    g.units += n
    g.turns += n // 2
    g.chunks += 3 * n


def load_latent_weights(g, sp):
    sp.dma_start(g.w_uq_sb[:, :, :], g.w_uq[0].rearrange("(k p) n -> p k n", p=P)).then_inc(g.l_in, 16)
    sp.dma_start(g.w_uk_sb[:, :, :], g.w_uk[0].rearrange("(k p) h e -> p k (h e)", p=P)).then_inc(g.l_in, 16)
    sp.dma_start(g.w_uv_sb[:, :, :], g.w_uv[0].rearrange("(k p) h e -> p k (h e)", p=P)).then_inc(g.l_in, 16)
    sp.dma_start(g.cos_b_sb[:, :, :], g.cos_b_c).then_inc(g.l_in, 16)
    sp.dma_start(g.sin_b_sb[:, :, :], g.sin_b_c).then_inc(g.l_in, 16)
    sp.dma_start(g.g_q_sb[:, :], g.g_q[0].rearrange("(k p) -> p k", p=P), allow_slow_non_contiguous=True).then_inc(g.l_in, 16)


def project_latents(g):
    nc = g.nc
    room = Room(nc, R1, R2)
    w_uq, w_uk, cos_b, sin_b, g_q, l_in = g.w_uq_sb, g.w_uk_sb, g.cos_b_sb, g.sin_b_sb, g.g_q_sb, g.l_in
    cq_t = room("cq_t", [P, 3, T])
    q_nat = room("q_nat", [P, 2, H * BH])
    ra = room("lat_ra2", [P, 2, H, 16])
    rb = room("lat_rb2", [P, 2, H, 16])
    root_q = room("lat_root_q", [P, NT])
    w_ukt = room("w_ukt", [E, H, 2, P])
    (rq_done, l_step, cq_full, cq_got,
     ck_full, ck_got, uk_full, uk_got, qf, qg, qr, qt, qtg, kf, kg, vf, vg, lf) = map(g.sem, (
         "l_rq", "q_step",
         "cq_full", "cq_got", "ck_full", "ck_got", "uk_full", "uk_got", "qb_full", "qb_got", "qb_turned",
         "qb_tr", "qb_tgot", "kn_full", "kn_got", "vb_full", "vb_got", "ql_full"))

    with nc.Block() as block:

        @block.vector
        def _(dve):
            dve.tensor_scalar(root_q[:, :], g.root[:, 0, :], BH ** -0.5, None, ALU.mult).then_inc(rq_done, 1)
            dve.wait_ge(l_in, 6 * 16)
            for t in range(NT):
                r = ROWS[t]
                toks = slice(t * P, t * P + r)
                dve.wait_ge(cq_full, t + 1)
                dve.tensor_tensor(cq_t[:, :, toks], g.bank[:, t % 2, :3 * P].rearrange("p (k c) -> p k c", k=3)[:, :, :r],
                                  g_q[:, :].unsqueeze(2).to_broadcast([P, 3, r]), ALU.mult).then_inc(cq_got, 1)
            for t in range(NT):
                r = ROWS[t]
                toks = slice(t * P, t * P + r)
                dve.wait_ge(ck_full, t + 1)
                b = g.bank[:, 2 + t % 2, :].rearrange("p (k c) -> p k c", k=4)
                if t < NT - 1:
                    dve.tensor_copy(g.kb_t[E:BH, :, toks], b[E:BH, 2:3, :].to_broadcast([RD, H, P]))
                else:
                    dve.tensor_copy(g.kpe_t[:, :], b[:RD, 2, :r])
                dve.tensor_copy(g.ckv_t[:, :, toks], b[:, 0:2, :r]).then_inc(ck_got, 1)
            for n in range(4):
                dve.wait_ge(uk_full, n + 1)
                dve.tensor_copy(w_ukt[:, 2 * n:2 * n + 2, :, :].rearrange("e h c p -> e (h c p)"), g.bank[:E, 4 + n, :]).then_inc(uk_got, 1)

        @block.tensor
        def _(pe):
            for t in range(NT):
                r = ROWS[t]
                if t >= 2:
                    pe.wait_ge(cq_got, t - 1)
                for k in range(3):
                    last = pe.transpose(g.bank[:, t % 2, k * P:k * P + r], g.cq[:r, t, k * P:(k + 1) * P], g.ident[:r, :r])
                last.then_inc(cq_full, 1)
            pe.wait_ge(l_in, 6 * 16)
            for n in range(4):
                for m in range(4):
                    h, c = 2 * n + m // 2, m % 2
                    last = pe.transpose(g.bank[:E, 4 + n, m * P:(m + 1) * P], w_uk[:, c, h * E:(h + 1) * E], g.ident[:, :])
                last.then_inc(uk_full, 1)
            for t in range(NT):
                r = ROWS[t]
                if t >= 2:
                    pe.wait_ge(ck_got, t - 1)
                for k in range(2):
                    pe.transpose(g.bank[:, 2 + t % 2, k * P:k * P + r], g.ckv[:r, t, k * P:(k + 1) * P], g.ident[:r, :r])
                w, c0 = (BH, KL - E) if t < NT - 1 else (RD, KL)
                pe.transpose(g.bank[:w, 2 + t % 2, 2 * P:2 * P + r], g.ckv[:r, t, c0:], g.ident[:r, :r]).then_inc(ck_full, 1)

    with nc.Block() as block:

        @block.tensor
        def _(pe):
            def turn(t):
                r = ROWS[t]
                pe.wait_ge(qr, t + 1)
                for half in range(2):
                    n = 2 * t + half
                    if n >= 2:
                        pe.wait_ge(qtg, n - 1)
                    for m in range(4):
                        h = 4 * half + m
                        last = pe.transpose(g.bank[:BH, 4 + half, m * P:m * P + r], q_nat[:r, t % 2, h * BH:(h + 1) * BH], g.ident[:r, :r])
                    last.then_inc(qt, 1)

            for t in range(NT):
                r = ROWS[t]
                for half in range(2):
                    n = 2 * t + half
                    if n >= 4:
                        pe.wait_ge(qg, n - 3)
                    for k in range(3):
                        last = pe.matmul(g.bank[:r, n % 4, :QL], cq_t[:, k, t * P:t * P + r], w_uq[:, k, half * QL:(half + 1) * QL],
                                         start=k == 0, stop=k == 2)
                    last.then_inc(qf, 1)
                if t >= 1:
                    turn(t - 1)
            for n in range(2 * H):
                h, half = divmod(n, 2)
                if n >= 2:
                    pe.wait_ge(kg, n - 1)
                for c in range(2):
                    last = pe.matmul(g.bank[:E, 6 + n % 2, :], w_uk[:, c, h * E:(h + 1) * E], g.ckv_t[:, c, half * 512:(half + 1) * 512],
                                     start=c == 0, stop=c == 1)
                last.then_inc(kf, 1)
                if n == 0:
                    turn(NT - 1)
            pe.wait_ge(qg, 2 * NT)
            for j in range(NT - 1):
                if j >= 4:
                    pe.wait_ge(vg, j - 3)
                for c in range(2):
                    last = pe.matmul(g.bank[:, j % 4, :], g.ckv_t[:, c, j * P:(j + 1) * P], g.w_uv_sb[:, c, :], start=c == 0, stop=c == 1)
                last.then_inc(vf, 1)
            pe.wait_ge(qtg, 2 * NT)
            for h in range(H):
                last = pe.transpose(g.bank[:RD, 4, h * NS:(h + 1) * NS], q_nat[:NS, (NT - 1) % 2, h * BH + E:(h + 1) * BH], g.ident[:NS, :NS])
            last.then_inc(lf, 1)
            for c in range(2):
                for h in range(H):
                    at = (c * H + h) * NS
                    last = pe.matmul(g.bank[:, 5, at:at + NS], w_ukt[:, h, c, :], g.qb_t[:E, h, SEQ:], start=True, stop=True)
            last.then_inc(lf, 1)

        @block.scalar
        def _(act):
            def turned_out(t):
                r = ROWS[t]
                for half in range(2):
                    act.wait_ge(qt, 2 * t + half + 1)
                    act.activation(g.qb_t[:, 4 * half:4 * half + 4, t * P:t * P + r],
                                   g.bank[:BH, 4 + half, :].rearrange("p (h c) -> p h c", h=4)[:, :, :r], ACT.Copy).then_inc(qtg, 1)

            for t in range(NT):
                r = ROWS[t]
                for half in range(2):
                    n = 2 * t + half
                    act.wait_ge(qf, n + 1)
                    if t >= 2:
                        act.wait_ge(qt, 2 * t - 2)
                    act.activation(q_nat[:r, t % 2, half * QL:(half + 1) * QL], g.bank[:r, n % 4, :QL], ACT.Copy,
                                   scale=root_q[:r, t:t + 1]).then_inc(qg, 1)
                if t >= 1:
                    turned_out(t - 1)
            turned_out(NT - 1)
            for j in range(NT - 1):
                act.wait_ge(vf, j + 1)
                act.activation(g.vb[:, j, :], g.bank[:, j % 4, :], ACT.Copy).then_inc(vg, 1)

        @block.vector
        def _(dve):
            for t in range(NT):
                r = ROWS[t]
                dve.wait_ge(qg, 2 * t + 2)
                rotate(dve, q_nat[:r, t % 2, :].rearrange("p (h e) -> p h e", e=BH)[:, :, E:], 16, cos_b[:r, t, :],
                       sin_b[:r, t, :], ra[:r], rb[:r], H, l_step, 2 * t, qr, t)
            for n in range(2 * H):
                h, half = divmod(n, 2)
                dve.wait_ge(kf, n + 1)
                dve.tensor_copy(g.kb_t[:E, h, half * 512:(half + 1) * 512], g.bank[:E, 6 + n % 2, :]).then_inc(kg, 1)
            dve.wait_ge(lf, 1)
            dve.tensor_copy(g.qpe_t[:, :, :, :].rearrange("r s h t -> r h s t"),
                            g.bank[:RD, 4, :H * NS].rearrange("r (h s t) -> r h s t", h=H, s=NSEQ))
            dve.wait_ge(lf, 2)
            for c in range(2):
                dve.tensor_copy(g.ql_t[:, c].rearrange("p s h t -> p h s t"),
                                g.bank[:, 5, c * H * NS:(c + 1) * H * NS].rearrange("p (h s t) -> p h s t", h=H, s=NSEQ))


def attend_prompt(g, kind, ahead):
    nc = g.nc
    window = kind == "window"
    room = Room(nc, R2 if window else g.room_b, ahead.start)
    sem = lambda name: g.sem(f"{kind[0]}_{name}")
    if window:
        q_t = room("qw_t", [P, H // 2, SEQ])
        k_t = room("kw_t", [P, H // 2, SEQ])
        v = room("vw", [P, NT - 1, H * E])
        load_window(g, room, q_t, k_t, v)
        head = lambda x, h: x[E * (h % 2):E * (h % 2) + E, h // 2, :]
    else:
        q_t, k_t, v = g.qb_t, g.kb_t, g.vb
        head = lambda x, h: x[:, h, :]
    mask = room(f"{kind}_mask", [P, NT - 1, P])
    prob = room(f"{kind}_prob", [P, 4, SEQ])
    prob_t = room(f"{kind}_prob_t", [P, 2, NT - 1, P])
    top = room(f"{kind}_top", [P, 4, 4])
    mask_in, s_full, s_got, negated, e_done, inv_done, p_ready, t_full, t_got, o_full, o_hi_s, o_got = map(sem, (
        "mask_in", "s_full", "s_got", "negated", "e_done", "inv_done", "p_ready", "t_full", "t_got", "o_full", "o_hi", "o_got"))
    steps = [(h, i) for h in range(H) for i in range(NT - 1)]
    groups = []
    n = 0
    for h, i in steps:
        mine = []
        for j in range(0, i + 1, 4):
            mine.append((n, j, min(j + 4, i + 1)))
            n += 1
        groups.append(mine)
    N = len(steps)
    with nc.Block() as block:

        @block.sync
        def _(sp):
            sp.dma_start(mask[:, :, :], g.mask_w_c if window else g.mask_b_c).then_inc(mask_in, 16)
            ahead.load(g, sp)
            if not window:
                for s in range(NSEQ):
                    sp.wait_ge(o_got, s * (N // NSEQ) + 1)
                    copy_cache(sp, g, g.cache_win_v, g.win_v_sample, s, 1)

        @block.gpsimd
        def _(pool):
            if not window:
                ahead.load_rotary(g, pool)

        @block.tensor
        def _(pe):
            def scores(s):
                h, i = steps[s]
                if s >= 2:
                    pe.wait_ge(s_got, s - 1)
                for at in range(0, (i + 1) * P, 512):
                    w = min(512, (i + 1) * P - at)
                    last = pe.matmul(g.bank[:, 2 * (s % 2) + at // 512, :w], head(q_t, h)[:, i * P:(i + 1) * P],
                                     head(k_t, h)[:, at:at + w], start=True, stop=True)
                last.then_inc(s_full, 1)

            def transposes(s):
                pe.wait_ge(p_ready, s + 1)
                for n, a, b in groups[s]:
                    if n >= 2:
                        pe.wait_ge(t_got, n - 1)
                    for j in range(a, b):
                        last = pe.transpose(g.bank[:, 4 + n % 2, (j - a) * P:(j - a + 1) * P],
                                            prob[:, s % 4, j * P:(j + 1) * P], g.ident[:, :])
                    last.then_inc(t_full, 1)

            def values(s):
                h, i = steps[s]
                if s >= 2:
                    pe.wait_ge(o_got, s - 1)
                lo = E * (h % 2)
                for n, a, b in groups[s]:
                    pe.wait_ge(t_got, n + 1)
                    for j in range(a, b):
                        last = pe.matmul(g.bank[lo:lo + E, 6 + s % 2, :P], v[:, j, h * E:(h + 1) * E],
                                         prob_t[:, s % 2, j, :], start=j == 0, stop=j == i)
                last.then_inc(o_full, 1)

            for s in range(3):
                scores(s)
            for s in range(N):
                if s + 3 < N:
                    scores(s + 3)
                transposes(s)
                if s >= 1:
                    values(s - 1)
            values(N - 1)

        @block.vector
        def _(dve):
            def largest(s):
                h, i = steps[s]
                w = (i + 1) * P
                dve.wait_ge(s_full, s + 1)
                if s >= 4:
                    dve.wait_ge(t_full, groups[s - 4][-1][0] + 1)
                dve.tensor_tensor_reduce(out=prob[:, s % 4, :w],
                                         in0=g.bank[:, 2 * (s % 2):2 * (s % 2) + 2, :].rearrange("p a b -> p (a b)")[:, :w],
                                         in1=mask[:, NT - 2 - i:, :].rearrange("p a b -> p (a b)"),
                                         scale=1.0, scalar=FLOOR, op0=ALU.add, op1=ALU.max,
                                         accum_out=top[:, s % 4, 0:1]).then_inc(s_got, 1)
                dve.wait_ge(s_got, s + 1)
                dve.tensor_scalar(top[:, s % 4, 1:2], top[:, s % 4, 0:1], -1.0, None, ALU.mult).then_inc(negated, 1)

            def divide(s):
                h, i = steps[s]
                w = (i + 1) * P
                dve.wait_ge(e_done, s + 1)
                dve.reciprocal(top[:, s % 4, 3:4], top[:, s % 4, 2:3]).then_inc(inv_done, 1)
                dve.wait_ge(inv_done, s + 1)
                dve.tensor_scalar(prob[:, s % 4, :w], prob[:, s % 4, :w], top[:, s % 4, 3:4], None, ALU.mult).then_inc(p_ready, 1)

            def take(s):
                h, i = steps[s]
                lo = E * (h % 2)
                tile = h // 2 + (0 if window else H // 2)
                place = (slice(lo, lo + E), tile, slice(i * P, (i + 1) * P))
                dve.wait_ge(o_full, s + 1)
                dve.tensor_copy(g.o_hi[place], g.bank[lo:lo + E, 6 + s % 2, :P]).then_inc(o_hi_s, 1)
                dve.wait_ge(o_hi_s, s + 1)
                dve.tensor_tensor(g.o_lo[place], g.bank[lo:lo + E, 6 + s % 2, :P], g.o_hi[place].bitcast(F32),
                                  ALU.subtract).then_inc(o_got, 1)

            dve.wait_ge(mask_in, 16)
            largest(0)
            largest(1)
            for s in range(N):
                divide(s)
                if s + 2 < N:
                    largest(s + 2)
                if s >= 2:
                    take(s - 2)
            take(N - 2)
            take(N - 1)

        @block.scalar
        def _(act):
            def exponent(s):
                h, i = steps[s]
                w = (i + 1) * P
                act.wait_ge(negated, s + 1)
                act.activation(prob[:, s % 4, :w], prob[:, s % 4, :w], ACT.Exp, bias=top[:, s % 4, 1:2],
                               accum_out=top[:, s % 4, 2:3]).then_inc(e_done, 1)

            exponent(0)
            exponent(1)
            for s in range(N):
                if s >= 2:
                    act.wait_ge(o_full, s - 1)
                for n, a, b in groups[s]:
                    act.wait_ge(t_full, n + 1)
                    act.activation(prob_t[:, s % 2, a:b, :].rearrange("p a b -> p (a b)"),
                                   g.bank[:, 4 + n % 2, :(b - a) * P], ACT.Copy).then_inc(t_got, 1)
                if s + 2 < N:
                    exponent(s + 2)


def load_window(g, room, q_t, k_t, v):
    nc = g.nc
    nat = room("win_nat", [P, 2, NT - 1, H * E // 2])
    wq_in, wv_in, wt_full, wt_got = map(g.sem, ("wq_in", "wv_in", "wt_full", "wt_got"))
    jobs = [(x, half) for x in range(2) for half in range(2)]
    with nc.Block() as block:

        @block.sync
        def _(sp):
            for m, (x, half) in enumerate(jobs):
                if m >= 2:
                    sp.wait_ge(wt_full, 4 * (m - 1))
                src = (g.q_d, g.k_d)[x][:SEQ, half * 256:(half + 1) * 256]
                sp.dma_start(nat[:, m % 2], src.rearrange("(t p) c -> p t c", p=P)).then_inc(wq_in, 16)
                sp.wait_ge(wq_in, 16 * (m + 1))
            sp.dma_start(v[:, :, :], g.v_d[:SEQ, :].rearrange("(t p) c -> p t c", p=P)).then_inc(wv_in, 16)
            sp.wait_ge(wv_in, 16)

        @block.tensor
        def _(pe):
            n = 0
            for m, (x, half) in enumerate(jobs):
                pe.wait_ge(wq_in, 16 * (m + 1))
                for tile in range(2):
                    for quad in range(2):
                        if n >= 4:
                            pe.wait_ge(wt_got, n - 3)
                        for t in range(4):
                            last = pe.transpose(g.bank[:, n % 4, t * P:(t + 1) * P],
                                                nat[:, m % 2, 4 * quad + t, tile * P:(tile + 1) * P], g.ident[:, :])
                        last.then_inc(wt_full, 1)
                        n += 1

        def take(eng, n, copy):
            m, tile, quad = n // 4, n // 2 % 2, n % 2
            x, half = jobs[m]
            eng.wait_ge(wt_full, n + 1)
            copy((q_t, k_t)[x][:, 2 * half + tile, quad * 512:(quad + 1) * 512], g.bank[:, n % 4, :]).then_inc(wt_got, 1)

        @block.vector
        def _(dve):
            for n in range(16):
                take(dve, n, dve.tensor_copy)


class Ahead:

    def __init__(self, g, kind):
        self.kind = kind
        if kind == "window":
            size = 2 * SK * H * E * BYTES
            room = Room(g.nc, TOP // 32 * 32 - size)
            self.keys, self.vals = (room(f"ws_{n}0", [P, SK, H * E]) for n in ("keys", "vals"))
            self.k_in, self.v_in = ([g.sem(f"ws_{n}_in{j}") for j in range(3)] for n in "kv")
        else:
            size = NPAGE * (KL + RD) * BYTES + NSEQ * NPAGE * BYTES
            room = Room(g.nc, TOP // 32 * 32 - size)
            self.keys = self.vals = room("ls_keys0", [P, NPAGE, KL + RD])
            self.pages = room("ls_pages", [1, NSEQ * NPAGE], I32)
            self.k_in, self.v_in = ([g.sem(f"ls_{n}_in{j}") for j in range(4)] for n in ("ckv", "kpe"))
            self.pages_in = g.sem("pages_in")
        self.start = TOP // 32 * 32 - size

    def load(self, g, sp):
        if self.kind == "window":
            load_cached_window(sp, g.cache_win_k, 0, self.keys, self.k_in[0])
            load_cached_window(sp, g.cache_win_v, 0, self.vals, self.v_in[0])
        else:
            sp.dma_start(self.pages[:, :], g.page_table.rearrange("(a s) n -> a (s n)", a=1)).then_inc(self.pages_in, 16)
            sp.wait_ge(self.pages_in, 16)
            load_pages(sp, self.pages, 0, g.cache_ckv, self.keys[:, :, :KL], self.k_in[0])

    def load_rotary(self, g, pool):
        pool.wait_ge(self.pages_in, 16)
        load_pages(pool, self.pages, 0, g.cache_kpe, self.keys[:, :, KL:], self.v_in[0])


def load_cached_window(sp, cache, s, dst, arrived):
    far = cache[0, s, 0:PAST // 2].rearrange("(m r) h e -> m r (h e)", r=16)
    for r in range(4):
        sp.dma_start(dst[32 * r:32 * r + 32, 0, :], far[:, r, :]).then_inc(arrived, 16)
    sp.dma_start(dst[:, 1:, :], cache[0, s, PAST // 2:].rearrange("(a p) h e -> p a (h e)", p=P)).then_inc(arrived, 16)


def load_pages(eng, pages, s, cache, dst, arrived):
    for n in range(NPAGE):
        page = eng.value_load(pages[0:1, s * NPAGE + n:s * NPAGE + n + 1], min_val=0, max_val=NPHYS - 1)
        eng.dma_start(dst[:, n, :], cache[0, bass.ds(page, 1)].rearrange("a p c -> p (a c)")).then_inc(arrived, 16)


def attend_sample(g, kind, ahead):
    nc = g.nc
    window = kind == "window"
    tag = "ws" if window else "ls"
    tiles = SK if window else NPAGE
    width = tiles * P + TDEC
    vcols = H * E if window else KL
    room = Room(nc, R2, ahead.start if window else g.room_kept)
    sem = lambda name: g.sem(f"{tag}_{name}")
    if window:
        keys = [ahead.keys] + [room(f"ws_keys{j}", [P, SK, H * E]) for j in (1, 2)]
        vals = [ahead.vals] + [room(f"ws_vals{j}", [P, SK, H * E]) for j in (1, 2)]
        key_t = room("ws_key_t", [P, H // 2, width])
        q_new = room("ws_q_new", [NS, H * E])
        k_new = room("ws_k_new", [NS, H * E])
        k_new_t = room("ws_k_new_t", [P, H // 2, NS])
        q_rows = room("ws_q_rows", [P, H // 2, NSEQ, H, TDEC])
        v_new = room("ws_v_new", [TDEC, NSEQ, H * E])
    else:
        keys = [ahead.keys] + [room(f"ls_keys{j}", [P, NPAGE, KL + RD]) for j in (1, 2, 3)]
        vals = keys
        key_t = room("ls_key_t", [P, 2, width])
        pe_t = room("ls_pe_t", [RD, width])
        v_new = room("ls_v_new", [TDEC, NSEQ, KL])
        o_t = room("ls_o_t", [P, 2, H, NSEQ, TDEC])
    mask = room(f"{tag}_mask", [NS, width])
    masked = room(f"{tag}_masked", [NS, width])
    prob = room(f"{tag}_prob", [NS, width])
    prob_t = room(f"{tag}_prob_t", [P, tiles + 1, NS])
    top = room(f"{tag}_top", [NS, 2, 4])
    o_nat = room(f"{tag}_o_nat", [NS, vcols])
    (c_in, new_full, new_got, q_set, k_full, s_full, s_got, negated, e_done, inv_done, p_ready,
     pt_full, pt_got, o_full, o_taken, ot_full, ot_got, o_hi_s, o_lo_s) = map(sem, (
         "c_in", "new_full", "new_got", "q_set", "k_full", "s_full", "s_got", "negated", "e_done",
         "inv_done", "p_ready", "pt_full", "pt_got", "o_full", "o_taken", "ot_full", "ot_got", "o_hi", "o_lo"))
    k_got = [sem(f"k_got{odd}") for odd in range(2)]
    k_in, v_in = ahead.k_in, ahead.v_in
    ring = len(keys)
    kv_count = 80 if window else 16 * NPAGE
    n_const = (4 if window else 2) * 16
    each = [len(range(odd, tiles, 2)) for odd in range(2)]

    def take_keys(eng, s, odd):
        copy = eng.tensor_copy if odd else lambda out, src: eng.activation(out, src, ACT.Copy)
        if s >= 1:
            eng.wait_ge(s_full, s)
        for n in range(odd, tiles, 2):
            eng.wait_ge(k_full, s * tiles + n + 1)
            cols = slice(n * P, (n + 1) * P)
            kt = 4 if window else 2
            last = copy(key_t[:, :, cols], g.bank[:, 3 + odd, :kt * P].rearrange("p (k c) -> p k c", k=kt))
            if not window:
                last = copy(pe_t[:, cols], g.bank[:RD, 3 + odd, 2 * P:3 * P])
            last.then_inc(k_got[odd], 1)

    def exponent(act, s):
        act.wait_ge(negated, s + 1)
        if s >= 1:
            act.wait_ge(pt_full, s)
        act.activation(prob[:, :], masked[:, :], ACT.Exp, bias=top[:, s % 2, 1:2], accum_out=top[:, s % 2, 2:3]).then_inc(e_done, 1)

    scores_flat = g.bank[:NS, 0:3, :].rearrange("p a b -> p (a b)")[:, :width]
    with nc.Block() as block:

        @block.sync
        def _(sp):
            sp.dma_start(mask[:, :], g.mask_ws_c if window else g.mask_ls_c).then_inc(c_in, 16)
            if window:
                sp.dma_start(q_new[:, :], g.q_d[SEQ:, :]).then_inc(c_in, 16)
                sp.dma_start(k_new[:, :], g.k_d[SEQ:, :]).then_inc(c_in, 16)
                sp.dma_start(v_new[:, :, :], g.v_d[SEQ:, :].rearrange("(s t) c -> t s c", t=TDEC)).then_inc(c_in, 16)
            else:
                sp.dma_start(v_new[:, :, :], g.ckv_sample[0].rearrange("s t c -> t s c")).then_inc(c_in, 16)
            for s in range(1, NSEQ):
                j = s % ring
                if s >= ring:
                    if window:
                        sp.wait_ge(k_full, (s - ring + 1) * tiles)
                    else:
                        sp.wait_ge(o_full, s - ring + 1)
                if window:
                    load_cached_window(sp, g.cache_win_k, s, keys[j], k_in[j])
                    if s >= ring:
                        sp.wait_ge(o_full, s - ring + 1)
                    load_cached_window(sp, g.cache_win_v, s, vals[j], v_in[j])
                else:
                    load_pages(sp, ahead.pages, s, g.cache_ckv, keys[j][:, :, :KL], k_in[j])

        @block.gpsimd
        def _(pool):
            if not window:
                for s in range(1, NSEQ):
                    j = s % ring
                    if s >= ring:
                        pool.wait_ge(o_full, s - ring + 1)
                    load_pages(pool, ahead.pages, s, g.cache_kpe, keys[j][:, :, KL:], v_in[j])

        @block.tensor
        def _(pe):
            def turn_keys(s):
                pe.wait_ge(k_in[s % ring], kv_count * (s // ring + 1))
                if not window:
                    pe.wait_ge(v_in[s % ring], kv_count * (s // ring + 1))
                for n in range(tiles):
                    if s or n >= 2:
                        pe.wait_ge(k_got[n % 2], s * each[n % 2] + n // 2)
                    b = 3 + n % 2
                    for k in range(4 if window else 2):
                        last = pe.transpose(g.bank[:, b, k * P:(k + 1) * P], keys[s % ring][:, n, k * P:(k + 1) * P], g.ident[:, :])
                    if not window:
                        last = pe.transpose(g.bank[:RD, b, 2 * P:3 * P], keys[s % ring][:, n, KL:], g.ident[:, :])
                    last.then_inc(k_full, 1)

            def scores(s):
                for odd in range(2):
                    pe.wait_ge(k_got[odd], (s + 1) * each[odd])
                pe.wait_ge(new_got, s + 1)
                if s >= 1:
                    pe.wait_ge(s_got, s)
                for at in range(0, width, 512):
                    w = min(512, width - at)
                    out = g.bank[:NS, at // 512, :w]
                    if window:
                        for k in range(4):
                            last = pe.matmul(out, q_rows[:, k, s].rearrange("p h t -> p (h t)"), key_t[:, k, at:at + w],
                                             start=k == 0, stop=k == 3)
                    else:
                        for k in range(2):
                            pe.matmul(out, g.ql_t[:, k, s].rearrange("p h t -> p (h t)"), key_t[:, k, at:at + w],
                                      start=k == 0, stop=False)
                        last = pe.matmul(out, g.qpe_t[:, s].rearrange("p h t -> p (h t)"), pe_t[:, at:at + w],
                                         start=False, stop=True)
                last.then_inc(s_full, 1)

            def turn_probs(s):
                pe.wait_ge(p_ready, s + 1)
                if s >= 1:
                    pe.wait_ge(pt_got, s)
                for n in range(tiles):
                    pe.transpose(g.bank[:, 5, n * NS:(n + 1) * NS], prob[:, n * P:(n + 1) * P], g.ident[:NS, :NS])
                pe.transpose(g.bank[:TDEC, 5, tiles * NS:(tiles + 1) * NS], prob[:, tiles * P:], g.ident[:NS, :NS]).then_inc(pt_full, 1)

            def values(s):
                if window:
                    pe.wait_ge(v_in[s % ring], kv_count * (s // ring + 1))
                pe.wait_ge(pt_got, s + 1)
                if s >= 1:
                    pe.wait_ge(o_taken, s)
                for n in range(tiles):
                    pe.matmul(g.bank[:NS, 6, :vcols], prob_t[:, n, :], vals[s % ring][:, n, :vcols], start=n == 0, stop=False)
                pe.matmul(g.bank[:NS, 6, :vcols], prob_t[:TDEC, tiles, :], v_new[:, s, :], start=False, stop=True).then_inc(o_full, 1)

            def turn_result(s):
                pe.wait_ge(o_taken, s + 1)
                if s >= 1:
                    pe.wait_ge(ot_got, s)
                for k in range(vcols // P):
                    last = pe.transpose(g.bank[:, 7, k * NS:(k + 1) * NS], o_nat[:, k * P:(k + 1) * P], g.ident[:NS, :NS])
                last.then_inc(ot_full, 1)

            if window:
                pe.wait_ge(c_in, n_const)
                for x in (q_new, k_new):
                    for k in range(4):
                        at = (0 if x is q_new else P) + k * NS
                        last = pe.transpose(g.bank[:, 7, at:at + NS], x[:, k * P:(k + 1) * P], g.ident[:NS, :NS])
                last.then_inc(new_full, 1)
            turn_keys(0)
            pe.wait_ge(q_set, 1)
            scores(0)
            turn_keys(1)
            for s in range(NSEQ):
                if s + 1 < NSEQ:
                    scores(s + 1)
                turn_probs(s)
                if s + 2 < NSEQ:
                    turn_keys(s + 2)
                if s >= 1:
                    turn_result(s - 1)
                values(s)
            turn_result(NSEQ - 1)
            if not window:
                pe.wait_ge(ot_got, NSEQ)
                for h in range(H):
                    lo = E * (h % 2)
                    for c in range(2):
                        last = pe.matmul(g.bank[lo:lo + E, 5 + h % 2, (h // 2) * NS:(h // 2 + 1) * NS], g.w_uv_sb[:, c, h * E:(h + 1) * E],
                                         o_t[:, c, h].rearrange("p s t -> p (s t)"), start=c == 0, stop=c == 1)
                last.then_inc(ot_full, 1)

        @block.scalar
        def _(act):
            for s in range(2):
                take_keys(act, s, 0)
                if s == 0:
                    exponent(act, s)
            for s in range(NSEQ):
                if s + 2 < NSEQ:
                    take_keys(act, s + 2, 0)
                if s + 1 < NSEQ:
                    exponent(act, s + 1)

        @block.vector
        def _(dve):
            def add_new(s):
                if s >= 1:
                    dve.wait_ge(s_full, s)
                if window:
                    dve.tensor_copy(key_t[:, :, SK * P:], k_new_t[:, :, s * TDEC:(s + 1) * TDEC]).then_inc(new_got, 1)
                else:
                    dve.tensor_copy(key_t[:, :, PAST:], g.ckv_t[:, :, SEQ + s * TDEC:SEQ + (s + 1) * TDEC])
                    dve.tensor_copy(pe_t[:, PAST:], g.kpe_t[:, s * TDEC:(s + 1) * TDEC]).then_inc(new_got, 1)

            if window:
                dve.memset(q_rows[:, :, :, :, :].rearrange("p k s h t -> p (k s h t)"), 0.0).then_inc(q_set, 1)
                dve.wait_ge(new_full, 1)
                dve.wait_ge(q_set, 1)
                for h in range(H):
                    lo, k = E * (h % 2), h // 2
                    dve.tensor_copy(q_rows[lo:lo + E, k, :, h, :],
                                    g.bank[lo:lo + E, 7, k * NS:(k + 1) * NS].rearrange("p (s t) -> p s t", s=NSEQ))
                dve.tensor_copy(k_new_t[:, :, :], g.bank[:, 7, P:2 * P].rearrange("p (k c) -> p k c", k=4)).then_inc(q_set, 1)
                dve.wait_ge(q_set, 2)
            else:
                dve.memset(masked[:, :], 0.0).then_inc(q_set, 1)
            def largest(s):
                dve.wait_ge(s_full, s + 1)
                if s >= 1:
                    dve.wait_ge(e_done, s)
                dve.tensor_tensor_reduce(out=masked[:, :], in0=scores_flat, in1=mask[:, :], scale=1.0, scalar=FLOOR,
                                         op0=ALU.add, op1=ALU.max, accum_out=top[:, s % 2, 0:1]).then_inc(s_got, 1)
                dve.wait_ge(s_got, s + 1)
                dve.tensor_scalar(top[:, s % 2, 1:2], top[:, s % 2, 0:1], -1.0, None, ALU.mult).then_inc(negated, 1)

            def divide(s):
                dve.wait_ge(e_done, s + 1)
                dve.reciprocal(top[:, s % 2, 3:4], top[:, s % 2, 2:3]).then_inc(inv_done, 1)
                dve.wait_ge(inv_done, s + 1)
                dve.tensor_scalar(prob[:, :], prob[:, :], top[:, s % 2, 3:4], None, ALU.mult).then_inc(p_ready, 1)

            def take_probs(s):
                dve.wait_ge(pt_full, s + 1)
                if s >= 1:
                    dve.wait_ge(o_full, s)
                dve.tensor_copy(prob_t[:, :tiles, :].rearrange("p a b -> p (a b)"), g.bank[:, 5, :tiles * NS])
                dve.tensor_copy(prob_t[:TDEC, tiles, :], g.bank[:TDEC, 5, tiles * NS:(tiles + 1) * NS]).then_inc(pt_got, 1)

            def take_result(s):
                dve.wait_ge(ot_full, s + 1)
                if window:
                    at = SEQ + s * TDEC
                    for odd in range(2):
                        lo = E * odd
                        src = g.bank[lo:lo + E, 7, 0:160].rearrange("p (a c) -> p a c", c=NS + 2 * TDEC)[:, :, odd * TDEC:(odd + 1) * TDEC]
                        place = (slice(lo, lo + E), slice(0, H // 2), slice(at, at + TDEC))
                        dve.tensor_copy(g.o_hi[place], src).then_inc(o_hi_s, 1)
                        dve.wait_ge(o_hi_s, 2 * s + odd + 1)
                        last = dve.tensor_tensor(g.o_lo[place], src, g.o_hi[place].bitcast(F32), ALU.subtract)
                    last.then_inc(ot_got, 1)
                else:
                    dve.tensor_copy(o_t[:, :, :, s, :], g.bank[:, 7, :2 * NS].rearrange("p (c h t) -> p c h t", c=2, h=H)).then_inc(ot_got, 1)

            add_new(0)
            take_keys(dve, 0, 1)
            dve.wait_ge(c_in, n_const)
            largest(0)
            add_new(1)
            take_keys(dve, 1, 1)
            divide(0)
            for s in range(NSEQ):
                if s + 1 < NSEQ:
                    largest(s + 1)
                take_probs(s)
                if s + 2 < NSEQ:
                    add_new(s + 2)
                    take_keys(dve, s + 2, 1)
                if s >= 1:
                    take_result(s - 1)
                if s + 1 < NSEQ:
                    divide(s + 1)
                dve.wait_ge(o_full, s + 1)
                if s >= 1:
                    dve.wait_ge(ot_full, s)
                dve.tensor_copy(o_nat[:, :], g.bank[:NS, 6, :vcols]).then_inc(o_taken, 1)
            take_result(NSEQ - 1)
            if not window:
                dve.wait_ge(ot_full, NSEQ + 1)
                for odd in range(2):
                    lo = E * odd
                    src = g.bank[lo:lo + E, 5 + odd, :P].rearrange("p (a c) -> p a c", a=4)
                    place = (slice(lo, lo + E), slice(H // 2, H), slice(SEQ, T))
                    dve.tensor_copy(g.o_hi[place], src).then_inc(o_hi_s, 1)
                    dve.wait_ge(o_hi_s, odd + 1)
                    dve.tensor_tensor(g.o_lo[place], src, g.o_hi[place].bitcast(F32), ALU.subtract)


class Step:

    def __init__(self, g, kind, w, act, out=None, gain=None, per_unit=3):
        self.kind, self.w, self.act, self.out, self.gain, self.per_unit = kind, w, act, out, gain, per_unit
        self.prev = g.steps[-1] if g.steps else None
        self.unit, self.chunk, self.turn, self.part, self.square = g.units, g.chunks, g.turns, g.parts, g.squares
        g.steps.append(self)
        g.units += KD
        g.chunks += per_unit * KD
        g.turns += KD // 2 * (2 if kind == "merge" else 1)
        g.parts += NCH * KD if out else 0
        g.squares += NCH * KD if gain is not None or kind == "ple" else 0


def run_tail(g):
    nc = g.nc
    unit_room(g, Room(nc, RW, RM), "fin")
    room = Room(nc, RM)
    g.hg, g.tmp = room("f_hg", [P, 2, CH]), room("f_tmp", [P, 2, CH])
    g.gate_in_sb = room("f_gates", [P, 2, 2, CH])
    room = Room(nc, R1, R2)
    h = (room("h2_hi", [P, KD, T], F32R), room("h2_lo", [P, KD, T], F32R))
    room = Room(nc, R2, RX)
    z = (room("z_hi", [P, KD, T], F32R), room("z_lo", [P, KD, T], F32R))
    room = Room(nc, R2, RX)
    a = (room("a_hi", [P, KD, T], F32R), room("a_lo", [P, KD, T], F32R))
    room = Room(nc, R2, RX)
    g.diag = room("f_diag", [P, NT, P])
    g.stat = room("f_stat", [P, NT])
    g.p_t = room("p_t_sb", [P, 2, T])
    g.p_hi, g.p_lo = room("p_hi", [P, 2, T], F32R), room("p_lo", [P, 2, T], F32R)
    g.wp = room("w_ple_sb", [P, 2, D])
    g.wp_hi, g.wp_lo = room("w_ple_hi", [P, 2, D], F32R), room("w_ple_lo", [P, 2, D], F32R)
    g.total = room("final_total", [P, T])
    g.sig = room("ple_sig", [P, 2, CH])
    g.root = room("y_root", [P, NT])
    g.x = Room(nc, RX, RW)("x_res", [P, KD, T])
    g.y = Room(nc, R1, R2)("y_nat", [P, 3, D])
    (g.hg_s, g.hi_s, g.lo_s, g.sq_s, g.acc_s, g.clear_s, g.x_in, g.sum_s, g.stat_s, g.mean_s, g.root_s,
     g.diag_s, g.bc_s, g.bc_got, g.p_in, g.p_hi_s, g.p_lo_s, g.sig_s, g.px_s, g.pdone_s, g.y_full, g.y_got) = map(g.sem, (
         "t_hg", "t_hi", "t_lo", "t_sq", "t_acc", "t_clear", "t_x_in", "t_sum", "t_stat", "t_mean", "t_root",
         "t_diag", "t_bc", "t_bc_got", "t_p_in", "t_p_hi", "t_p_lo", "t_sig", "t_px", "t_pdone", "t_y_full", "t_y_got"))
    g.gates_in = [g.sem(f"t_gates_in{j}") for j in range(2)]
    y_out = [g.sem(f"y_out{j}") for j in range(3)]
    g.parts = g.squares = 0
    g.steps = []
    Step(g, "merge", None, (g.o_hi, g.o_lo), z, per_unit=6)
    Step(g, "residual", g.w_o[0], z, h, gain=1)
    for f in range(NF):
        Step(g, "up", g.w_up[0, :, f * D:(f + 1) * D], h, a)
        out, gain = (h, 2) if f == NF - 1 else (None, None)
        Step(g, "residual", g.w_down[0, f * D:(f + 1) * D, :], a, out, gain)
    Step(g, "ple", g.w_ple_gate[0], h, per_unit=6)
    factors = [g.steps[2], g.steps[-1]]
    steps = g.steps

    with nc.Block() as block:

        @block.sync
        def _(sp):
            sp.dma_start(g.x[:, :, :], g.xt_d).then_inc(g.x_in, 16)
            for st in steps:
                def pair(i, st=st):
                    for j in range(2):
                        sp.wait_ge(g.w_split, i * 2 + st.unit + j - 1)
                        if st.kind == "merge":
                            for half, w in enumerate((g.w_oa, g.w_ob)):
                                sp.dma_start(g.w_stage[:, j, 4 * half:4 * half + 4, :], columns(w[0], i * 2 + j)).then_inc(g.w_loaded[j], 16)
                        else:
                            sp.dma_start(g.w_stage[:, j], columns(st.w, i * 2 + j)).then_inc(g.w_loaded[j], 16)
                in_pairs(sp, KD, pair, peel=False)
                if st is steps[-2]:
                    sp.wait_ge(g.full, steps[-1].chunk)
                    sp.dma_start(g.p_t[:, :, :], g.p_t_d).then_inc(g.p_in, 16)
                    sp.dma_start(g.wp[:, :, :], g.w_ple[0].rearrange("(k p) c -> p k c", p=P)).then_inc(g.p_in, 16)
            for t in range(NT):
                sp.wait_ge(g.y_got, t + 1)
                dst = g.y_prompt[0, t * P:(t + 1) * P, :] if t < NT - 1 else g.y_sample.rearrange("s t d -> (s t) d")
                sp.dma_start(dst, g.y[:ROWS[t], t % 3, :]).then_inc(y_out[t % 3], 16)
            for j in range(3):
                sp.wait_ge(y_out[j], 16 * len(range(j, NT, 3)))
            sp.wait_ge(g.copied, 16 * 2 * NSEQ)

        @block.gpsimd
        def _(pool):
            for st in steps:
                def pair(i, st=st):
                    for j in range(2):
                        per = 2 if st.kind == "merge" else 1
                        pool.wait_ge(g.w_loaded[j], (i * per + st.turn + per) * 16)
                        before = st.prev.per_unit if first(i) and st.prev else st.per_unit
                        pool.wait_ge(g.full, i * (2 * st.per_unit) + st.chunk - (before if j == 0 else 0))
                        split_weights(pool, g, j, i * 2 + st.unit + j + 1)
                        if j == 1:
                            low_parts(pool, g, st, i, 0)
                        elif not first(i):
                            low_parts(pool, g, st, i - 1, 1)
                        else:
                            if st.prev:
                                low_parts(pool, g, st.prev, KD // 2 - 1, 1)
                            if st in factors:
                                pool.wait_ge(g.stat_s, 2 * factors.index(st) + 2)
                                inverse_root(pool, g, g.stat[:, :], g.stat[:, :], 1.0 / D, g.mean_s, factors.index(st) + 1, g.root_s)
                in_pairs(pool, KD, pair)
            pool.wait_ge(g.stat_s, 6)
            inverse_root(pool, g, g.root[:, :], g.stat[:, :], 1.0 / D, g.mean_s, 3, g.root_s)

        @block.tensor
        def _(pe):
            for st in steps:
                if st.kind == "ple":
                    for m in range(KD):
                        embed_unit(pe, g, st, m, factors)
                    continue

                def pair(i, st=st):
                    for j in range(2):
                        pe.wait_ge(g.w_split, i * 2 + st.unit + j + 1)
                        for n in range(st.per_unit):
                            c, half = (n // 2, n % 2) if st.kind == "merge" else (n, 0)
                            if first(i) and j == 0 and st.prev and half == 0:
                                pe.wait_ge(g.lo_s, st.part - 2 + c)
                            pe.wait_ge(g.free, i * (2 * st.per_unit) + st.chunk + st.per_unit * j + n - 5)
                            ks = [(4 * half + k, 4 * half + k) for k in range(4)] if st.kind == "merge" else [(k, k) for k in range(KD)]
                            multiply_chunk(pe, g, (st.per_unit * j + n) % 6, j, c, ks, *st.act)
                            if first(i) and st in factors:
                                factor_products(pe, g, factors.index(st), [(0, 0), (0, 2), (1, 0)], (j, n))
                in_pairs(pe, KD, pair)
            write_products(pe, g)

        @block.vector
        def _(dve):
            dve.memset(g.rstd_bc[:, :], 0.0).then_inc(g.clear_s, 1)
            for st in steps:
                if st.kind == "ple":
                    dve.memset(g.total[:, :], 0.0).then_inc(g.clear_s, 1)
                    dve.wait_ge(g.p_hi_s, 2)
                    dve.tensor_tensor(g.p_lo[:, :, :], g.p_t[:, :, :], g.p_hi[:, :, :].bitcast(F32), ALU.subtract).then_inc(g.p_lo_s, 1)
                    dve.tensor_tensor(g.wp_lo[:, :, :], g.wp[:, :, :], g.wp_hi[:, :, :].bitcast(F32), ALU.subtract).then_inc(g.p_lo_s, 1)
                    dve.wait_ge(g.clear_s, 3)
                if st in factors:
                    spread_factors(dve, g, factors.index(st))
                if st.kind == "residual" and st.prev.kind == "merge":
                    dve.wait_ge(g.x_in, 16)
                    dve.wait_ge(g.clear_s, 1)
                if st is steps[-2]:
                    dve.memset(g.rstd_bc[:, :], 0.0).then_inc(g.clear_s, 1)
                    dve.wait_ge(g.clear_s, 2)
                take = {"merge": take_merge, "residual": take_residual, "up": take_up, "ple": take_embedding}[st.kind]
                in_pairs(dve, KD, lambda i, st=st, take=take: take(dve, g, st, i), peel=st.prev is None)
            dve.memset(g.stat[:, :], float(D)).then_inc(g.stat_s, 1)
            copy_sums(dve, g, 3)

        @block.scalar
        def _(act):
            for q in range(2):
                load_gates(act, g, 0, q)
            for st in steps:
                if st.kind == "ple":
                    act.wait_ge(g.p_in, 32)
                    act.activation(g.p_hi[:, :, :], g.p_t[:, :, :], ACT.Copy).then_inc(g.p_hi_s, 1)
                    act.activation(g.wp_hi[:, :, :], g.wp[:, :, :], ACT.Copy).then_inc(g.p_hi_s, 1)

                def pair(i, st=st, last=False):
                    for q in range(6):
                        if st.kind == "ple":
                            act.wait_ge(g.free, i * 12 + st.chunk + 2 * q + 1)
                            act.activation(g.sig[:, q % 2, :], g.tmp[:, q % 2, :], ACT.Sigmoid).then_inc(g.sig_s, 1)
                            act.wait_ge(g.px_s, i * 6 + q + 1)
                        if st.gain is not None:
                            act.wait_ge(g.free, i * 6 + st.chunk + q + 1)
                        if st.gain is not None or st.kind == "ple":
                            if not (st is steps[1] and first(i) and q == 0):
                                act.wait_ge(g.acc_s, i * 6 + st.square + q)
                            act.activation(g.sq[:, :].unsqueeze(1), chunk_of(g.x, i, q), ACT.Square).then_inc(g.sq_s, 1)
                        if st.out:
                            act.wait_ge(g.hg_s, i * 6 + st.part + q + 1)
                            act.activation(chunk_of(st.out[0], i, q), g.hg[:, q % 2:q % 2 + 1, :], ACT.Copy).then_inc(g.hi_s, 1)
                        if st.kind == "merge" and not (last and q >= 4):
                            load_gates(act, g, i + (q + 2) // 6, (q + 2) % 6, i * 6 + q + 1)
                if st.kind == "merge":
                    pair(0)
                    with act.Fori(1, KD // 2 - 1) as i:
                        pair(i)
                    pair(KD // 2 - 1, last=True)
                elif st.out or st.kind == "ple":
                    in_pairs(act, KD, pair, peel=st is steps[1])
            act.wait_ge(g.root_s, 3)
            for t in range(NT):
                r = ROWS[t]
                act.wait_ge(g.y_full, t + 1)
                if t >= 3:
                    act.wait_ge(y_out[t % 3], 16 * (t // 3))
                act.activation(g.y[:r, t % 3, :], g.bank[:r, 2 * (t % 3):2 * (t % 3) + 2, :].rearrange("p a b -> p (a b)"),
                               ACT.Copy, scale=g.root[:r, t:t + 1]).then_inc(g.y_got, 1)


def chunk_of(x, i, q):
    c = q % 3
    return x[:, bass.ds(i * 2 + q // 3, 1), c * CH:(c + 1) * CH]


def split_weights(pool, g, j, n):
    one = g.ones[:, 0:1].unsqueeze(2).to_broadcast([P, KD, P])
    pool.tensor_tensor(g.wu_hi[:, j], g.w_stage[:, j], one, ALU.mult).then_inc(g.w_hi, 1)
    pool.wait_ge(g.w_hi, n)
    pool.tensor_tensor(g.wu_lo[:, j], g.w_stage[:, j], g.wu_hi[:, j].bitcast(F32), ALU.subtract).then_inc(g.w_split, 1)


def low_parts(pool, g, st, i, j):
    if not st.out:
        return
    for c in range(NCH):
        q = 3 * j + c
        pool.wait_ge(g.hi_s, i * 6 + st.part + q + 1)
        pool.tensor_tensor(chunk_of(st.out[1], i, q), g.hg[:, q % 2:q % 2 + 1, :], chunk_of(st.out[0], i, q).bitcast(F32),
                           ALU.subtract).then_inc(g.lo_s, 1)


def load_gates(act, g, i, q, free=None):
    if free is not None:
        act.wait_ge(g.hg_s, free)
    c = q % 3
    src = g.gate_d.rearrange("a k p t -> k p a t")[bass.ds(i * 2 + q // 3, 1), :, :, c * CH:(c + 1) * CH]
    act.dma_start(g.gate_in_sb[:, q % 2], src.rearrange("k p a t -> p (k a) t")).then_inc(g.gates_in[q % 2], 16)


def take_merge(dve, g, st, i):
    for q in range(6):
        dve.wait_ge(g.gates_in[q % 2], (i * 3 + q // 2 + 1) * 16)
        for half in range(2):
            n = 2 * q + half
            dve.wait_ge(g.full, i * 12 + st.chunk + n + 1)
            if half == 0 and not (first(i) and q == 0):
                dve.wait_ge(g.hg_s, i * 6 + q)
            dve.tensor_tensor(g.tmp[:, half, :], g.bank[:, n % 6, :CH], g.gate_in_sb[:, q % 2, half, :], ALU.mult).then_inc(g.free, 1)
        dve.wait_ge(g.free, i * 12 + st.chunk + 2 * q + 2)
        if not (first(i) and q < 2):
            dve.wait_ge(g.lo_s, i * 6 + st.part + q - 1)
        dve.tensor_tensor(g.hg[:, q % 2, :], g.tmp[:, 0, :], g.tmp[:, 1, :], ALU.add).then_inc(g.hg_s, 1)


def take_residual(dve, g, st, i):
    for q in range(6):
        x = chunk_of(g.x, i, q)
        dve.wait_ge(g.full, i * 6 + st.chunk + q + 1)
        dve.tensor_tensor(x, g.bank[:, q:q + 1, :CH], x, ALU.add).then_inc(g.free, 1)
        if st.gain is not None:
            dve.wait_ge(g.free, i * 6 + st.chunk + q + 1)
            dve.wait_ge(g.lo_s, i * 6 + st.part + q - 1)
            dve.tensor_scalar(g.hg[:, q % 2:q % 2 + 1, :], x, g.gains[:, st.gain, bass.ds(i * 2 + q // 3, 1)], None,
                              ALU.mult).then_inc(g.hg_s, 1)
            add_square(dve, g, g.rstd_bc, q % 3, i * 6 + st.square + q + 1)


def take_up(dve, g, st, i):
    for q in range(6):
        c = q % 3
        dve.wait_ge(g.full, i * 6 + st.chunk + q + 1)
        dve.tensor_tensor(g.tmp[:, q % 2, :], g.bank[:, q, :CH], g.rstd_bc[:, c * CH:(c + 1) * CH], ALU.mult).then_inc(g.free, 1)
        dve.wait_ge(g.free, i * 6 + st.chunk + q + 1)
        dve.wait_ge(g.lo_s, i * 6 + st.part + q - 1)
        dve.scalar_tensor_tensor(g.hg[:, q % 2, :], g.tmp[:, q % 2, :], 0.0, g.tmp[:, q % 2, :], ALU.max, ALU.mult).then_inc(g.hg_s, 1)


def take_embedding(dve, g, st, i):
    for q in range(6):
        c = q % 3
        x = chunk_of(g.x, i, q)
        dve.wait_ge(g.full, i * 12 + st.chunk + 2 * q + 1)
        dve.tensor_tensor(g.tmp[:, q % 2, :], g.bank[:, 2 * c, :CH], g.rstd_bc[:, c * CH:(c + 1) * CH], ALU.mult).then_inc(g.free, 1)
        dve.wait_ge(g.full, i * 12 + st.chunk + 2 * q + 2)
        dve.wait_ge(g.sig_s, i * 6 + q + 1)
        dve.tensor_tensor(g.hg[:, q % 2, :], g.bank[:, 2 * c + 1, :CH], g.sig[:, q % 2, :], ALU.mult).then_inc(g.free, 1)
        dve.wait_ge(g.free, i * 12 + st.chunk + 2 * q + 2)
        dve.tensor_tensor(x, x, g.hg[:, q % 2:q % 2 + 1, :], ALU.add).then_inc(g.px_s, 1)
        add_square(dve, g, g.total, c, i * 6 + st.square + q + 1)
        dve.tensor_scalar(x, x, g.gains[:, 3, bass.ds(i * 2 + q // 3, 1)], None, ALU.mult).then_inc(g.pdone_s, 1)


def add_square(dve, g, total, c, at):
    dve.wait_ge(g.sq_s, at)
    cols = slice(c * CH, (c + 1) * CH)
    dve.tensor_tensor(total[:, cols], total[:, cols], g.sq[:, :], ALU.add).then_inc(g.acc_s, 1)


def embed_unit(pe, g, st, m, factors):
    pe.wait_ge(g.w_split, st.unit + m + 1)
    for c in range(NCH):
        n = 6 * m + 2 * c
        if m == 0:
            pe.wait_ge(g.lo_s, st.part - 2 + c)
        pe.wait_ge(g.free, st.chunk + n - 5)
        multiply_chunk(pe, g, 2 * c, m % 2, c, [(k, k) for k in range(KD)], *st.act)
        if m == 0:
            factor_products(pe, g, factors.index(st), [(0, 0), (0, 2), (0, 4)], (0, 2 * c))
        if n == 0:
            pe.wait_ge(g.p_lo_s, 2)
        pe.wait_ge(g.free, st.chunk + n - 4)
        out = g.bank[:, 2 * c + 1, :CH]
        for k in range(2):
            w, v = g.wp_hi[:, k, m * P:(m + 1) * P], g.wp_lo[:, k, m * P:(m + 1) * P]
            a, b = g.p_hi[:, k, c * CH:(c + 1) * CH], g.p_lo[:, k, c * CH:(c + 1) * CH]
            pe.matmul(out, w, a, start=k == 0, stop=False)
            pe.matmul(out, w, b, start=False, stop=False)
            last = pe.matmul(out, v, a, start=False, stop=k == 1)
        last.then_inc(g.full, 1)


def factor_products(pe, g, n, places, at):
    if at == places[0]:
        pe.wait_ge(g.acc_s, NCH * KD * (n + 1))
        sum_features(pe, g, g.rstd_bc)
    elif at == places[1]:
        pe.wait_ge(g.diag_s, n + 1)
        for b in range(2):
            for t in range(4):
                last = pe.matmul(g.bank[:, 6 + b, t * P:(t + 1) * P], g.ones[:, :], g.diag[:, 4 * b + t, :], start=True, stop=True)
            last.then_inc(g.bc_s, 1)
    elif at == places[2]:
        pe.wait_ge(g.bc_got, 3 * n + 1)
        pe.matmul(g.bank[:, 6, :NS], g.ones[:NS, :], g.diag[:NS, NT - 1, :NS], start=True, stop=True).then_inc(g.bc_s, 1)


def sum_features(pe, g, total):
    for t in range(NT):
        last = pe.matmul(g.bank[:ROWS[t], 7, t:t + 1], total[:, t * P:t * P + ROWS[t]], g.ones[:, 0:1], start=True, stop=True)
    last.then_inc(g.sum_s, 1)


def copy_sums(dve, g, n):
    dve.wait_ge(g.stat_s, 2 * n - 1)
    dve.wait_ge(g.sum_s, n)
    dve.tensor_copy(g.stat[:, :NT - 1], g.bank[:, 7, :NT - 1])
    dve.tensor_copy(g.stat[:NS, NT - 1:], g.bank[:NS, 7, NT - 1:NT]).then_inc(g.stat_s, 1)


def spread_factors(dve, g, n):
    dve.memset(g.stat[:, :], float(D)).then_inc(g.stat_s, 1)
    copy_sums(dve, g, n + 1)
    dve.wait_ge(g.root_s, n + 1)
    shape = [P, NT, P]
    dve.tensor_tensor(g.diag[:, :, :], g.ident[:, :].unsqueeze(1).to_broadcast(shape),
                      g.stat[:, :].unsqueeze(2).to_broadcast(shape), ALU.mult).then_inc(g.diag_s, 1)
    for b, (bank, a, z) in enumerate(((6, 0, 512), (7, 512, 1024), (6, 1024, T))):
        dve.wait_ge(g.bc_s, 3 * n + b + 1)
        dve.tensor_copy(g.rstd_bc[:, a:z], g.bank[:, bank, :z - a]).then_inc(g.bc_got, 1)
    dve.wait_ge(g.bc_got, 3 * n + 3)


def write_products(pe, g):
    pe.wait_ge(g.acc_s, g.squares)
    sum_features(pe, g, g.total)
    pe.wait_ge(g.pdone_s, NCH * KD)
    pe.wait_ge(g.free, g.chunks)
    for t in range(NT):
        r = ROWS[t]
        if t >= 3:
            pe.wait_ge(g.y_got, t - 2)
        for k in range(KD):
            last = pe.transpose(g.bank[:r, 2 * (t % 3) + k // 4, (k % 4) * P:(k % 4 + 1) * P], g.x[:, k, t * P:t * P + r], g.ident[:, :])
        last.then_inc(g.y_full, 1)


_INS = ["x_prompt", "x_sample", "cache_win_k", "cache_win_v", "cache_ckv", "cache_kpe", "page_table", "p_prompt",
        "p_sample", "g_mix", "w_in", "g_q", "w_uq", "g_kv", "w_uk", "w_uv", "w_oa", "w_ob", "w_o", "g_ffn", "w_up",
        "w_down", "g_ple", "w_ple_gate", "w_ple", "g_final"]
_OUTS = {
    "y_prompt": (1, SEQ, D), "y_sample": (NSEQ, TDEC, D),
    "win_k_prompt": (1, 1, SEQ, H, E), "win_v_prompt": (1, 1, SEQ, H, E),
    "ckv_prompt": (1, 1, SEQ, KL), "kpe_prompt": (1, 1, SEQ, RD),
    "win_k_sample": (1, NSEQ, PAST + TDEC, H, E), "win_v_sample": (1, NSEQ, PAST + TDEC, H, E),
    "ckv_sample": (1, NSEQ, TDEC, KL), "kpe_sample": (1, NSEQ, TDEC, RD),
}


def _log_count(dist):
    count = sum(((dist >= 0) & (dist <= w) & (dist % d == 0)).astype(np.float32) for w, d in PATTERNS)
    return np.where(count > 0, np.log(np.maximum(count, 1)), NEG).astype(np.float32)


def _constants():
    pos = np.concatenate([np.arange(SEQ), np.tile(PAST + np.arange(TDEC), NSEQ), np.zeros(P - NS)]).astype(np.float32)
    out = {"ident_c": np.eye(P, dtype=np.float32)}
    for tag, rot in (("a", E // 4), ("b", RD)):
        half = rot // 2
        inv = np.float32(500000.0) ** (-np.arange(half, dtype=np.float32) * np.float32(2.0 / rot))
        ang = (pos[:, None] * inv[None, :].astype(np.float32)).astype(np.float32)
        for fn, name in ((np.cos, "cos"), (np.sin, "sin")):
            out[f"{name}_{tag}_c"] = np.ascontiguousarray(fn(ang).astype(np.float32).reshape(NT, P, half).transpose(1, 0, 2))
    q, k = np.arange(P)[:, None, None], np.arange(P)[None, None, :]
    dist = (NT - 2 - np.arange(NT - 1))[None, :, None] * P + q - k
    out["mask_w_c"] = _log_count(dist)
    out["mask_b_c"] = np.where(dist >= 0, 0.0, NEG).astype(np.float32)
    far = np.array([16 * m + r for r in range(4) for m in range(32)])
    keys = np.concatenate([far, np.arange(PAST // 2, PAST + TDEC)])
    t = np.tile(np.arange(TDEC), H)[:, None]
    out["mask_ws_c"] = _log_count(PAST + t - keys[None, :])
    out["mask_ls_c"] = np.where(np.arange(PAST + TDEC)[None, :] <= PAST + t, 0.0, NEG).astype(np.float32)
    return out


def kernel(**inputs):
    import concourse.bacc as _bacc
    from concourse.bass_utils import run_bass_kernel_spmd as _run

    nc = _bacc.Bacc("TRN2", target_bir_lowering=False, num_devices=1)
    arrays, io = {}, {}
    for name, a in [(n, np.asarray(inputs[n])) for n in _INS] + list(_constants().items()):
        a = np.ascontiguousarray(a)
        arrays[f"in_{name}"] = a
        io[name] = nc.dram_tensor(f"in_{name}", a.shape, mybir.dt.from_np(a.dtype), kind="ExternalInput").ap()
    for name, shape in _OUTS.items():
        io[name] = nc.dram_tensor(f"out_{name}", shape, F32, kind="ExternalOutput").ap()
    build(nc, io)
    r = _run(nc, [arrays], core_ids=[0])
    return tuple(r.results[0][f"out_{name}"] for name in _OUTS)
```

```python
from contextlib import ExitStack

import numpy as np

import concourse.bass as bass
from concourse import mybir

F32 = mybir.dt.float32
F32R = mybir.dt.float32r
I32 = mybir.dt.int32
ALU = mybir.AluOpType
ACT = mybir.ActivationFunctionType

P = 128
D = 1024
SEQ = 1024
NSEQ, TDEC = 8, 4
NS = NSEQ * TDEC
T = SEQ + NS
NT = SEQ // P + 1
ROWS = [P] * (NT - 1) + [NS]
NCH = 3
CH = T // NCH
KD = D // P
H = 8
E = 64
PATTERNS = ((128, 1), (512, 4), (2048, 16))
QL, KL, RD = 384, 256, 32
BH = E + RD
FF = 4 * D
NF = FF // D
PLE = 256
PAST, PAGE = 1024, 128
NPAGE = PAST // PAGE
NPHYS = (5 * NSEQ * NPAGE + 3) // 4
SK = 5
EPS = 1e-6
NEG = -1e30
FLOOR = -3e38
LATENT_COL = 3 * H * E
GATE_COL = LATENT_COL + QL + KL + RD
BLK_COLS = [(LATENT_COL, QL), (LATENT_COL + QL, KL + RD)] + [(n * H * E, H * E) for n in range(3)]

BYTES = 4
BASE = 16512
R1 = BASE + 7168
R2 = R1 + 2 * KD * T * BYTES
RW = R2 + 2 * KD * T * BYTES
RX = RW + 6 * KD * P * BYTES
RM = RX + KD * T * BYTES
TOP = 229368
R_CQ = (TOP - NT * (QL + KL + RD) * BYTES) // 32 * 32 - 64


class Room:

    def __init__(self, nc, start, end=TOP):
        self.nc, self.next, self.end = nc, start, end

    def __call__(self, name, shape, dt=F32):
        size = -(-int(np.prod(shape[1:])) * BYTES // 32) * 32
        assert self.next + size <= self.end, (name, self.next + size, self.end)
        made = self.nc.alloc_sbuf_tensor_at(name, list(shape), dt, offset=self.next)
        self.next += size
        return made


class Program:

    def __init__(self, nc, io):
        self.nc = nc
        self.x_prompt = io["x_prompt"]
        self.x_sample = io["x_sample"]
        self.cache_win_k = io["cache_win_k"]
        self.cache_win_v = io["cache_win_v"]
        self.cache_ckv = io["cache_ckv"]
        self.cache_kpe = io["cache_kpe"]
        self.page_table = io["page_table"]
        self.p_prompt = io["p_prompt"]
        self.p_sample = io["p_sample"]
        self.g_mix = io["g_mix"]
        self.w_in = io["w_in"]
        self.g_q = io["g_q"]
        self.w_uq = io["w_uq"]
        self.g_kv = io["g_kv"]
        self.w_uk = io["w_uk"]
        self.w_uv = io["w_uv"]
        self.w_oa = io["w_oa"]
        self.w_ob = io["w_ob"]
        self.w_o = io["w_o"]
        self.g_ffn = io["g_ffn"]
        self.w_up = io["w_up"]
        self.w_down = io["w_down"]
        self.g_ple = io["g_ple"]
        self.w_ple_gate = io["w_ple_gate"]
        self.w_ple = io["w_ple"]
        self.g_final = io["g_final"]
        self.ident_c = io["ident_c"]
        self.cos_a_c = io["cos_a_c"]
        self.sin_a_c = io["sin_a_c"]
        self.cos_b_c = io["cos_b_c"]
        self.sin_b_c = io["sin_b_c"]
        self.mask_w_c = io["mask_w_c"]
        self.mask_b_c = io["mask_b_c"]
        self.mask_ws_c = io["mask_ws_c"]
        self.mask_ls_c = io["mask_ls_c"]
        self.y_prompt = io["y_prompt"]
        self.y_sample = io["y_sample"]
        self.win_k_prompt = io["win_k_prompt"]
        self.win_v_prompt = io["win_v_prompt"]
        self.ckv_prompt = io["ckv_prompt"]
        self.kpe_prompt = io["kpe_prompt"]
        self.win_k_sample = io["win_k_sample"]
        self.win_v_sample = io["win_v_sample"]
        self.ckv_sample = io["ckv_sample"]
        self.kpe_sample = io["kpe_sample"]


def build(nc, io):
    with ExitStack() as ctx:
        g = Program(nc, io)
        g.stage_sems = []

        def sem(name):
            g.stage_sems.append(nc.alloc_semaphore(name=name))
            return g.stage_sems[-1]

        g.sem = sem
        g.bank = ctx.enter_context(nc.psum_tensor("bank", [P, 8, 512], F32))
        dram = lambda name, shape: nc.dram_tensor(name, shape, F32, kind="Internal").ap()
        g.xt_d = dram("xt_d", (P, KD, T))
        g.p_t_d = dram("p_t_d", (P, 2, T))
        g.gate_d = dram("gate_d", (2, KD, P, T))
        g.q_d = dram("q_d", (T, H * E))
        g.k_d = dram("k_d", (T, H * E))
        g.v_d = dram("v_d", (T, H * E))
        room = Room(nc, BASE, R1)
        g.ident = room("ident", [P, P])
        g.ones = room("ones", [P, P])
        g.nhalf = room("nhalf", [P, 1])
        g.gains = room("gains", [P, 4, KD])
        g.rstd_bc = room("rstd_bc", [P, T])
        g.rstd = room("rstd", [P, NT])
        g.rstd8 = room("rstd8", [P, NT])
        g.sq = room("tail_square", [P, CH])
        g.root = room("lat_root", [P, 2, NT])
        g.w_loaded = [ctx.enter_context(nc.semaphore(f"w_loaded{j}")) for j in range(2)]
        g.w_hi, g.w_split, g.full, g.free = (
            ctx.enter_context(nc.semaphore(n)) for n in ("w_hi", "w_split", "full", "free"))
        g.copied = ctx.enter_context(nc.semaphore("copied"))
        g.units = g.chunks = g.turns = 0
        room = Room(nc, R1, R2)
        g.h_hi = room("h_hi", [P, KD, T], F32R)
        g.h_lo = room("h_lo", [P, KD, T], F32R)
        room = Room(nc, R_CQ)
        g.cq = room("cq", [P, NT, QL])
        g.ckv_at = room.next
        g.ckv = room("ckv", [P, NT, KL + RD])
        room = Room(nc, R2)
        g.qb_t = room("qb_t", [BH, H, T])
        g.kb_t = room("kb_t", [BH, H, SEQ])
        g.vb = room("vb", [P, NT - 1, H * E])
        g.room_kept = room.next
        g.w_uv_sb = room("w_uv_sb", [P, 2, H * E])
        g.ckv_t = room("ckv_t", [P, 2, T])
        g.kpe_t = room("kpe_t", [RD, NS])
        g.ql_t = room("ql_t", [P, 2, NSEQ, H, TDEC])
        g.qpe_t = room("qpe_t", [RD, NSEQ, H, TDEC])
        g.room_b = room.next
        room = Room(nc, g.room_b, R_CQ)
        g.w_uq_sb = room("w_uq_sb", [P, 3, H * BH])
        g.w_uk_sb = room("w_uk_sb", [P, 2, H * E])
        g.cos_b_sb = room("cos_b_sb", [P, NT, 16])
        g.sin_b_sb = room("sin_b_sb", [P, NT, 16])
        g.g_q_sb = room("g_q_sb", [P, 3])
        g.l_in = g.sem("l_in")
        project_natural(g)
        project_gates(g)
        room = Room(nc, R1, R2)
        g.o_hi = room("o_hi", [P, KD, T], F32R)
        g.o_lo = room("o_lo", [P, KD, T], F32R)
        g.latent_mask = Room(nc, Ahead.start_of("latent") - SEQ * BYTES)("latent_mask", [P, NT - 1, P])
        project_latents(g)
        renew_semaphores(g)
        g.win_nat = Room(nc, g.room_b)("win_nat", [P, 3, NT - 1, H * E // 2])
        g.wqk_in = [g.sem(f"wqk_in{m}") for m in range(4)]
        g.wt_full = g.sem("wt_full")
        g.wt_got = [g.sem(f"wt_got{odd}") for odd in range(2)]
        for kind in ("latent", "window"):
            ahead = Ahead(g, kind)
            attend_prompt(g, kind, ahead)
            attend_sample(g, kind, ahead)
        renew_semaphores(g)
        run_tail(g)
        nc.clear_and_free_semaphores(g.stage_sems)


def renew_semaphores(g):
    g.nc.clear_and_free_semaphores(g.stage_sems)
    g.stage_sems.clear()
    g.nc.all_engine_barrier()


def inverse_root(pool, g, out, total, scale, scaled, at, done):
    pool.tensor_scalar(out, total, scale, EPS, ALU.mult, ALU.add).then_inc(scaled, 1)
    pool.wait_ge(scaled, at)
    half = g.nhalf[:out.shape[0], :].to_broadcast(list(out.shape))
    pool.tensor_tensor(out, out, half, ALU.pow).then_inc(done, 1)


def project_natural(g):
    nc = g.nc
    room = Room(nc, R2, R_CQ)
    g.gate_stage_at = room.next
    w_st = room("wn_st", [P, KD, 512])
    g.gate_split_at = room.next + KD * 512 * BYTES
    w_hi = room("wn_hi", [P, 2, KD, 512], F32R)
    w_lo = room("wn_lo", [P, 2, KD, 512], F32R)
    early = Room(nc, room.next)
    nat = early("nat", [P, 3, 512])
    room_after_nat = early.next
    x_nat = room("x_nat", [P, 3, D])
    x_nat_end = room.next
    x_t = room("x_t", [P, 2, KD, P])
    hg = room("hg", [P, 2, KD // 2, P])
    p_nat = room("p_nat", [P, 2, PLE])
    p_t = room("p_t", [P, 2, 2, P])
    diag = room("diag", [P, 2, P])
    gain_nat = room("gain_nat", [4 * KD, P])
    stat = room("stat", [P, NT])
    ra = room("rope_a", [P, 2, H, 8])
    rb = room("rope_b", [P, 2, H, 8])
    cos_a = room("cos_a", [P, NT, 8])
    sin_a = room("sin_a", [P, NT, 8])
    square = Room(nc, g.ckv_at)("square", [P, D])
    room = Room(nc, room_after_nat, x_nat_end)
    lat_square = room("lat_square", [P, QL])
    g_kv = room("g_kv_sb", [P, KL])
    cos_b = room("cos_b", [P, NT, 16])
    sin_b = room("sin_b", [P, NT, 16])
    la = room("lat_ra", [P, 2, 1, 16])
    lb = room("lat_rb", [P, 2, 1, 16])
    lat_stat = room("lat_stat", [P, 2, NT])
    squared, scaled, rooted, normed, turned, l_step, lat_out, lat_tabs, l_set = map(g.sem, (
        "l_squared", "l_scaled", "l_rooted", "l_normed", "l_turned", "l_step", "l_out", "l_tabs", "l_set"))
    (consts, x_squared, tr, t_copied, hg_ready, hi_done, lo_done, stat_ready, rstd_ready, diag_ready, bc_full,
     bc_got, gain_in, gain_t, set_up, got_gain, p_full, p_got, rstd8_set) = map(g.sem, (
         "consts", "x_squared", "tr", "t_copied", "hg_ready", "hi_done", "lo_done", "stat_ready", "rstd_ready",
         "diag_ready", "bc_full", "bc_got", "gain_in", "gain_t", "set_up", "got_gain", "p_full", "p_got", "rstd8_set"))
    x_in = [g.sem(f"x_in{j}") for j in range(3)]
    x_out = [g.sem(f"x_out{j}") for j in range(2)]
    p_in = [g.sem(f"p_in{j}") for j in range(2)]
    p_out = [g.sem(f"p_out{j}") for j in range(2)]
    wn_in, wn_hi, wn_lo, n_full, n_got, roped, tabs, ra_s = map(
        g.sem, ("wn_in", "wn_hi", "wn_lo", "n_full", "n_got", "roped", "tabs", "ra_s"))
    nat_out = [g.sem(f"nat_out{j}") for j in range(3)]
    g.w_stage = Room(nc, g.gate_stage_at)("w_stage_gates", [P, 2, KD, P])
    split_room(g, Room(nc, g.gate_split_at), "gates")
    gates = g.w_in[0].rearrange("(k p) c -> p k c", p=P)
    dest = {2: (g.q_d, None), 3: (g.k_d, g.win_k_prompt), 4: (g.v_d, g.win_v_prompt)}
    steps = [(b, t) for b in range(5) for t in range(NT)]
    stored = [s for s in steps if s[0] >= 2]

    def written(m, place):
        return 16 * sum(1 if stored[n][0] == 2 else 2 for n in range(place, m, 3))

    def low_block(eng, b):
        n = BLK_COLS[b][1]
        eng.tensor_tensor(w_lo[:, b % 2, :, :n], w_st[:, :, :n], w_hi[:, b % 2, :, :n].bitcast(F32),
                          ALU.subtract).then_inc(wn_lo, 1)

    with nc.Block() as block:

        @block.sync
        def _(sp):
            def load_x(t):
                if t >= 3:
                    sp.wait_ge(tr, 2 * (t - 2))
                    sp.wait_ge(x_squared, t - 2)
                src = g.x_prompt[0, t * P:(t + 1) * P, :] if t < NT - 1 else g.x_sample.rearrange("n t d -> (n t) d")
                sp.dma_start(x_nat[:ROWS[t], t % 3, :], src).then_inc(x_in[t % 3], 16)

            def load_p(t):
                if t >= 2:
                    sp.wait_ge(p_full, t - 1)
                src = g.p_prompt[0, 0, t * P:(t + 1) * P, :] if t < NT - 1 else g.p_sample[0].rearrange("s t c -> (s t) c")
                sp.dma_start(p_nat[:ROWS[t], t % 2, :], src).then_inc(p_in[t % 2], 16)

            def load_block(b):
                c0, n = BLK_COLS[b]
                if b >= 1:
                    sp.wait_ge(wn_lo, b)
                sp.dma_start(w_st[:, :, :n], g.w_in[0, :, c0:c0 + n].rearrange("(k p) n -> p k n", p=P)).then_inc(wn_in, 16)

            load_x(0)
            sp.dma_start(g.ident[:, :], g.ident_c).then_inc(consts, 16)
            for n, gain in enumerate((g.g_mix, g.g_ffn, g.g_ple, g.g_final)):
                row = gain if n == 3 else gain[0, :]
                sp.dma_start(gain_nat[n * KD:(n + 1) * KD, :], row.rearrange("(k p) -> k p", p=P)).then_inc(gain_in, 16)
            load_x(1)
            load_block(0)
            load_x(2)
            for tab, src in ((cos_a, g.cos_a_c), (sin_a, g.sin_a_c)):
                sp.dma_start(tab[:, :, :], src).then_inc(tabs, 16)
            for t in range(NT):
                sp.wait_ge(t_copied, 2 * t + 2)
                toks = slice(t * P, t * P + ROWS[t])
                sp.dma_start(g.xt_d[:, :, toks], x_t[:, t % 2, :, :ROWS[t]]).then_inc(x_out[t % 2], 16)
                if t + 3 < NT:
                    load_x(t + 3)
                if t == 3:
                    load_block(1)
            load_p(0)
            load_p(1)
            sp.wait_ge(tr, 2 * NT)
            sp.wait_ge(x_squared, NT)
            for tab, src in ((cos_b, g.cos_b_c), (sin_b, g.sin_b_c)):
                sp.dma_start(tab[:, :, :], src).then_inc(lat_tabs, 16)
            sp.dma_start(g_kv[:, :], g.g_kv[0:1, :].to_broadcast([P, KL])).then_inc(lat_tabs, 16)
            for t in range(NT):
                sp.wait_ge(p_got, t + 1)
                toks = slice(t * P, t * P + ROWS[t])
                sp.dma_start(g.p_t_d[:, :, toks], p_t[:, t % 2, :, :ROWS[t]]).then_inc(p_out[t % 2], 16)
                if t + 2 < NT:
                    load_p(t + 2)
                if t == 0:
                    load_block(2)
            load_block(3)
            load_block(4)
            sp.wait_ge(wn_lo, 5)
            for j in range(2):
                sp.dma_start(g.w_stage[:, j], gates[:, :, GATE_COL + j * P:GATE_COL + (j + 1) * P]).then_inc(g.w_loaded[j], 16)
            for t in range(NT):
                r = ROWS[t]
                sp.wait_ge(normed, t + 1)
                sp.wait_ge(turned, t + 1)
                for out, new, part in ((g.ckv_prompt, g.ckv_sample, slice(0, KL)), (g.kpe_prompt, g.kpe_sample, slice(KL, KL + RD))):
                    dst = out[0, 0, t * P:(t + 1) * P, :] if t < NT - 1 else new[0].rearrange("n t c -> (n t) c")
                    sp.dma_start(dst, g.ckv[:r, t, part]).then_inc(lat_out, 16)
            sp.wait_ge(lat_out, 32 * NT)
            for j in range(2):
                sp.wait_ge(x_out[j], 16 * len(range(j, NT, 2)))
                sp.wait_ge(p_out[j], 16 * len(range(j, NT, 2)))

        @block.gpsimd
        def _(pool):
            for n in range(2 * NT):
                t, half = divmod(n, 2)
                pool.wait_ge(hi_done, n + 1)
                where = (slice(None), slice(4 * half, 4 * half + 4), slice(t * P, t * P + ROWS[t]))
                pool.tensor_tensor(g.h_lo[where], hg[:, n % 2, :, :ROWS[t]], g.h_hi[where].bitcast(F32),
                                   ALU.subtract).then_inc(lo_done, 1)
                if n % 6 == 5:
                    pool.wait_ge(x_squared, t + 1)
                    inverse_root(pool, g, g.rstd[:, t - 2:t + 1], stat[:, t - 2:t + 1], 1.0 / D, stat_ready, t // 3 + 1, rstd_ready)
            for b in range(1, 5):
                pool.wait_ge(wn_hi, b + 1)
                low_block(pool, b)
                if b == 3:
                    pool.wait_ge(squared, 2 * NT)
                    inverse_root(pool, g, g.root[:, 0, :], lat_stat[:, 0, :], 1.0 / QL, scaled, 1, rooted)
                    inverse_root(pool, g, g.root[:, 1, :], lat_stat[:, 1, :], 1.0 / KL, scaled, 2, rooted)
            pool.wait_ge(n_full, 4 * NT)
            for j in range(2):
                pool.wait_ge(g.w_loaded[j], 16)
                split_weights(pool, g, j, j + 1)

        @block.tensor
        def _(pe):
            def turn_x(t):
                pe.wait_ge(x_in[t % 3], 16 * (t // 3 + 1))
                for half in range(2):
                    n = 2 * t + half
                    if n >= 2:
                        pe.wait_ge(t_copied, n - 1)
                    for k in range(4):
                        at = (4 * half + k) * P
                        last = pe.transpose(g.bank[:, 4 + n % 2, k * P:k * P + ROWS[t]],
                                            x_nat[:ROWS[t], t % 3, at:at + P], g.ident[:ROWS[t], :ROWS[t]])
                    last.then_inc(tr, 1)

            def product(s):
                b, t = steps[s]
                n = BLK_COLS[b][1]
                if t == 0:
                    pe.wait_ge(wn_lo, b + 1)
                if b == 0:
                    pe.wait_ge(lo_done, 2 * t + 2)
                if s >= 4:
                    pe.wait_ge(n_got, s - 3)
                toks = slice(t * P, t * P + ROWS[t])
                out = g.bank[:ROWS[t], s % 4, :n]
                for k in range(KD):
                    a, c = g.h_hi[:, k, toks], g.h_lo[:, k, toks]
                    w, v = w_hi[:, b % 2, k, :n], w_lo[:, b % 2, k, :n]
                    pe.matmul(out, a, w, start=k == 0, stop=False)
                    pe.matmul(out, a, v, start=False, stop=False)
                    last = pe.matmul(out, c, w, start=False, stop=k == KD - 1)
                last.then_inc(n_full, 1)

            pe.wait_ge(consts, 16)
            pe.wait_ge(gain_in, 64)
            pe.transpose(g.bank[:, 7, 0:4 * KD], gain_nat[:, :], g.ident[:4 * KD, :4 * KD]).then_inc(gain_t, 1)
            turn_x(0)
            turn_x(1)
            for t in range(NT):
                if t + 2 < NT:
                    turn_x(t + 2)
                product(t)
            for t in range(NT):
                r = ROWS[t]
                product(NT + t)
                pe.wait_ge(diag_ready, t + 1)
                if t == 0:
                    pe.wait_ge(got_gain, 1)
                if t >= 6:
                    pe.wait_ge(bc_got, 1)
                pe.matmul(g.bank[:, 6 + t // 3 % 2, (t % 3) * P:(t % 3) * P + r], g.ones[:r, :],
                          diag[:r, t % 2, :r], start=True, stop=True).then_inc(bc_full, 1)
                pe.wait_ge(p_in[t % 2], 16 * (t // 2 + 1))
                if t >= 2:
                    pe.wait_ge(p_got, t - 1)
                for k in range(2):
                    last = pe.transpose(g.bank[:, 4 + t % 2, k * P:k * P + r], p_nat[:r, t % 2, k * P:(k + 1) * P], g.ident[:r, :r])
                last.then_inc(p_full, 1)
            for s in range(2 * NT, 5 * NT):
                product(s)

        @block.scalar
        def _(act):
            def high_block(b):
                n = BLK_COLS[b][1]
                act.wait_ge(wn_in, 16 * (b + 1))
                if b >= 2:
                    act.wait_ge(n_full, NT * (b - 1))
                act.activation(w_hi[:, b % 2, :, :n], w_st[:, :, :n], ACT.Copy).then_inc(wn_hi, 1)

            def take(s):
                b, t = steps[s]
                r, n = ROWS[t], BLK_COLS[b][1]
                act.wait_ge(n_full, s + 1)
                if b == 0 and t % 3 == 0:
                    act.wait_ge(rstd_ready, t // 3 + 1)
                if s == NT:
                    act.wait_ge(x_squared, NT)
                if s == 2 * NT:
                    act.wait_ge(rstd8_set, 1)
                m = s - 2 * NT
                if b < 2:
                    out = (g.cq, g.ckv)[b][:r, t, :]
                else:
                    if m >= 3:
                        act.wait_ge(nat_out[m % 3], written(m, m % 3))
                    out = nat[:r, m % 3, :]
                factor = g.rstd8 if b == 2 else g.rstd
                act.activation(out, g.bank[:r, s % 4, :n], ACT.Copy, scale=factor[:r, t:t + 1]).then_inc(n_got, 1)
                if b >= 2:
                    if b < 4:
                        act.wait_ge(roped, m + 1)
                    else:
                        act.wait_ge(n_got, s + 1)
                    scratch, result = dest[b]
                    act.dma_start(scratch[t * P:t * P + r, :], out).then_inc(nat_out[m % 3], 16)
                    if result is not None:
                        if t < NT - 1:
                            o = result[0, 0, t * P:t * P + r, :, :].rearrange("s h e -> s (h e)")
                        else:
                            new = g.win_k_sample if b == 3 else g.win_v_sample
                            o = new[0, :, PAST:PAST + TDEC, :, :].rearrange("n s h e -> n s (h e)")
                        act.dma_start(o, out).then_inc(nat_out[m % 3], 16)

            act.wait_ge(set_up, 1)
            for t in range(NT):
                act.wait_ge(x_in[t % 3], 16 * (t // 3 + 1))
                if t >= 1:
                    act.wait_ge(x_squared, t)
                act.activation(square[:ROWS[t], :], x_nat[:ROWS[t], t % 3, :], ACT.Square,
                               accum_out=stat[:ROWS[t], t:t + 1]).then_inc(x_squared, 1)
                for half in range(2):
                    n = 2 * t + half
                    act.wait_ge(hg_ready, n + 1)
                    act.activation(g.h_hi[:, 4 * half:4 * half + 4, t * P:t * P + ROWS[t]], hg[:, n % 2, :, :ROWS[t]],
                                   ACT.Copy).then_inc(hi_done, 1)
                if t == 0:
                    high_block(0)
                if t >= 4:
                    take(t - 4)
            for s in range(NT - 4, 5 * NT):
                if s == NT - 3:
                    high_block(1)
                if s >= NT and s % NT == 4 and s // NT < 4:
                    high_block(s // NT + 1)
                take(s)
                if s == 2 * NT:
                    act.wait_ge(n_got, 2 * NT)
                    act.wait_ge(l_set, 1)
                if 2 * NT <= s < 3 * NT:
                    t = s - 2 * NT
                    for which, (x, w) in enumerate(((g.cq, QL), (g.ckv, KL))):
                        if t or which:
                            act.wait_ge(squared, 2 * t + which)
                        act.activation(lat_square[:ROWS[t], :w], x[:ROWS[t], t, :w], ACT.Square,
                                       accum_out=lat_stat[:ROWS[t], which, t:t + 1]).then_inc(squared, 1)
            for j in range(3):
                act.wait_ge(nat_out[j], written(len(stored), j))

        @block.vector
        def _(dve):
            dve.memset(g.ones[:, :], 1.0)
            dve.memset(g.nhalf[:, :], -0.5)
            dve.memset(stat[:, :], float(D)).then_inc(set_up, 1)
            dve.wait_ge(gain_t, 1)
            dve.tensor_copy(g.gains[:, :, :].rearrange("p a b -> p (a b)"), g.bank[:, 7, 0:4 * KD]).then_inc(got_gain, 1)
            dve.wait_ge(got_gain, 1)
            for t in range(NT):
                for half in range(2):
                    n = 2 * t + half
                    r = ROWS[t]
                    dve.wait_ge(tr, n + 1)
                    got = g.bank[:, 4 + n % 2, :].rearrange("p (k c) -> p k c", k=4)[:, :, :r]
                    ks = slice(4 * half, 4 * half + 4)
                    if n >= 2:
                        dve.wait_ge(lo_done, n - 1)
                    gain = g.gains[:, 0, ks].unsqueeze(2).to_broadcast([P, 4, r])
                    dve.tensor_tensor(hg[:, n % 2, :, :r], got, gain, ALU.mult).then_inc(hg_ready, 1)
                    if t >= 2:
                        dve.wait_ge(x_out[t % 2], 16 * (t // 2))
                    dve.tensor_copy(x_t[:, t % 2, ks, :r], got).then_inc(t_copied, 1)
                if t == 0:
                    dve.wait_ge(wn_hi, 1)
                    low_block(dve, 0)
            dve.wait_ge(rstd_ready, 3)
            dve.tensor_scalar(g.rstd8[:, :], g.rstd[:, :], E ** -0.5, None, ALU.mult).then_inc(rstd8_set, 1)
            for t in range(NT):
                r = ROWS[t]
                if t >= 2:
                    dve.wait_ge(bc_full, t - 1)
                dve.tensor_scalar(diag[:, t % 2, :], g.ident[:, :], g.rstd[:, t:t + 1], None, ALU.mult).then_inc(diag_ready, 1)
                if t % 3 == 2:
                    dve.wait_ge(bc_full, t + 1)
                    at, w = (t - 2) * P, 2 * P + r
                    dve.tensor_copy(g.rstd_bc[:, at:at + w], g.bank[:, 6 + t // 3 % 2, :w]).then_inc(bc_got, 1)
                dve.wait_ge(p_full, t + 1)
                if t >= 2:
                    dve.wait_ge(p_out[t % 2], 16 * (t // 2))
                dve.tensor_copy(p_t[:, t % 2, :, :r],
                                g.bank[:, 4 + t % 2, :2 * P].rearrange("p (k c) -> p k c", k=2)[:, :, :r]).then_inc(p_got, 1)
            dve.wait_ge(tabs, 32)
            dve.wait_ge(lat_tabs, 48)
            dve.memset(lat_stat[:, :, :], float(QL)).then_inc(l_set, 1)
            for m, (b, t) in enumerate(stored):
                if b == 4:
                    break
                r = ROWS[t]
                dve.wait_ge(n_got, 2 * NT + m + 1)
                rotate(dve, nat[:r, m % 3, :].rearrange("p (h e) -> p h e", e=E), 8,
                       cos_a[:r, t, :], sin_a[:r, t, :], ra[:r], rb[:r], H, ra_s, 2 * m, roped, m)
                if b == 2:
                    rotate(dve, g.ckv[:r, t, KL:].rearrange("p (h e) -> p h e", h=1), 16, cos_b[:r, t, :],
                           sin_b[:r, t, :], la[:r], lb[:r], 1, l_step, 2 * t, turned, t)
                else:
                    dve.wait_ge(rooted, 2)
                    dve.scalar_tensor_tensor(g.ckv[:r, t, :KL], g.ckv[:r, t, :KL], g.root[:r, 1, t:t + 1],
                                             g_kv[:r, :], ALU.mult, ALU.mult).then_inc(normed, 1)


def copy_cache(eng, g, cache, out, s, n):
    eng.dma_start(out[0, bass.ds(s, n), 0:PAST, :, :].rearrange("n s h e -> n s (h e)"),
                  cache[0, bass.ds(s, n)].rearrange("n s h e -> n s (h e)")).then_inc(g.copied, 16)


def rotate(dve, x, half, cos, sin, ra, rb, heads, step, at, done, turn):
    shape = [x.shape[0], heads, half]
    c, s = cos.unsqueeze(1).to_broadcast(shape), sin.unsqueeze(1).to_broadcast(shape)
    x1, x2 = x[:, :, 0:half], x[:, :, half:2 * half]
    if turn:
        dve.wait_ge(done, turn)
    dve.tensor_tensor(ra[:, 0], x1, c, ALU.mult)
    dve.tensor_tensor(ra[:, 1], x2, c, ALU.mult)
    dve.tensor_tensor(rb[:, 0], x2, s, ALU.mult)
    dve.tensor_tensor(rb[:, 1], x1, s, ALU.mult).then_inc(step, 1)
    dve.wait_ge(step, at + 1)
    dve.tensor_tensor(x1, ra[:, 0], rb[:, 0], ALU.subtract).then_inc(step, 1)
    dve.wait_ge(step, at + 2)
    dve.tensor_tensor(x2, ra[:, 1], rb[:, 1], ALU.add).then_inc(done, 1)


def multiply_chunk(pe, g, bank, j, c, ks, act_hi, act_lo):
    out = g.bank[:, bank, :CH]
    cols = slice(c * CH, (c + 1) * CH)
    for n, (kw, ka) in enumerate(ks):
        w, v = g.wu_hi[:, j, kw], g.wu_lo[:, j, kw]
        a, b = act_hi[:, ka, cols], act_lo[:, ka, cols]
        pe.matmul(out, w, a, start=n == 0, stop=False)
        pe.matmul(out, w, b, start=False, stop=False)
        last = pe.matmul(out, v, a, start=False, stop=n == len(ks) - 1)
    last.then_inc(g.full, 1)


def unit_room(g, room, tag):
    g.w_stage = room(f"w_stage_{tag}", [P, 2, KD, P])
    split_room(g, room, tag)


def split_room(g, room, tag):
    g.wu_hi = room(f"wu_hi_{tag}", [P, 2, KD, P], F32R)
    g.wu_lo = room(f"wu_lo_{tag}", [P, 2, KD, P], F32R)


def columns(w, m):
    return w.rearrange("(k p) c -> p k c", p=P)[:, :, bass.ds(m * P, P)]


def in_pairs(eng, n, body, peel=True):
    if peel:
        body(0)
    with eng.Fori(1 if peel else 0, n // 2) as i:
        body(i)


def first(i):
    return isinstance(i, int) and i == 0


def project_gates(g):
    nc = g.nc
    room = Room(nc, g.gate_split_at + KD * 512 * BYTES, g.room_kept)
    scaled = room("gt_scaled", [P, 2, CH])
    gate = room("gate_out", [P, 2, T])
    n = 2 * KD
    U, C = g.units, g.chunks
    gate_ready = g.sem("gt_ready")
    gate_out = [g.sem(f"gt_out{j}") for j in range(2)]
    gates = g.w_in[0].rearrange("(k p) c -> p k c", p=P)
    dst = g.gate_d.rearrange("a k p t -> (a k) p t")
    with nc.Block() as block:

        @block.sync
        def _(sp):
            def pair(i):
                for j in range(2):
                    sp.wait_ge(g.w_split, i * 2 + U + j - 1)
                    sp.dma_start(g.w_stage[:, j], gates[:, :, bass.ds(i * 256 + GATE_COL + j * P, P)]).then_inc(g.w_loaded[j], 16)
                copy_cache(sp, g, g.cache_win_k, g.win_k_sample, i, 1)

            copy_cache(sp, g, g.cache_win_k, g.win_k_sample, 0, 1)
            load_latent_weights(g, sp)
            with sp.Fori(1, n // 2) as i:
                pair(i)

        @block.gpsimd
        def _(pool):
            def pair(i):
                for j in range(2):
                    pool.wait_ge(g.w_loaded[j], i * 16 + 16)
                    pool.wait_ge(g.full, i * 6 + C + 3 * j - 3)
                    split_weights(pool, g, j, i * 2 + U + j + 1)

            with pool.Fori(1, n // 2) as i:
                pair(i)

        @block.tensor
        def _(pe):
            def pair(i):
                for j in range(2):
                    pe.wait_ge(g.w_split, i * 2 + U + j + 1)
                    for c in range(NCH):
                        if not first(i):
                            pe.wait_ge(g.free, i * 6 + C + 3 * j + c - 5)
                        multiply_chunk(pe, g, 3 * j + c, j, c, [(k, k) for k in range(KD)], g.h_hi, g.h_lo)
            in_pairs(pe, n, pair)

        @block.vector
        def _(dve):
            def pair(i):
                for q in range(6):
                    c = q % 3
                    dve.wait_ge(g.full, i * 6 + C + q + 1)
                    if not (first(i) and q < 2):
                        dve.wait_ge(gate_ready, i * 6 + q - 1)
                    dve.tensor_tensor(scaled[:, q % 2, :], g.bank[:, q, :CH], g.rstd_bc[:, c * CH:(c + 1) * CH],
                                      ALU.mult).then_inc(g.free, 1)
            in_pairs(dve, n, pair)

        @block.scalar
        def _(act):
            def pair(i):
                for q in range(6):
                    j, c = divmod(q, 3)
                    act.wait_ge(g.free, i * 6 + C + q + 1)
                    if not first(i) and c == 0:
                        act.wait_ge(gate_out[j], i * 16)
                    act.activation(gate[:, j, c * CH:(c + 1) * CH], scaled[:, q % 2, :], ACT.Sigmoid).then_inc(gate_ready, 1)
                    if c == NCH - 1:
                        act.wait_ge(gate_ready, i * 6 + q + 1)
                        act.dma_start(dst[bass.ds(i * 2 + j, 1)].rearrange("a p t -> p (a t)"), gate[:, j, :]).then_inc(gate_out[j], 16)
            in_pairs(act, n, pair)
            for j in range(2):
                act.wait_ge(gate_out[j], 16 * (n // 2))
    g.units += n
    g.turns += n // 2
    g.chunks += 3 * n


def load_latent_weights(g, sp):
    sp.dma_start(g.w_uq_sb[:, :, :], g.w_uq[0].rearrange("(k p) n -> p k n", p=P)).then_inc(g.l_in, 16)
    sp.dma_start(g.w_uk_sb[:, :, :], g.w_uk[0].rearrange("(k p) h e -> p k (h e)", p=P)).then_inc(g.l_in, 16)
    sp.dma_start(g.w_uv_sb[:, :, :], g.w_uv[0].rearrange("(k p) h e -> p k (h e)", p=P)).then_inc(g.l_in, 16)
    sp.dma_start(g.cos_b_sb[:, :, :], g.cos_b_c).then_inc(g.l_in, 16)
    sp.dma_start(g.sin_b_sb[:, :, :], g.sin_b_c).then_inc(g.l_in, 16)
    sp.dma_start(g.g_q_sb[:, :], g.g_q[0].rearrange("(k p) -> p k", p=P), allow_slow_non_contiguous=True).then_inc(g.l_in, 16)


def project_latents(g):
    nc = g.nc
    room = Room(nc, R1, R2)
    w_uq, w_uk, cos_b, sin_b, g_q, l_in = g.w_uq_sb, g.w_uk_sb, g.cos_b_sb, g.sin_b_sb, g.g_q_sb, g.l_in
    cq_t = room("cq_t", [P, 3, T])
    q_nat = room("q_nat", [P, 2, H * BH])
    ra = room("lat_ra2", [P, 2, H, 16])
    rb = room("lat_rb2", [P, 2, H, 16])
    root_q = room("lat_root_q", [P, NT])
    w_ukt = room("w_ukt", [E, H, 2, P])
    (mask_in, rq_done, l_step, cq_full, cq_got,
     ck_full, ck_got, uk_full, uk_got, qf, qg, qr, qt, qtg, kf, kg, vf, vg, lf) = map(g.sem, (
         "lm_in", "l_rq", "q_step",
         "cq_full", "cq_got", "ck_full", "ck_got", "uk_full", "uk_got", "qb_full", "qb_got", "qb_turned",
         "qb_tr", "qb_tgot", "kn_full", "kn_got", "vb_full", "vb_got", "ql_full"))

    with nc.Block() as block:

        @block.sync
        def _(sp):
            sp.wait_ge(cq_full, NT)
            sp.wait_ge(ck_full, NT)
            sp.dma_start(g.latent_mask[:, :, :], g.mask_b_c).then_inc(mask_in, 16)
            sp.wait_ge(mask_in, 16)

        @block.tensor
        def _(pe):
            def turn_latents(t):
                r = ROWS[t]
                if t >= 1:
                    pe.wait_ge(cq_got, t)
                for k in range(3):
                    last = pe.transpose(g.bank[:, 6, k * P:k * P + r], g.cq[:r, t, k * P:(k + 1) * P], g.ident[:r, :r])
                last.then_inc(cq_full, 1)
                if t >= 1:
                    pe.wait_ge(ck_got, t)
                for k in range(2):
                    pe.transpose(g.bank[:, 7, k * P:k * P + r], g.ckv[:r, t, k * P:(k + 1) * P], g.ident[:r, :r])
                w, c0 = (BH, KL - E) if t < NT - 1 else (RD, KL)
                pe.transpose(g.bank[:w, 7, 2 * P:2 * P + r], g.ckv[:r, t, c0:], g.ident[:r, :r]).then_inc(ck_full, 1)

            def queries(t):
                r = ROWS[t]
                pe.wait_ge(cq_got, t + 1)
                for half in range(2):
                    n = 2 * t + half
                    if n >= 4:
                        pe.wait_ge(qg, n - 3)
                    for k in range(3):
                        last = pe.matmul(g.bank[:r, n % 4, :QL], cq_t[:, k, t * P:t * P + r], w_uq[:, k, half * QL:(half + 1) * QL],
                                         start=k == 0, stop=k == 2)
                    last.then_inc(qf, 1)

            def turn_queries(t):
                r = ROWS[t]
                pe.wait_ge(qr, t + 1)
                for half in range(2):
                    n = 2 * t + half
                    if n >= 2:
                        pe.wait_ge(qtg, n - 1)
                    for m in range(4):
                        h = 4 * half + m
                        last = pe.transpose(g.bank[:BH, 4 + half, m * P:m * P + r], q_nat[:r, t % 2, h * BH:(h + 1) * BH], g.ident[:r, :r])
                    last.then_inc(qt, 1)

            pe.wait_ge(l_in, 6 * 16)
            for t in range(NT + 2):
                if t < NT:
                    turn_latents(t)
                if 1 <= t <= NT:
                    queries(t - 1)
                if t >= 2:
                    turn_queries(t - 2)
            for n in range(4):
                if n < 2:
                    pe.wait_ge((cq_got, ck_got)[n], NT)
                else:
                    pe.wait_ge(uk_got, n - 1)
                for m in range(4):
                    h, c = 2 * n + m // 2, m % 2
                    last = pe.transpose(g.bank[:E, 6 + n % 2, m * P:(m + 1) * P], w_uk[:, c, h * E:(h + 1) * E], g.ident[:, :])
                last.then_inc(uk_full, 1)
            for n in range(2 * H):
                h, half = divmod(n, 2)
                if n < 2:
                    pe.wait_ge(uk_got, n + 3)
                else:
                    pe.wait_ge(kg, n - 1)
                for c in range(2):
                    last = pe.matmul(g.bank[:E, 6 + n % 2, :], w_uk[:, c, h * E:(h + 1) * E], g.ckv_t[:, c, half * 512:(half + 1) * 512],
                                     start=c == 0, stop=c == 1)
                last.then_inc(kf, 1)
            pe.wait_ge(qg, 2 * NT)
            for j in range(NT - 1):
                if j >= 4:
                    pe.wait_ge(vg, j - 3)
                for c in range(2):
                    last = pe.matmul(g.bank[:, j % 4, :], g.ckv_t[:, c, j * P:(j + 1) * P], g.w_uv_sb[:, c, :], start=c == 0, stop=c == 1)
                last.then_inc(vf, 1)
            pe.wait_ge(qtg, 2 * NT)
            for h in range(H):
                last = pe.transpose(g.bank[:RD, 4, h * NS:(h + 1) * NS], q_nat[:NS, (NT - 1) % 2, h * BH + E:(h + 1) * BH], g.ident[:NS, :NS])
            last.then_inc(lf, 1)
            for c in range(2):
                for h in range(H):
                    at = (c * H + h) * NS
                    last = pe.matmul(g.bank[:, 5, at:at + NS], w_ukt[:, h, c, :], g.qb_t[:E, h, SEQ:], start=True, stop=True)
            last.then_inc(lf, 1)

        @block.scalar
        def _(act):
            def turned_out(t):
                r = ROWS[t]
                for half in range(2):
                    act.wait_ge(qt, 2 * t + half + 1)
                    act.activation(g.qb_t[:, 4 * half:4 * half + 4, t * P:t * P + r],
                                   g.bank[:BH, 4 + half, :].rearrange("p (h c) -> p h c", h=4)[:, :, :r], ACT.Copy).then_inc(qtg, 1)

            act.wait_ge(rq_done, 1)
            for t in range(NT):
                r = ROWS[t]
                for half in range(2):
                    n = 2 * t + half
                    act.wait_ge(qf, n + 1)
                    if t >= 2:
                        act.wait_ge(qt, 2 * t - 2)
                    act.activation(q_nat[:r, t % 2, half * QL:(half + 1) * QL], g.bank[:r, n % 4, :QL], ACT.Copy,
                                   scale=root_q[:r, t:t + 1]).then_inc(qg, 1)
                if t >= 1:
                    turned_out(t - 1)
            turned_out(NT - 1)
            for j in range(NT - 1):
                act.wait_ge(vf, j + 1)
                act.activation(g.vb[:, j, :], g.bank[:, j % 4, :], ACT.Copy).then_inc(vg, 1)

        @block.vector
        def _(dve):
            def take_latents(t):
                r = ROWS[t]
                toks = slice(t * P, t * P + r)
                dve.wait_ge(cq_full, t + 1)
                dve.tensor_tensor(cq_t[:, :, toks], g.bank[:, 6, :3 * P].rearrange("p (k c) -> p k c", k=3)[:, :, :r],
                                  g_q[:, :].unsqueeze(2).to_broadcast([P, 3, r]), ALU.mult).then_inc(cq_got, 1)
                dve.wait_ge(ck_full, t + 1)
                b = g.bank[:, 7, :].rearrange("p (k c) -> p k c", k=4)
                if t < NT - 1:
                    dve.tensor_copy(g.kb_t[E:BH, :, toks], b[E:BH, 2:3, :].to_broadcast([RD, H, P]))
                else:
                    dve.tensor_copy(g.kpe_t[:, :], b[:RD, 2, :r])
                dve.tensor_copy(g.ckv_t[:, :, toks], b[:, 0:2, :r]).then_inc(ck_got, 1)

            dve.tensor_scalar(root_q[:, :], g.root[:, 0, :], BH ** -0.5, None, ALU.mult).then_inc(rq_done, 1)
            dve.wait_ge(l_in, 6 * 16)
            take_latents(0)
            for t in range(NT):
                if t + 1 < NT:
                    take_latents(t + 1)
                r = ROWS[t]
                dve.wait_ge(qg, 2 * t + 2)
                rotate(dve, q_nat[:r, t % 2, :].rearrange("p (h e) -> p h e", e=BH)[:, :, E:], 16, cos_b[:r, t, :],
                       sin_b[:r, t, :], ra[:r], rb[:r], H, l_step, 2 * t, qr, t)
            for n in range(4):
                dve.wait_ge(uk_full, n + 1)
                dve.tensor_copy(w_ukt[:, 2 * n:2 * n + 2, :, :].rearrange("e h c p -> e (h c p)"), g.bank[:E, 6 + n % 2, :]).then_inc(uk_got, 1)
            for n in range(2 * H):
                h, half = divmod(n, 2)
                dve.wait_ge(kf, n + 1)
                dve.tensor_copy(g.kb_t[:E, h, half * 512:(half + 1) * 512], g.bank[:E, 6 + n % 2, :]).then_inc(kg, 1)
            dve.wait_ge(lf, 1)
            dve.tensor_copy(g.qpe_t[:, :, :, :].rearrange("r s h t -> r h s t"),
                            g.bank[:RD, 4, :H * NS].rearrange("r (h s t) -> r h s t", h=H, s=NSEQ))
            dve.wait_ge(lf, 2)
            for c in range(2):
                dve.tensor_copy(g.ql_t[:, c].rearrange("p s h t -> p h s t"),
                                g.bank[:, 5, c * H * NS:(c + 1) * H * NS].rearrange("p (h s t) -> p h s t", h=H, s=NSEQ))


def attend_prompt(g, kind, ahead):
    nc = g.nc
    window = kind == "window"
    room = Room(nc, R2, ahead.start) if window else Room(nc, g.room_b, ahead.start - SEQ * BYTES)
    sem = lambda name: g.sem(f"{kind[0]}_{name}")
    if window:
        q_t = room("qw_t", [P, H // 2, SEQ])
        k_t = room("kw_t", [P, H // 2, SEQ])
        v = room("vw", [P, NT - 1, H * E])
        head = lambda x, h: x[E * (h % 2):E * (h % 2) + E, h // 2, :]
    else:
        q_t, k_t, v = g.qb_t, g.kb_t, g.vb
        head = lambda x, h: x[:, h, :]
    mask = room(f"{kind}_mask", [P, NT - 1, P]) if window else g.latent_mask
    prob = room(f"{kind}_prob", [P, 4, SEQ])
    prob_t = room(f"{kind}_prob_t", [P, 2, NT - 1, P])
    top = room(f"{kind}_top", [P, 4, 4])
    mask_in, v_in, s_full, s_got, e_done, inv_done, p_ready, t_full, t_got, o_full, o_hi_s, o_got = map(sem, (
        "mask_in", "v_in", "s_full", "s_got", "e_done", "inv_done", "p_ready", "t_full", "t_got", "o_full", "o_hi", "o_got"))
    steps = [(h, i) for h in range(H) for i in reversed(range(NT - 1))]
    groups = []
    n = 0
    for h, i in steps:
        mine = []
        for j in range(0, i + 1, 4):
            mine.append((n, j, min(j + 4, i + 1)))
            n += 1
        groups.append(mine)
    N = len(steps)
    with nc.Block() as block:

        @block.sync
        def _(sp):
            if window:
                sp.dma_start(mask[:, :, :], g.mask_w_c).then_inc(mask_in, 16)
                load_queries_and_keys(g, sp, (3,))
                sp.dma_start(v[:, :, :], g.v_d[:SEQ, :].rearrange("(t p) c -> p t c", p=P)).then_inc(v_in, 16)
                sp.wait_ge(g.wt_full, 16)
            ahead.load(g, sp)
            if not window:
                for s in range(NSEQ):
                    sp.wait_ge(o_got, s * (N // NSEQ) + 1)
                    copy_cache(sp, g, g.cache_win_v, g.win_v_sample, s, 1)

        @block.gpsimd
        def _(pool):
            if not window:
                ahead.load_rotary(g, pool)

        @block.tensor
        def _(pe):
            def scores(s):
                h, i = steps[s]
                if s >= 2:
                    pe.wait_ge(s_got, s - 1)
                for at in range(0, (i + 1) * P, 512):
                    w = min(512, (i + 1) * P - at)
                    last = pe.matmul(g.bank[:, 2 * (s % 2) + at // 512, :w], head(q_t, h)[:, i * P:(i + 1) * P],
                                     head(k_t, h)[:, at:at + w], start=True, stop=True)
                last.then_inc(s_full, 1)

            def transposes(s):
                pe.wait_ge(p_ready, s + 1)
                for n, a, b in groups[s]:
                    if n >= 2:
                        pe.wait_ge(t_got, n - 1)
                    for j in range(a, b):
                        last = pe.transpose(g.bank[:, 4 + n % 2, (j - a) * P:(j - a + 1) * P],
                                            prob[:, s % 4, j * P:(j + 1) * P], g.ident[:, :])
                    last.then_inc(t_full, 1)

            def values(s):
                h, i = steps[s]
                if window and s == 0:
                    pe.wait_ge(v_in, 16)
                if s >= 2:
                    pe.wait_ge(o_got, s - 1)
                lo = E * (h % 2)
                for n, a, b in groups[s]:
                    pe.wait_ge(t_got, n + 1)
                    for j in range(a, b):
                        last = pe.matmul(g.bank[lo:lo + E, 6 + s % 2, :P], v[:, j, h * E:(h + 1) * E],
                                         prob_t[:, s % 2, j, :], start=j == 0, stop=j == i)
                last.then_inc(o_full, 1)

            if window:
                turn_window(pe, g)
                for odd in range(2):
                    pe.wait_ge(g.wt_got[odd], 8)
            for s in range(3):
                scores(s)
            for s in range(N):
                if s + 3 < N:
                    scores(s + 3)
                transposes(s)
                if s >= 1:
                    values(s - 1)
            values(N - 1)

        @block.vector
        def _(dve):
            def largest(s):
                h, i = steps[s]
                w = (i + 1) * P
                dve.wait_ge(s_full, s + 1)
                if s >= 4:
                    dve.wait_ge(t_full, groups[s - 4][-1][0] + 1)
                dve.tensor_tensor_reduce(out=prob[:, s % 4, :w],
                                         in0=g.bank[:, 2 * (s % 2):2 * (s % 2) + 2, :].rearrange("p a b -> p (a b)")[:, :w],
                                         in1=mask[:, NT - 2 - i:, :].rearrange("p a b -> p (a b)"),
                                         scale=-1.0, scalar=-FLOOR, op0=ALU.add, op1=ALU.min,
                                         accum_out=top[:, s % 4, 0:1]).then_inc(s_got, 1)

            def divide(s):
                h, i = steps[s]
                w = (i + 1) * P
                dve.wait_ge(e_done, s + 1)
                dve.reciprocal(top[:, s % 4, 3:4], top[:, s % 4, 2:3]).then_inc(inv_done, 1)
                dve.wait_ge(inv_done, s + 1)
                dve.tensor_scalar(prob[:, s % 4, :w], prob[:, s % 4, :w], top[:, s % 4, 3:4], None, ALU.mult).then_inc(p_ready, 1)

            def take(s):
                h, i = steps[s]
                lo = E * (h % 2)
                tile = h // 2 + (0 if window else H // 2)
                place = (slice(lo, lo + E), tile, slice(i * P, (i + 1) * P))
                dve.wait_ge(o_full, s + 1)
                dve.tensor_copy(g.o_hi[place], g.bank[lo:lo + E, 6 + s % 2, :P]).then_inc(o_hi_s, 1)
                dve.wait_ge(o_hi_s, s + 1)
                dve.tensor_tensor(g.o_lo[place], g.bank[lo:lo + E, 6 + s % 2, :P], g.o_hi[place].bitcast(F32),
                                  ALU.subtract).then_inc(o_got, 1)

            if window:
                take_window(g, 1, dve.tensor_copy, dve, q_t, k_t)
                dve.wait_ge(mask_in, 16)
            largest(0)
            largest(1)
            for s in range(N):
                divide(s)
                if s + 2 < N:
                    largest(s + 2)
                if s >= 2:
                    take(s - 2)
            take(N - 2)
            take(N - 1)

        @block.scalar
        def _(act):
            def exponent(s):
                h, i = steps[s]
                w = (i + 1) * P
                act.wait_ge(s_got, s + 1)
                act.activation(prob[:, s % 4, :w], prob[:, s % 4, :w], ACT.Exp, scale=-1.0, bias=top[:, s % 4, 0:1],
                               accum_out=top[:, s % 4, 2:3]).then_inc(e_done, 1)

            if window:
                take_window(g, 0, lambda out, src: act.activation(out, src, ACT.Copy), act, q_t, k_t)
            exponent(0)
            exponent(1)
            for s in range(N):
                if s >= 2:
                    act.wait_ge(o_full, s - 1)
                for n, a, b in groups[s]:
                    act.wait_ge(t_full, n + 1)
                    act.activation(prob_t[:, s % 2, a:b, :].rearrange("p a b -> p (a b)"),
                                   g.bank[:, 4 + n % 2, :(b - a) * P], ACT.Copy).then_inc(t_got, 1)
                if s + 2 < N:
                    exponent(s + 2)


def load_queries_and_keys(g, sp, jobs):
    for m in jobs:
        x, half = divmod(m, 2)
        if m >= 3:
            sp.wait_ge(g.wt_full, 4 * (m - 2))
        src = (g.q_d, g.k_d)[x][:SEQ, half * 256:(half + 1) * 256]
        sp.dma_start(g.win_nat[:, m % 3], src.rearrange("(t p) c -> p t c", p=P)).then_inc(g.wqk_in[m], 16)


def turn_window(pe, g):
    for n in range(16):
        m, tile, quad = n // 4, n // 2 % 2, n % 2
        pe.wait_ge(g.wqk_in[m], 16)
        if n >= 4:
            pe.wait_ge(g.wt_got[n % 2], n // 2 - 1)
        for t in range(4):
            last = pe.transpose(g.bank[:, 4 + n % 4, t * P:(t + 1) * P],
                                g.win_nat[:, m % 3, 4 * quad + t, tile * P:(tile + 1) * P], g.ident[:, :])
        last.then_inc(g.wt_full, 1)


def take_window(g, odd, copy, eng, q_t, k_t):
    for n in range(odd, 16, 2):
        m, tile, quad = n // 4, n // 2 % 2, n % 2
        x, half = divmod(m, 2)
        eng.wait_ge(g.wt_full, n + 1)
        copy((q_t, k_t)[x][:, 2 * half + tile, quad * 512:(quad + 1) * 512], g.bank[:, 4 + n % 4, :]).then_inc(g.wt_got[odd], 1)


class Ahead:

    @staticmethod
    def start_of(kind):
        size = 2 * SK * H * E if kind == "window" else NPAGE * (KL + RD) + NSEQ * NPAGE
        return TOP // 32 * 32 - size * BYTES

    def __init__(self, g, kind):
        self.kind, self.start = kind, self.start_of(kind)
        room = Room(g.nc, self.start)
        if kind == "window":
            self.keys, self.vals = (room(f"ws_{n}0", [P, SK, H * E]) for n in ("keys", "vals"))
            self.k_in, self.v_in = ([g.sem(f"ws_{n}_in{j}") for j in range(3)] for n in "kv")
        else:
            self.keys = self.vals = room("ls_keys0", [P, NPAGE, KL + RD])
            self.pages = room("ls_pages", [1, NSEQ * NPAGE], I32)
            self.k_in, self.v_in = ([g.sem(f"ls_{n}_in{j}") for j in range(4)] for n in ("ckv", "kpe"))
            self.pages_in = g.sem("pages_in")

    def load(self, g, sp):
        if self.kind == "window":
            load_cached_window(sp, g.cache_win_k, 0, self.keys, self.k_in[0])
            load_cached_window(sp, g.cache_win_v, 0, self.vals, self.v_in[0])
        else:
            sp.dma_start(self.pages[:, :], g.page_table.rearrange("(a s) n -> a (s n)", a=1)).then_inc(self.pages_in, 16)
            sp.wait_ge(self.pages_in, 16)
            load_pages(sp, self.pages, 0, g.cache_ckv, self.keys[:, :, :KL], self.k_in[0])

    def load_rotary(self, g, pool):
        pool.wait_ge(self.pages_in, 16)
        load_pages(pool, self.pages, 0, g.cache_kpe, self.keys[:, :, KL:], self.v_in[0])


def load_cached_window(sp, cache, s, dst, arrived):
    far = cache[0, s, 0:PAST // 2].rearrange("(m r) h e -> m r (h e)", r=16)
    for r in range(4):
        sp.dma_start(dst[32 * r:32 * r + 32, 0, :], far[:, r, :]).then_inc(arrived, 16)
    sp.dma_start(dst[:, 1:, :], cache[0, s, PAST // 2:].rearrange("(a p) h e -> p a (h e)", p=P)).then_inc(arrived, 16)


def load_pages(eng, pages, s, cache, dst, arrived):
    for n in range(NPAGE):
        page = eng.value_load(pages[0:1, s * NPAGE + n:s * NPAGE + n + 1], min_val=0, max_val=NPHYS - 1)
        eng.dma_start(dst[:, n, :], cache[0, bass.ds(page, 1)].rearrange("a p c -> p (a c)")).then_inc(arrived, 16)


def attend_sample(g, kind, ahead):
    nc = g.nc
    window = kind == "window"
    tag = "ws" if window else "ls"
    tiles = SK if window else NPAGE
    width = tiles * P + TDEC
    vcols = H * E if window else KL
    room = Room(nc, R2, RW if window else g.room_kept)
    sem = lambda name: g.sem(f"{tag}_{name}")
    if window:
        keys = [ahead.keys] + [room("ws_keys1", [P, SK, H * E])]
        vals = [ahead.vals] + [room(f"ws_vals{j}", [P, SK, H * E]) for j in (1, 2)]
        unit_room(g, Room(nc, RW, RX), "tail")
        key_t = room("ws_key_t", [P, H // 2, width])
        q_new = room("ws_q_new", [NS, H * E])
        k_new = room("ws_k_new", [NS, H * E])
        k_new_t = room("ws_k_new_t", [P, H // 2, NS])
        q_rows = room("ws_q_rows", [P, H // 2, NSEQ, H, TDEC])
        v_new = room("ws_v_new", [TDEC, 3, H * E])
        v_new_in = [sem(f"v_new_in{j}") for j in range(3)]
    else:
        keys = [ahead.keys] + [room(f"ls_keys{j}", [P, NPAGE, KL + RD]) for j in (1, 2, 3)]
        vals = keys
        key_t = room("ls_key_t", [P, 2, width])
        pe_t = room("ls_pe_t", [RD, width])
        v_new = room("ls_v_new", [TDEC, NSEQ, KL])
        o_t = room("ls_o_t", [P, 2, H, NSEQ, TDEC])
    mask = room(f"{tag}_mask", [NS, width])
    masked = room(f"{tag}_masked", [NS, width])
    prob = room(f"{tag}_prob", [NS, width])
    prob_t = room(f"{tag}_prob_t", [P, tiles + 1, NS])
    top = room(f"{tag}_top", [NS, 2, 4])
    o_nat = room(f"{tag}_o_nat", [NS, vcols])
    (c_in, new_full, new_got, q_set, k_full, s_full, s_got, e_done, inv_done, p_ready,
     pt_full, pt_got, o_full, o_taken, ot_full, ot_got, o_hi_s) = map(sem, (
         "c_in", "new_full", "new_got", "q_set", "k_full", "s_full", "s_got", "e_done",
         "inv_done", "p_ready", "pt_full", "pt_got", "o_full", "o_taken", "ot_full", "ot_got", "o_hi"))
    k_got = [sem(f"k_got{odd}") for odd in range(2)]
    k_in, v_in = ahead.k_in, ahead.v_in
    k_ring, v_ring = len(keys), len(vals)
    kv_count = 80 if window else 16 * NPAGE
    n_const = (3 if window else 2) * 16
    each = [len(range(odd, tiles, 2)) for odd in range(2)]

    def take_keys(eng, s, odd):
        copy = eng.tensor_copy if odd else lambda out, src: eng.activation(out, src, ACT.Copy)
        if s >= 1:
            eng.wait_ge(s_full, s)
        for n in range(odd, tiles, 2):
            eng.wait_ge(k_full, s * tiles + n + 1)
            cols = slice(n * P, (n + 1) * P)
            kt = 4 if window else 2
            last = copy(key_t[:, :, cols], g.bank[:, 3 + odd, :kt * P].rearrange("p (k c) -> p k c", k=kt))
            if not window:
                last = copy(pe_t[:, cols], g.bank[:RD, 3 + odd, 2 * P:3 * P])
            last.then_inc(k_got[odd], 1)

    def exponent(act, s):
        act.wait_ge(s_got, s + 1)
        if s >= 1:
            act.wait_ge(pt_full, s)
        act.activation(prob[:, :], masked[:, :], ACT.Exp, scale=-1.0, bias=top[:, s % 2, 0:1], accum_out=top[:, s % 2, 2:3]).then_inc(e_done, 1)

    scores_flat = g.bank[:NS, 0:3, :].rearrange("p a b -> p (a b)")[:, :width]
    with nc.Block() as block:

        @block.sync
        def _(sp):
            sp.dma_start(mask[:, :], g.mask_ws_c if window else g.mask_ls_c).then_inc(c_in, 16)
            if window:
                sp.dma_start(q_new[:, :], g.q_d[SEQ:, :]).then_inc(c_in, 16)
                sp.dma_start(k_new[:, :], g.k_d[SEQ:, :]).then_inc(c_in, 16)
                sp.dma_start(v_new[:, 0, :], g.v_d[SEQ:SEQ + TDEC, :]).then_inc(v_new_in[0], 16)
            else:
                sp.dma_start(v_new[:, :, :], g.ckv_sample[0].rearrange("s t c -> t s c")).then_inc(c_in, 16)
            for s in range(1, NSEQ):
                j, jv = s % k_ring, s % v_ring
                if window:
                    if s >= k_ring:
                        sp.wait_ge(k_full, (s - k_ring + 1) * tiles)
                    load_cached_window(sp, g.cache_win_k, s, keys[j], k_in[j])
                    if s >= v_ring:
                        sp.wait_ge(o_full, s - v_ring + 1)
                    load_cached_window(sp, g.cache_win_v, s, vals[jv], v_in[jv])
                    sp.dma_start(v_new[:, jv, :], g.v_d[SEQ + s * TDEC:SEQ + (s + 1) * TDEC, :]).then_inc(v_new_in[jv], 16)
                    if s == 2:
                        for m in range(2):
                            load_merge_unit(sp, g, m, m)
                else:
                    if s >= k_ring:
                        sp.wait_ge(o_full, s - k_ring + 1)
                    load_pages(sp, ahead.pages, s, g.cache_ckv, keys[j][:, :, :KL], k_in[j])
                    if s == NSEQ // 2:
                        load_queries_and_keys(g, sp, (0, 1, 2))

        @block.gpsimd
        def _(pool):
            if window:
                for j in range(2):
                    pool.wait_ge(g.w_loaded[j], (g.turns + 2) * 16)
                    split_weights(pool, g, j, g.units + j + 1)
            else:
                for s in range(1, NSEQ):
                    j = s % v_ring
                    if s >= v_ring:
                        pool.wait_ge(o_full, s - v_ring + 1)
                    load_pages(pool, ahead.pages, s, g.cache_kpe, keys[j][:, :, KL:], v_in[j])

        @block.tensor
        def _(pe):
            def turn_tile(s, n):
                if n == 0:
                    pe.wait_ge(k_in[s % k_ring], kv_count * (s // k_ring + 1))
                    if not window:
                        pe.wait_ge(v_in[s % v_ring], kv_count * (s // v_ring + 1))
                if s or n >= 2:
                    pe.wait_ge(k_got[n % 2], s * each[n % 2] + n // 2)
                b = 3 + n % 2
                for k in range(4 if window else 2):
                    last = pe.transpose(g.bank[:, b, k * P:(k + 1) * P], keys[s % k_ring][:, n, k * P:(k + 1) * P], g.ident[:, :])
                if not window:
                    last = pe.transpose(g.bank[:RD, b, 2 * P:3 * P], keys[s % k_ring][:, n, KL:], g.ident[:, :])
                last.then_inc(k_full, 1)

            def scores(s):
                for odd in range(2):
                    pe.wait_ge(k_got[odd], (s + 1) * each[odd])
                pe.wait_ge(new_got, s + 1)
                if s >= 1:
                    pe.wait_ge(s_got, s)
                for at in range(0, width, 512):
                    w = min(512, width - at)
                    out = g.bank[:NS, at // 512, :w]
                    if window:
                        for k in range(4):
                            last = pe.matmul(out, q_rows[:, k, s].rearrange("p h t -> p (h t)"), key_t[:, k, at:at + w],
                                             start=k == 0, stop=k == 3)
                    else:
                        for k in range(2):
                            pe.matmul(out, g.ql_t[:, k, s].rearrange("p h t -> p (h t)"), key_t[:, k, at:at + w],
                                      start=k == 0, stop=False)
                        last = pe.matmul(out, g.qpe_t[:, s].rearrange("p h t -> p (h t)"), pe_t[:, at:at + w],
                                         start=False, stop=True)
                last.then_inc(s_full, 1)

            def turn_probs(s):
                pe.wait_ge(p_ready, s + 1)
                if s >= 1:
                    pe.wait_ge(pt_got, s)
                for n in range(tiles):
                    pe.transpose(g.bank[:, 5, n * NS:(n + 1) * NS], prob[:, n * P:(n + 1) * P], g.ident[:NS, :NS])
                pe.transpose(g.bank[:TDEC, 5, tiles * NS:(tiles + 1) * NS], prob[:, tiles * P:], g.ident[:NS, :NS]).then_inc(pt_full, 1)

            def values(s, n):
                if n == 0:
                    if window:
                        pe.wait_ge(v_in[s % v_ring], kv_count * (s // v_ring + 1))
                        pe.wait_ge(v_new_in[s % v_ring], 16 * (s // v_ring + 1))
                    pe.wait_ge(pt_got, s + 1)
                    if s >= 1:
                        pe.wait_ge(o_taken, s)
                if n < tiles:
                    pe.matmul(g.bank[:NS, 6, :vcols], prob_t[:, n, :], vals[s % v_ring][:, n, :vcols], start=n == 0, stop=False)
                else:
                    pe.matmul(g.bank[:NS, 6, :vcols], prob_t[:TDEC, tiles, :], v_new[:, s % v_ring if window else s, :],
                              start=False, stop=True).then_inc(o_full, 1)

            def turn_result(s):
                pe.wait_ge(o_taken, s + 1)
                if s >= 1:
                    pe.wait_ge(ot_got, s)
                for k in range(vcols // P):
                    last = pe.transpose(g.bank[:, 7, k * NS:(k + 1) * NS], o_nat[:, k * P:(k + 1) * P], g.ident[:NS, :NS])
                last.then_inc(ot_full, 1)

            for n in range(tiles):
                turn_tile(0, n)
            if window:
                pe.wait_ge(c_in, n_const)
                for x in (q_new, k_new):
                    for k in range(4):
                        at = (0 if x is q_new else P) + k * NS
                        last = pe.transpose(g.bank[:, 7, at:at + NS], x[:, k * P:(k + 1) * P], g.ident[:NS, :NS])
                last.then_inc(new_full, 1)
            pe.wait_ge(q_set, 1)
            scores(0)
            for n in range(tiles):
                turn_tile(1, n)
            for s in range(NSEQ):
                turn_probs(s)
                if s >= 1:
                    turn_result(s - 1)
                if s + 1 < NSEQ:
                    scores(s + 1)
                for n in range(tiles + 2):
                    if s + 2 < NSEQ and n < tiles:
                        turn_tile(s + 2, n)
                    if n >= 1:
                        values(s, n - 1)
            turn_result(NSEQ - 1)
            if not window:
                pe.wait_ge(ot_got, NSEQ)
                for h in range(H):
                    lo = E * (h % 2)
                    for c in range(2):
                        last = pe.matmul(g.bank[lo:lo + E, 5 + h % 2, (h // 2) * NS:(h // 2 + 1) * NS], g.w_uv_sb[:, c, h * E:(h + 1) * E],
                                         o_t[:, c, h].rearrange("p s t -> p (s t)"), start=c == 0, stop=c == 1)
                last.then_inc(ot_full, 1)

        @block.scalar
        def _(act):
            for s in range(2):
                take_keys(act, s, 0)
                if s == 0:
                    exponent(act, s)
            for s in range(NSEQ):
                if s + 2 < NSEQ:
                    take_keys(act, s + 2, 0)
                if s + 1 < NSEQ:
                    exponent(act, s + 1)

        @block.vector
        def _(dve):
            def add_new(s):
                if s >= 1:
                    dve.wait_ge(s_full, s)
                if window:
                    dve.tensor_copy(key_t[:, :, SK * P:], k_new_t[:, :, s * TDEC:(s + 1) * TDEC]).then_inc(new_got, 1)
                else:
                    dve.tensor_copy(key_t[:, :, PAST:], g.ckv_t[:, :, SEQ + s * TDEC:SEQ + (s + 1) * TDEC])
                    dve.tensor_copy(pe_t[:, PAST:], g.kpe_t[:, s * TDEC:(s + 1) * TDEC]).then_inc(new_got, 1)

            if window:
                dve.memset(q_rows[:, :, :, :, :].rearrange("p k s h t -> p (k s h t)"), 0.0).then_inc(q_set, 1)
                take_keys(dve, 0, 1)
                dve.wait_ge(new_full, 1)
                dve.wait_ge(q_set, 1)
                for h in range(H):
                    lo, k = E * (h % 2), h // 2
                    dve.tensor_copy(q_rows[lo:lo + E, k, :, h, :],
                                    g.bank[lo:lo + E, 7, k * NS:(k + 1) * NS].rearrange("p (s t) -> p s t", s=NSEQ))
                dve.tensor_copy(k_new_t[:, :, :], g.bank[:, 7, P:2 * P].rearrange("p (k c) -> p k c", k=4)).then_inc(q_set, 1)
                dve.wait_ge(q_set, 2)
            else:
                dve.memset(masked[:, :], 0.0).then_inc(q_set, 1)
                take_keys(dve, 0, 1)
            def largest(s):
                dve.wait_ge(s_full, s + 1)
                if s >= 1:
                    dve.wait_ge(e_done, s)
                dve.tensor_tensor_reduce(out=masked[:, :], in0=scores_flat, in1=mask[:, :], scale=-1.0, scalar=-FLOOR,
                                         op0=ALU.add, op1=ALU.min, accum_out=top[:, s % 2, 0:1]).then_inc(s_got, 1)

            def divide(s):
                dve.wait_ge(e_done, s + 1)
                dve.reciprocal(top[:, s % 2, 3:4], top[:, s % 2, 2:3]).then_inc(inv_done, 1)
                dve.wait_ge(inv_done, s + 1)
                dve.tensor_scalar(prob[:, :], prob[:, :], top[:, s % 2, 3:4], None, ALU.mult).then_inc(p_ready, 1)

            def take_probs(s):
                dve.wait_ge(pt_full, s + 1)
                if s >= 1:
                    dve.wait_ge(o_full, s)
                dve.tensor_copy(prob_t[:, :tiles, :].rearrange("p a b -> p (a b)"), g.bank[:, 5, :tiles * NS])
                dve.tensor_copy(prob_t[:TDEC, tiles, :], g.bank[:TDEC, 5, tiles * NS:(tiles + 1) * NS]).then_inc(pt_got, 1)

            def take_result(s):
                dve.wait_ge(ot_full, s + 1)
                if window:
                    at = SEQ + s * TDEC
                    for odd in range(2):
                        lo = E * odd
                        src = g.bank[lo:lo + E, 7, 0:160].rearrange("p (a c) -> p a c", c=NS + 2 * TDEC)[:, :, odd * TDEC:(odd + 1) * TDEC]
                        place = (slice(lo, lo + E), slice(0, H // 2), slice(at, at + TDEC))
                        dve.tensor_copy(g.o_hi[place], src).then_inc(o_hi_s, 1)
                        dve.wait_ge(o_hi_s, 2 * s + odd + 1)
                        last = dve.tensor_tensor(g.o_lo[place], src, g.o_hi[place].bitcast(F32), ALU.subtract)
                    last.then_inc(ot_got, 1)
                else:
                    dve.tensor_copy(o_t[:, :, :, s, :], g.bank[:, 7, :2 * NS].rearrange("p (c h t) -> p c h t", c=2, h=H)).then_inc(ot_got, 1)

            add_new(0)
            dve.wait_ge(c_in, n_const)
            largest(0)
            add_new(1)
            take_keys(dve, 1, 1)
            divide(0)
            for s in range(NSEQ):
                take_probs(s)
                if s >= 1:
                    take_result(s - 1)
                if s + 1 < NSEQ:
                    largest(s + 1)
                if s + 2 < NSEQ:
                    add_new(s + 2)
                    take_keys(dve, s + 2, 1)
                if s + 1 < NSEQ:
                    divide(s + 1)
                dve.wait_ge(o_full, s + 1)
                if s >= 1:
                    dve.wait_ge(ot_full, s)
                dve.tensor_copy(o_nat[:, :], g.bank[:NS, 6, :vcols]).then_inc(o_taken, 1)
            take_result(NSEQ - 1)
            if not window:
                dve.wait_ge(ot_full, NSEQ + 1)
                for odd in range(2):
                    lo = E * odd
                    src = g.bank[lo:lo + E, 5 + odd, :P].rearrange("p (a c) -> p a c", a=4)
                    place = (slice(lo, lo + E), slice(H // 2, H), slice(SEQ, T))
                    dve.tensor_copy(g.o_hi[place], src).then_inc(o_hi_s, 1)
                    dve.wait_ge(o_hi_s, odd + 1)
                    dve.tensor_tensor(g.o_lo[place], src, g.o_hi[place].bitcast(F32), ALU.subtract)


class Step:

    def __init__(self, g, kind, w, act, out=None, gain=None, per_unit=3):
        self.kind, self.w, self.act, self.out, self.gain, self.per_unit = kind, w, act, out, gain, per_unit
        self.prev = g.steps[-1] if g.steps else None
        self.unit, self.chunk, self.turn, self.part, self.square = g.units, g.chunks, g.turns, g.parts, g.squares
        g.steps.append(self)
        g.units += KD
        g.chunks += per_unit * KD
        g.turns += KD // 2 * (2 if kind == "merge" else 1)
        g.parts += NCH * KD if out else 0
        g.squares += NCH * KD if gain is not None or kind == "ple" else 0


def run_tail(g):
    nc = g.nc
    room = Room(nc, RM)
    g.hg, g.tmp = room("f_hg", [P, 2, CH]), room("f_tmp", [P, 2, CH])
    g.gate_in_sb = room("f_gates", [P, 2, 2, CH])
    room = Room(nc, R1, R2)
    h = (room("h2_hi", [P, KD, T], F32R), room("h2_lo", [P, KD, T], F32R))
    room = Room(nc, R2, RW)
    z = (room("z_hi", [P, KD, T], F32R), room("z_lo", [P, KD, T], F32R))
    room = Room(nc, R2, RW)
    a = (room("a_hi", [P, KD, T], F32R), room("a_lo", [P, KD, T], F32R))
    room = Room(nc, R2, RW)
    g.diag = room("f_diag", [P, NT, P])
    g.stat = room("f_stat", [P, NT])
    g.p_t = room("p_t_sb", [P, 2, T])
    g.p_hi, g.p_lo = room("p_hi", [P, 2, T], F32R), room("p_lo", [P, 2, T], F32R)
    g.wp = room("w_ple_sb", [P, 2, D])
    g.wp_hi, g.wp_lo = room("w_ple_hi", [P, 2, D], F32R), room("w_ple_lo", [P, 2, D], F32R)
    g.total = room("final_total", [P, T])
    g.sig = room("ple_sig", [P, 2, CH])
    g.root = room("y_root", [P, NT])
    g.x = Room(nc, RX, RM)("x_res", [P, KD, T])
    g.y = Room(nc, R1, R2)("y_nat", [P, 3, D])
    (g.hg_s, g.hi_s, g.lo_s, g.sq_s, g.acc_s, g.clear_s, g.x_in, g.sum_s, g.stat_s, g.mean_s, g.root_s,
     g.diag_s, g.bc_s, g.bc_got, g.p_in, g.wp_in, g.p_hi_s, g.p_lo_s, g.wp_lo_s, g.sig_s, g.px_s, g.pdone_s, g.y_full) = map(g.sem, (
         "t_hg", "t_hi", "t_lo", "t_sq", "t_acc", "t_clear", "t_x_in", "t_sum", "t_stat", "t_mean", "t_root",
         "t_diag", "t_bc", "t_bc_got", "t_p_in", "t_wp_in", "t_p_hi", "t_p_lo", "t_wp_lo", "t_sig", "t_px", "t_pdone", "t_y_full"))
    g.y_got = [g.sem(f"t_y_got{odd}") for odd in range(2)]
    g.gates_in = [g.sem(f"t_gates_in{j}") for j in range(2)]
    y_out = [g.sem(f"y_out{j}") for j in range(3)]
    g.parts = g.squares = 0
    g.steps = []
    Step(g, "merge", None, (g.o_hi, g.o_lo), z, per_unit=6)
    Step(g, "residual", g.w_o[0], z, h, gain=1)
    for f in range(NF):
        Step(g, "up", g.w_up[0, :, f * D:(f + 1) * D], h, a)
        out, gain = (h, 2) if f == NF - 1 else (None, None)
        Step(g, "residual", g.w_down[0, f * D:(f + 1) * D, :], a, out, gain)
    Step(g, "ple", g.w_ple_gate[0], h, per_unit=6)
    factors = [g.steps[2], g.steps[-1]]
    steps = g.steps

    with nc.Block() as block:

        @block.sync
        def _(sp):
            sp.dma_start(g.x[:, :, :], g.xt_d).then_inc(g.x_in, 16)
            for st in steps:
                def pair(i, st=st):
                    for j in range(2):
                        sp.wait_ge(g.w_split, i * 2 + st.unit + j - 1)
                        if st.kind == "merge":
                            load_merge_unit(sp, g, i * 2 + j, j)
                        else:
                            sp.dma_start(g.w_stage[:, j], columns(st.w, i * 2 + j)).then_inc(g.w_loaded[j], 16)
                if st.kind == "ple":
                    pair(0)
                    sp.wait_ge(g.full, st.chunk)
                    sp.dma_start(g.wp[:, :, :], g.w_ple[0].rearrange("(k p) c -> p k c", p=P)).then_inc(g.wp_in, 16)
                    sp.dma_start(g.p_t[:, :, :], g.p_t_d).then_inc(g.p_in, 16)
                with sp.Fori(1 if st.kind in ("merge", "ple") else 0, KD // 2) as i:
                    pair(i)
            for t in range(NT):
                sp.wait_ge(g.y_got[t % 2], t // 2 + 1)
                dst = g.y_prompt[0, t * P:(t + 1) * P, :] if t < NT - 1 else g.y_sample.rearrange("s t d -> (s t) d")
                sp.dma_start(dst, g.y[:ROWS[t], t % 3, :]).then_inc(y_out[t % 3], 16)
            for j in range(3):
                sp.wait_ge(y_out[j], 16 * len(range(j, NT, 3)))
            sp.wait_ge(g.copied, 16 * 2 * NSEQ)

        @block.gpsimd
        def _(pool):
            for st in steps:
                def pair(i, st=st):
                    for j in range(2):
                        if not (first(i) and st.kind == "merge"):
                            per = 2 if st.kind == "merge" else 1
                            pool.wait_ge(g.w_loaded[j], (i * per + st.turn + per) * 16)
                            before = st.prev.per_unit if first(i) else st.per_unit
                            pool.wait_ge(g.full, i * (2 * st.per_unit) + st.chunk - (before if j == 0 else 0))
                            split_weights(pool, g, j, i * 2 + st.unit + j + 1)
                        if j == 1:
                            low_parts(pool, g, st, i, 0)
                        elif not first(i):
                            low_parts(pool, g, st, i - 1, 1)
                        else:
                            if st.prev:
                                low_parts(pool, g, st.prev, KD // 2 - 1, 1)
                            if st in factors:
                                pool.wait_ge(g.stat_s, 2 * factors.index(st) + 2)
                                inverse_root(pool, g, g.stat[:, :], g.stat[:, :], 1.0 / D, g.mean_s, factors.index(st) + 1, g.root_s)
                            if st.kind == "ple":
                                pool.wait_ge(g.p_hi_s, 1)
                                pool.tensor_tensor(g.wp_lo[:, :, :], g.wp[:, :, :], g.wp_hi[:, :, :].bitcast(F32),
                                                   ALU.subtract).then_inc(g.wp_lo_s, 1)
                in_pairs(pool, KD, pair)
            pool.wait_ge(g.stat_s, 6)
            inverse_root(pool, g, g.root[:, :], g.stat[:, :], 1.0 / D, g.mean_s, 3, g.root_s)

        @block.tensor
        def _(pe):
            for st in steps:
                if st.kind == "ple":
                    for m in range(KD):
                        embed_unit(pe, g, st, m, factors)
                    continue

                def pair(i, st=st):
                    for j in range(2):
                        pe.wait_ge(g.w_split, i * 2 + st.unit + j + 1)
                        for n in range(st.per_unit):
                            c, half = (n // 2, n % 2) if st.kind == "merge" else (n, 0)
                            if first(i) and j == 0 and st.prev and half == 0:
                                pe.wait_ge(g.lo_s, st.part - 2 + c)
                            pe.wait_ge(g.free, i * (2 * st.per_unit) + st.chunk + st.per_unit * j + n - 5)
                            ks = [(4 * half + k, 4 * half + k) for k in range(4)] if st.kind == "merge" else [(k, k) for k in range(KD)]
                            multiply_chunk(pe, g, (st.per_unit * j + n) % 6, j, c, ks, *st.act)
                            if first(i) and st in factors:
                                factor_products(pe, g, factors.index(st), [(0, 0), (0, 2), (1, 0)], (j, n))
                in_pairs(pe, KD, pair)
            write_products(pe, g)

        @block.vector
        def _(dve):
            dve.memset(g.rstd_bc[:, :], 0.0).then_inc(g.clear_s, 1)
            for st in steps:
                if st.kind == "ple":
                    dve.memset(g.total[:, :], 0.0).then_inc(g.clear_s, 1)
                    dve.wait_ge(g.clear_s, 3)
                if st in factors:
                    spread_factors(dve, g, factors.index(st))
                if st.kind == "ple":
                    dve.wait_ge(g.p_hi_s, 2)
                    dve.tensor_tensor(g.p_lo[:, :, :], g.p_t[:, :, :], g.p_hi[:, :, :].bitcast(F32), ALU.subtract).then_inc(g.p_lo_s, 1)
                if st.kind == "residual" and st.prev.kind == "merge":
                    dve.wait_ge(g.x_in, 16)
                    dve.wait_ge(g.clear_s, 1)
                if st is steps[-2]:
                    dve.memset(g.rstd_bc[:, :], 0.0).then_inc(g.clear_s, 1)
                    dve.wait_ge(g.clear_s, 2)
                take = {"merge": take_merge, "residual": take_residual, "up": take_up, "ple": take_embedding}[st.kind]
                in_pairs(dve, KD, lambda i, st=st, take=take: take(dve, g, st, i), peel=st.prev is None or st.kind == "ple")
            dve.memset(g.stat[:, :], float(D)).then_inc(g.stat_s, 1)
            copy_sums(dve, g, 3)
            take_y(g, y_out, dve, 1)

        @block.scalar
        def _(act):
            for q in range(2):
                load_gates(act, g, 0, q)
            for st in steps:
                if st.kind == "ple":
                    act.wait_ge(g.wp_in, 16)
                    act.activation(g.wp_hi[:, :, :], g.wp[:, :, :], ACT.Copy).then_inc(g.p_hi_s, 1)
                    act.wait_ge(g.p_in, 16)
                    act.activation(g.p_hi[:, :, :], g.p_t[:, :, :], ACT.Copy).then_inc(g.p_hi_s, 1)

                def pair(i, st=st, last=False):
                    for q in range(6):
                        if st.kind == "ple":
                            act.wait_ge(g.free, i * 12 + st.chunk + 2 * q + 1)
                            act.activation(g.sig[:, q % 2, :], g.tmp[:, q % 2, :], ACT.Sigmoid).then_inc(g.sig_s, 1)
                            act.wait_ge(g.px_s, i * 6 + q + 1)
                        if st.gain is not None:
                            act.wait_ge(g.free, i * 6 + st.chunk + q + 1)
                        if st.gain is not None or st.kind == "ple":
                            if not (st is steps[1] and first(i) and q == 0):
                                act.wait_ge(g.acc_s, i * 6 + st.square + q)
                            act.activation(g.sq[:, :].unsqueeze(1), chunk_of(g.x, i, q), ACT.Square).then_inc(g.sq_s, 1)
                        if st.out:
                            act.wait_ge(g.hg_s, i * 6 + st.part + q + 1)
                            act.activation(chunk_of(st.out[0], i, q), g.hg[:, q % 2:q % 2 + 1, :], ACT.Copy).then_inc(g.hi_s, 1)
                        if st.kind == "merge" and not (last and q >= 4):
                            load_gates(act, g, i + (q + 2) // 6, (q + 2) % 6, i * 6 + q + 1)
                if st.kind == "merge":
                    pair(0)
                    with act.Fori(1, KD // 2 - 1) as i:
                        pair(i)
                    pair(KD // 2 - 1, last=True)
                elif st.out or st.kind == "ple":
                    in_pairs(act, KD, pair, peel=st is steps[1])
            take_y(g, y_out, act, 0)


def take_y(g, y_out, eng, odd):
    eng.wait_ge(g.root_s, 3)
    for t in range(odd, NT, 2):
        r = ROWS[t]
        eng.wait_ge(g.y_full, t + 1)
        if t >= 3:
            eng.wait_ge(y_out[t % 3], 16 * (t // 3))
        out, src = g.y[:r, t % 3, :], g.bank[:r, 2 * (t % 3):2 * (t % 3) + 2, :].rearrange("p a b -> p (a b)")
        if odd:
            eng.tensor_scalar(out, src, g.root[:r, t:t + 1], None, ALU.mult).then_inc(g.y_got[odd], 1)
        else:
            eng.activation(out, src, ACT.Copy, scale=g.root[:r, t:t + 1]).then_inc(g.y_got[odd], 1)


def load_merge_unit(sp, g, m, j):
    for half, w in enumerate((g.w_oa, g.w_ob)):
        sp.dma_start(g.w_stage[:, j, 4 * half:4 * half + 4, :], columns(w[0], m)).then_inc(g.w_loaded[j], 16)


def chunk_of(x, i, q):
    c = q % 3
    return x[:, bass.ds(i * 2 + q // 3, 1), c * CH:(c + 1) * CH]


def split_weights(pool, g, j, n):
    one = g.ones[:, 0:1].unsqueeze(2).to_broadcast([P, KD, P])
    pool.tensor_tensor(g.wu_hi[:, j], g.w_stage[:, j], one, ALU.mult).then_inc(g.w_hi, 1)
    pool.wait_ge(g.w_hi, n)
    pool.tensor_tensor(g.wu_lo[:, j], g.w_stage[:, j], g.wu_hi[:, j].bitcast(F32), ALU.subtract).then_inc(g.w_split, 1)


def low_parts(pool, g, st, i, j):
    if not st.out:
        return
    for c in range(NCH):
        q = 3 * j + c
        pool.wait_ge(g.hi_s, i * 6 + st.part + q + 1)
        pool.tensor_tensor(chunk_of(st.out[1], i, q), g.hg[:, q % 2:q % 2 + 1, :], chunk_of(st.out[0], i, q).bitcast(F32),
                           ALU.subtract).then_inc(g.lo_s, 1)


def load_gates(act, g, i, q, free=None):
    if free is not None:
        act.wait_ge(g.hg_s, free)
    c = q % 3
    src = g.gate_d.rearrange("a k p t -> k p a t")[bass.ds(i * 2 + q // 3, 1), :, :, c * CH:(c + 1) * CH]
    act.dma_start(g.gate_in_sb[:, q % 2], src.rearrange("k p a t -> p (k a) t")).then_inc(g.gates_in[q % 2], 16)


def take_merge(dve, g, st, i):
    for q in range(6):
        dve.wait_ge(g.gates_in[q % 2], (i * 3 + q // 2 + 1) * 16)
        for half in range(2):
            n = 2 * q + half
            dve.wait_ge(g.full, i * 12 + st.chunk + n + 1)
            if half == 0 and not (first(i) and q == 0):
                dve.wait_ge(g.hg_s, i * 6 + q)
            dve.tensor_tensor(g.tmp[:, half, :], g.bank[:, n % 6, :CH], g.gate_in_sb[:, q % 2, half, :], ALU.mult).then_inc(g.free, 1)
        dve.wait_ge(g.free, i * 12 + st.chunk + 2 * q + 2)
        if not (first(i) and q < 2):
            dve.wait_ge(g.lo_s, i * 6 + st.part + q - 1)
        dve.tensor_tensor(g.hg[:, q % 2, :], g.tmp[:, 0, :], g.tmp[:, 1, :], ALU.add).then_inc(g.hg_s, 1)


def take_residual(dve, g, st, i):
    for q in range(6):
        x = chunk_of(g.x, i, q)
        dve.wait_ge(g.full, i * 6 + st.chunk + q + 1)
        dve.tensor_tensor(x, g.bank[:, q:q + 1, :CH], x, ALU.add).then_inc(g.free, 1)
        if st.gain is not None:
            dve.wait_ge(g.free, i * 6 + st.chunk + q + 1)
            dve.wait_ge(g.lo_s, i * 6 + st.part + q - 1)
            dve.tensor_scalar(g.hg[:, q % 2:q % 2 + 1, :], x, g.gains[:, st.gain, bass.ds(i * 2 + q // 3, 1)], None,
                              ALU.mult).then_inc(g.hg_s, 1)
            add_square(dve, g, g.rstd_bc, q % 3, i * 6 + st.square + q + 1)


def take_up(dve, g, st, i):
    for q in range(6):
        c = q % 3
        dve.wait_ge(g.full, i * 6 + st.chunk + q + 1)
        dve.tensor_tensor(g.tmp[:, q % 2, :], g.bank[:, q, :CH], g.rstd_bc[:, c * CH:(c + 1) * CH], ALU.mult).then_inc(g.free, 1)
        dve.wait_ge(g.free, i * 6 + st.chunk + q + 1)
        dve.wait_ge(g.lo_s, i * 6 + st.part + q - 1)
        dve.scalar_tensor_tensor(g.hg[:, q % 2, :], g.tmp[:, q % 2, :], 0.0, g.tmp[:, q % 2, :], ALU.max, ALU.mult).then_inc(g.hg_s, 1)


def take_embedding(dve, g, st, i):
    for q in range(6):
        c = q % 3
        x = chunk_of(g.x, i, q)
        gate, embedding = (q, 3 + q) if first(i) and q < 3 else (2 * q, 2 * q + 1)
        dve.wait_ge(g.full, i * 12 + st.chunk + gate + 1)
        dve.tensor_tensor(g.tmp[:, q % 2, :], g.bank[:, 2 * c, :CH], g.rstd_bc[:, c * CH:(c + 1) * CH], ALU.mult).then_inc(g.free, 1)
        dve.wait_ge(g.full, i * 12 + st.chunk + embedding + 1)
        dve.wait_ge(g.sig_s, i * 6 + q + 1)
        dve.tensor_tensor(g.hg[:, q % 2, :], g.bank[:, 2 * c + 1, :CH], g.sig[:, q % 2, :], ALU.mult).then_inc(g.free, 1)
        dve.wait_ge(g.free, i * 12 + st.chunk + 2 * q + 2)
        dve.tensor_tensor(x, x, g.hg[:, q % 2:q % 2 + 1, :], ALU.add).then_inc(g.px_s, 1)
        add_square(dve, g, g.total, c, i * 6 + st.square + q + 1)
        dve.tensor_scalar(x, x, g.gains[:, 3, bass.ds(i * 2 + q // 3, 1)], None, ALU.mult).then_inc(g.pdone_s, 1)


def add_square(dve, g, total, c, at):
    dve.wait_ge(g.sq_s, at)
    cols = slice(c * CH, (c + 1) * CH)
    dve.tensor_tensor(total[:, cols], total[:, cols], g.sq[:, :], ALU.add).then_inc(g.acc_s, 1)


def embed_unit(pe, g, st, m, factors):
    def gate(c):
        if m == 0:
            pe.wait_ge(g.lo_s, st.part - 2 + c)
        pe.wait_ge(g.free, st.chunk + 6 * m + 2 * c - 5)
        multiply_chunk(pe, g, 2 * c, m % 2, c, [(k, k) for k in range(KD)], *st.act)
        if m == 0:
            factor_products(pe, g, factors.index(st), [(0, 0), (0, 2), (0, 4)], (0, 2 * c))

    def embedding(c):
        pe.wait_ge(g.free, st.chunk + 6 * m + 2 * c - 4)
        out = g.bank[:, 2 * c + 1, :CH]
        for k in range(2):
            w, v = g.wp_hi[:, k, m * P:(m + 1) * P], g.wp_lo[:, k, m * P:(m + 1) * P]
            a, b = g.p_hi[:, k, c * CH:(c + 1) * CH], g.p_lo[:, k, c * CH:(c + 1) * CH]
            pe.matmul(out, w, a, start=k == 0, stop=False)
            pe.matmul(out, w, b, start=False, stop=False)
            last = pe.matmul(out, v, a, start=False, stop=k == 1)
        last.then_inc(g.full, 1)

    pe.wait_ge(g.w_split, st.unit + m + 1)
    if m == 0:
        for c in range(NCH):
            gate(c)
        pe.wait_ge(g.wp_lo_s, 1)
        pe.wait_ge(g.p_lo_s, 1)
        for c in range(NCH):
            embedding(c)
    else:
        for c in range(NCH):
            gate(c)
            embedding(c)


def factor_products(pe, g, n, places, at):
    if at == places[0]:
        pe.wait_ge(g.acc_s, NCH * KD * (n + 1))
        sum_features(pe, g, g.rstd_bc)
    elif at == places[1]:
        pe.wait_ge(g.diag_s, n + 1)
        for b in range(2):
            for t in range(4):
                last = pe.matmul(g.bank[:, 6 + b, t * P:(t + 1) * P], g.ones[:, :], g.diag[:, 4 * b + t, :], start=True, stop=True)
            last.then_inc(g.bc_s, 1)
    elif at == places[2]:
        pe.wait_ge(g.bc_got, 3 * n + 1)
        pe.matmul(g.bank[:, 6, :NS], g.ones[:NS, :], g.diag[:NS, NT - 1, :NS], start=True, stop=True).then_inc(g.bc_s, 1)


def sum_features(pe, g, total):
    for t in range(NT):
        last = pe.matmul(g.bank[:ROWS[t], 7, t:t + 1], total[:, t * P:t * P + ROWS[t]], g.ones[:, 0:1], start=True, stop=True)
    last.then_inc(g.sum_s, 1)


def copy_sums(dve, g, n):
    dve.wait_ge(g.stat_s, 2 * n - 1)
    dve.wait_ge(g.sum_s, n)
    dve.tensor_copy(g.stat[:, :NT - 1], g.bank[:, 7, :NT - 1])
    dve.tensor_copy(g.stat[:NS, NT - 1:], g.bank[:NS, 7, NT - 1:NT]).then_inc(g.stat_s, 1)


def spread_factors(dve, g, n):
    dve.memset(g.stat[:, :], float(D)).then_inc(g.stat_s, 1)
    copy_sums(dve, g, n + 1)
    dve.wait_ge(g.root_s, n + 1)
    shape = [P, NT, P]
    dve.tensor_tensor(g.diag[:, :, :], g.ident[:, :].unsqueeze(1).to_broadcast(shape),
                      g.stat[:, :].unsqueeze(2).to_broadcast(shape), ALU.mult).then_inc(g.diag_s, 1)
    for b, (bank, a, z) in enumerate(((6, 0, 512), (7, 512, 1024), (6, 1024, T))):
        dve.wait_ge(g.bc_s, 3 * n + b + 1)
        dve.tensor_copy(g.rstd_bc[:, a:z], g.bank[:, bank, :z - a]).then_inc(g.bc_got, 1)
    dve.wait_ge(g.bc_got, 3 * n + 3)


def write_products(pe, g):
    pe.wait_ge(g.acc_s, g.squares)
    sum_features(pe, g, g.total)
    pe.wait_ge(g.pdone_s, NCH * KD)
    pe.wait_ge(g.free, g.chunks)
    for t in range(NT):
        r = ROWS[t]
        if t >= 3:
            pe.wait_ge(g.y_got[(t - 3) % 2], (t - 3) // 2 + 1)
        for k in range(KD):
            last = pe.transpose(g.bank[:r, 2 * (t % 3) + k // 4, (k % 4) * P:(k % 4 + 1) * P], g.x[:, k, t * P:t * P + r], g.ident[:, :])
        last.then_inc(g.y_full, 1)


_INS = ["x_prompt", "x_sample", "cache_win_k", "cache_win_v", "cache_ckv", "cache_kpe", "page_table", "p_prompt",
        "p_sample", "g_mix", "w_in", "g_q", "w_uq", "g_kv", "w_uk", "w_uv", "w_oa", "w_ob", "w_o", "g_ffn", "w_up",
        "w_down", "g_ple", "w_ple_gate", "w_ple", "g_final"]
_OUTS = {
    "y_prompt": (1, SEQ, D), "y_sample": (NSEQ, TDEC, D),
    "win_k_prompt": (1, 1, SEQ, H, E), "win_v_prompt": (1, 1, SEQ, H, E),
    "ckv_prompt": (1, 1, SEQ, KL), "kpe_prompt": (1, 1, SEQ, RD),
    "win_k_sample": (1, NSEQ, PAST + TDEC, H, E), "win_v_sample": (1, NSEQ, PAST + TDEC, H, E),
    "ckv_sample": (1, NSEQ, TDEC, KL), "kpe_sample": (1, NSEQ, TDEC, RD),
}


def _log_count(dist):
    count = sum(((dist >= 0) & (dist <= w) & (dist % d == 0)).astype(np.float32) for w, d in PATTERNS)
    return np.where(count > 0, np.log(np.maximum(count, 1)), NEG).astype(np.float32)


def _constants():
    pos = np.concatenate([np.arange(SEQ), np.tile(PAST + np.arange(TDEC), NSEQ), np.zeros(P - NS)]).astype(np.float32)
    out = {"ident_c": np.eye(P, dtype=np.float32)}
    for tag, rot in (("a", E // 4), ("b", RD)):
        half = rot // 2
        inv = np.float32(500000.0) ** (-np.arange(half, dtype=np.float32) * np.float32(2.0 / rot))
        ang = (pos[:, None] * inv[None, :].astype(np.float32)).astype(np.float32)
        for fn, name in ((np.cos, "cos"), (np.sin, "sin")):
            out[f"{name}_{tag}_c"] = np.ascontiguousarray(fn(ang).astype(np.float32).reshape(NT, P, half).transpose(1, 0, 2))
    q, k = np.arange(P)[:, None, None], np.arange(P)[None, None, :]
    dist = (NT - 2 - np.arange(NT - 1))[None, :, None] * P + q - k
    out["mask_w_c"] = _log_count(dist)
    out["mask_b_c"] = np.where(dist >= 0, 0.0, NEG).astype(np.float32)
    far = np.array([16 * m + r for r in range(4) for m in range(32)])
    keys = np.concatenate([far, np.arange(PAST // 2, PAST + TDEC)])
    t = np.tile(np.arange(TDEC), H)[:, None]
    out["mask_ws_c"] = _log_count(PAST + t - keys[None, :])
    out["mask_ls_c"] = np.where(np.arange(PAST + TDEC)[None, :] <= PAST + t, 0.0, NEG).astype(np.float32)
    return out


def kernel(**inputs):
    import concourse.bacc as _bacc
    from concourse.bass_utils import run_bass_kernel_spmd as _run

    nc = _bacc.Bacc("TRN2", target_bir_lowering=False, num_devices=1)
    arrays, io = {}, {}
    for name, a in [(n, np.asarray(inputs[n])) for n in _INS] + list(_constants().items()):
        a = np.ascontiguousarray(a)
        arrays[f"in_{name}"] = a
        io[name] = nc.dram_tensor(f"in_{name}", a.shape, mybir.dt.from_np(a.dtype), kind="ExternalInput").ap()
    for name, shape in _OUTS.items():
        io[name] = nc.dram_tensor(f"out_{name}", shape, F32, kind="ExternalOutput").ap()
    build(nc, io)
    r = _run(nc, [arrays], core_ids=[0])
    return tuple(r.results[0][f"out_{name}"] for name in _OUTS)
```
